# Optimizing a Trainium2 kernel written in Bass

```python
import jax, jax.numpy as jnp
from jax import lax
import numpy as np
import math

D_MODEL = 1024
BATCH = 1
SEQ = 256
DEPTH = 2

EPS = 1e-6
HG_HEADS = 4
HG_HEAD_DIM = 128
HG_DIM = HG_HEADS * HG_HEAD_DIM
GLA_HEADS = 4
GLA_DK = 64
GLA_DV = 128
GLA_KDIM = GLA_HEADS * GLA_DK
GLA_VDIM = GLA_HEADS * GLA_DV
GLA_RANK = 16
GLA_TAU = 16.0
LA_CHUNK = 64
NSA_HEADS = 8
NSA_KV_GROUPS = 2
NSA_REP = NSA_HEADS // NSA_KV_GROUPS
NSA_DH = 64
NSA_DIM = NSA_HEADS * NSA_DH
NSA_KV_DIM = NSA_KV_GROUPS * NSA_DH
CMP_STRIDE = 16
CMP_BLK = 2 * CMP_STRIDE
CMP_HID = 128
SLC_BLK = 64
N_SEL = 16
WIN = 512
Q_BLOCK = 128
ROPE_THETA = 500000.0
ROT_DIM = NSA_DH // 4
N_BRANCH = 3
FF_DIM = ((8 * D_MODEL // 3 + 255) // 256) * 256

IN_SPLITS = (HG_DIM, HG_DIM, HG_DIM, HG_DIM,
             GLA_KDIM, GLA_KDIM, GLA_VDIM, GLA_RANK, GLA_VDIM,
             NSA_DIM, NSA_KV_DIM, NSA_KV_DIM, NSA_KV_DIM, NSA_KV_DIM, NSA_KV_DIM, NSA_KV_DIM,
             3 * NSA_HEADS,
             N_BRANCH * D_MODEL)
IN_COLS = sum(IN_SPLITS)


def rmsnorm(x, g):
    x32 = x.astype(jnp.float32)
    y = x32 * lax.rsqrt(jnp.mean(x32 * x32, axis=-1, keepdims=True) + EPS)
    return y.astype(x.dtype) * g

def split_cols(z):
    outs = []
    start = 0
    for n in IN_SPLITS:
        outs.append(z[..., start:start + n])
        start += n
    return outs

def heads(z, n):
    B, T, _ = z.shape
    return z.reshape(B, T, n, -1).transpose(0, 2, 1, 3)

def head_rmsnorm(o, g, dtype):
    B, H, T, dv = o.shape
    o = o.astype(jnp.float32).transpose(0, 2, 1, 3)
    o = o * lax.rsqrt(jnp.mean(o * o, axis=-1, keepdims=True) + EPS)
    return o.reshape(B, T, H * dv).astype(dtype) * g

def chunked_gated_linear_attention(q, k, v, log_g):
    B, H, T, dk = q.shape
    dv = v.shape[-1]
    n = T // LA_CHUNK

    def to_chunks(a):
        return jnp.moveaxis(a.astype(jnp.float32).reshape(B, H, n, LA_CHUNK, a.shape[-1]), 2, 0)

    causal = jnp.tril(jnp.ones((LA_CHUNK, LA_CHUNK), dtype=bool))[:, :, None]

    def step(state, inp):
        qc, kc, vc, gc = inp
        b = jnp.cumsum(gc, axis=2)
        o_inter = jnp.einsum('bhtd,bhdv->bhtv', qc * jnp.exp(b), state)
        decay = jnp.exp(jnp.where(causal, b[:, :, :, None, :] - b[:, :, None, :, :], -jnp.inf))
        scores = jnp.einsum('bhtd,bhtsd,bhsd->bhts', qc, decay, kc)
        o = o_inter + jnp.einsum('bhts,bhsv->bhtv', scores, vc)
        b_last = b[:, :, -1:, :]
        state = (jnp.exp(b_last[:, :, 0, :, None]) * state
                 + jnp.einsum('bhsd,bhsv->bhdv', kc * jnp.exp(b_last - b), vc))
        return state, o

    s0 = jnp.zeros((B, H, dk, dv), jnp.float32)
    _, o = lax.scan(step, s0, (to_chunks(q), to_chunks(k), to_chunks(v), to_chunks(log_g)))
    return jnp.moveaxis(o, 0, 2).reshape(B, H, T, dv)

def partial_rope(x, cos, sin):
    half = ROT_DIM // 2
    c = cos[None, :, None, :].astype(x.dtype)
    s = sin[None, :, None, :].astype(x.dtype)
    x1 = x[..., :half]
    x2 = x[..., half:ROT_DIM]
    return jnp.concatenate([x1 * c - x2 * s, x2 * c + x1 * s, x[..., ROT_DIM:]], axis=-1)

def masked_softmax(s, mask):
    s = jnp.where(mask, s.astype(jnp.float32), -1e30)
    return jnp.where(mask, jax.nn.softmax(s, axis=-1), 0.0)

def compress(k, pos, w1, w2):
    B, G, T, dh = k.shape
    c = k.reshape(B, G, T // CMP_STRIDE, CMP_STRIDE, dh)
    blocks = jnp.concatenate([c[:, :, :-1], c[:, :, 1:]], axis=3) + pos
    flat = blocks.reshape(B, G, blocks.shape[2], CMP_BLK * dh)
    return jax.nn.gelu(flat @ w1) @ w2

def nsa_attention(q, kc, vc, ks, vs, kw, vw, gates):
    B, T, H, dh = q.shape
    G, R = NSA_KV_GROUPS, NSA_REP
    ncmp = kc.shape[2]
    nslc = T // SLC_BLK
    n_sel = min(N_SEL, nslc)
    nq = T // Q_BLOCK
    cmp_start = jnp.arange(ncmp) * CMP_STRIDE
    cmp_end = cmp_start + CMP_BLK - 1
    blk = jnp.arange(nslc)
    overlap = ((cmp_start[:, None] < (blk[None, :] + 1) * SLC_BLK)
               & (cmp_end[:, None] >= blk[None, :] * SLC_BLK)).astype(jnp.float32)
    ks_b = ks.reshape(B, G, nslc, SLC_BLK, dh)
    vs_b = vs.reshape(B, G, nslc, SLC_BLK, dh)
    kw_pad = jnp.pad(kw, ((0, 0), (0, 0), (WIN, 0), (0, 0)))
    vw_pad = jnp.pad(vw, ((0, 0), (0, 0), (WIN, 0), (0, 0)))
    b_idx = jnp.arange(B)[:, None, None, None]
    g_idx = jnp.arange(G)[None, :, None, None]
    q_blocks = jnp.moveaxis(q.reshape(B, nq, Q_BLOCK, G, R, dh), 1, 0).transpose(0, 1, 3, 4, 2, 5)

    def block_fn(args):
        c, qb = args
        t = c * Q_BLOCK + jnp.arange(Q_BLOCK)
        mask_c = cmp_end[None, :] <= t[:, None]
        p_c = masked_softmax(jnp.einsum('bgrqd,bgnd->bgrqn', qb, kc), mask_c)
        o_c = jnp.einsum('bgrqn,bgnd->bgrqd', p_c.astype(vc.dtype), vc)
        imp = jnp.einsum('bgrqn,nj->bgqj', p_c, overlap)
        cur = t // SLC_BLK
        valid = blk[None, :] <= cur[:, None]
        forced = (blk[None, :] == 0) | (blk[None, :] == cur[:, None]) | (blk[None, :] == cur[:, None] - 1)
        score = jnp.where(valid & forced, 1e9, jnp.where(valid, imp, -1e9))
        top_s, top_i = lax.top_k(score, n_sel)
        k_sel = ks_b[b_idx, g_idx, top_i].reshape(B, G, Q_BLOCK, n_sel * SLC_BLK, dh)
        v_sel = vs_b[b_idx, g_idx, top_i].reshape(B, G, Q_BLOCK, n_sel * SLC_BLK, dh)
        tok = (top_i[..., None] * SLC_BLK + jnp.arange(SLC_BLK)).reshape(B, G, Q_BLOCK, n_sel * SLC_BLK)
        mask_s = (tok <= t[None, None, :, None]) & jnp.repeat(top_s > -1e8, SLC_BLK, axis=-1)
        p_s = masked_softmax(jnp.einsum('bgrqd,bgqmd->bgrqm', qb, k_sel), mask_s[:, :, None])
        o_s = jnp.einsum('bgrqm,bgqmd->bgrqd', p_s.astype(v_sel.dtype), v_sel)
        k_win = lax.dynamic_slice_in_dim(kw_pad, c * Q_BLOCK, WIN + Q_BLOCK, axis=2)
        v_win = lax.dynamic_slice_in_dim(vw_pad, c * Q_BLOCK, WIN + Q_BLOCK, axis=2)
        kp = c * Q_BLOCK - WIN + jnp.arange(WIN + Q_BLOCK)
        mask_w = (kp[None, :] <= t[:, None]) & (kp[None, :] > t[:, None] - WIN) & (kp[None, :] >= 0)
        p_w = masked_softmax(jnp.einsum('bgrqd,bgkd->bgrqk', qb, k_win), mask_w)
        o_w = jnp.einsum('bgrqk,bgkd->bgrqd', p_w.astype(v_win.dtype), v_win)
        return jnp.stack([o_c, o_s, o_w], axis=-1)

    out = lax.map(block_fn, (jnp.arange(nq), q_blocks))
    out = out.transpose(1, 0, 4, 2, 3, 5, 6).reshape(B, T, H, dh, 3)
    return jnp.einsum('bthdk,bthk->bthd', out, gates).reshape(B, T, H * dh)

def hybrid_mixer(h, lb, w_in, hg_norm_g, gla_w2, gla_b, gla_norm_g, cmp_pos_k, cmp_pos_v,
                 cmp_w1_k, cmp_w2_k, cmp_w1_v, cmp_w2_v, w_br_hg, w_br_gla, w_br_nsa, w_out, cos, sin):
    B, T, _ = h.shape
    (hq, hf, hi, hog, gq, gk, gv, glr, gog,
     nq_, nkc, nvc, nks, nvs, nkw, nvw, ngate, mgate) = split_cols(h @ w_in)
    lbh = lb.reshape(1, HG_HEADS, 1, HG_HEAD_DIM)
    log_f = jnp.logaddexp(jnp.log(lbh), jnp.log1p(-lbh)
                          + jax.nn.log_sigmoid(heads(hf, HG_HEADS).astype(jnp.float32)))
    o_hg = chunked_gated_linear_attention(jax.nn.silu(heads(hq, HG_HEADS)), -jnp.expm1(log_f),
                                          heads(hi, HG_HEADS), log_f)
    y_hg = head_rmsnorm(o_hg, hg_norm_g, h.dtype) * jax.nn.silu(hog)
    log_a = jax.nn.log_sigmoid((glr @ gla_w2 + gla_b).astype(jnp.float32)) / GLA_TAU
    o_gla = chunked_gated_linear_attention(heads(gq, GLA_HEADS) * GLA_DK ** -0.5, heads(gk, GLA_HEADS),
                                           heads(gv, GLA_HEADS), heads(log_a, GLA_HEADS))
    y_gla = head_rmsnorm(o_gla, gla_norm_g, h.dtype) * jax.nn.silu(gog)
    q = partial_rope(nq_.reshape(B, T, NSA_HEADS, NSA_DH), cos, sin) * NSA_DH ** -0.5

    def kv(z):
        return z.reshape(B, T, NSA_KV_GROUPS, NSA_DH)

    def to_g(z):
        return z.transpose(0, 2, 1, 3)

    kc = compress(to_g(partial_rope(kv(nkc), cos, sin)), cmp_pos_k, cmp_w1_k, cmp_w2_k)
    vc = compress(to_g(kv(nvc)), cmp_pos_v, cmp_w1_v, cmp_w2_v)
    ks = to_g(partial_rope(kv(nks), cos, sin))
    vs = to_g(kv(nvs))
    kw = to_g(partial_rope(kv(nkw), cos, sin))
    vw = to_g(kv(nvw))
    gates = jax.nn.sigmoid(ngate).reshape(B, T, NSA_HEADS, 3)
    y_nsa = nsa_attention(q, kc, vc, ks, vs, kw, vw, gates)
    g = jax.nn.sigmoid(mgate).reshape(B, T, N_BRANCH, D_MODEL)
    m = (g[:, :, 0] * (y_hg @ w_br_hg) + g[:, :, 1] * (y_gla @ w_br_gla)
         + g[:, :, 2] * (y_nsa @ w_br_nsa))
    return m @ w_out

def swiglu(h, w_gate, w_up, w_down):
    return (jax.nn.silu(h @ w_gate) * (h @ w_up)) @ w_down

def first_inputs(seed: int = 0) -> dict:
    key = jax.random.key(seed)
    k = jax.random.split(key, 24)
    L, D = DEPTH, D_MODEL

    def nrm(kk, shape, scale):
        return jax.random.normal(kk, shape, jnp.float32) * scale

    def gain(kk, shape):
        return 1.0 + 0.02 * jax.random.normal(kk, shape, jnp.float32)

    return {
        'x': nrm(k[0], (BATCH, SEQ, D), 1.0),
        'norm1_g': gain(k[1], (L, D)),
        'w_in': nrm(k[2], (L, D, IN_COLS), D ** -0.5),
        'hg_lb': nrm(k[3], (L, HG_DIM), 0.5),
        'hg_norm_g': gain(k[4], (L, HG_DIM)),
        'gla_w2': nrm(k[5], (L, GLA_RANK, GLA_KDIM), GLA_RANK ** -0.5),
        'gla_b': nrm(k[6], (L, GLA_KDIM), 0.1),
        'gla_norm_g': gain(k[7], (L, GLA_VDIM)),
        'cmp_pos_k': nrm(k[8], (L, CMP_BLK, NSA_DH), 0.1),
        'cmp_pos_v': nrm(k[9], (L, CMP_BLK, NSA_DH), 0.1),
        'cmp_w1_k': nrm(k[10], (L, CMP_BLK * NSA_DH, CMP_HID), (CMP_BLK * NSA_DH) ** -0.5),
        'cmp_w2_k': nrm(k[11], (L, CMP_HID, NSA_DH), CMP_HID ** -0.5),
        'cmp_w1_v': nrm(k[12], (L, CMP_BLK * NSA_DH, CMP_HID), (CMP_BLK * NSA_DH) ** -0.5),
        'cmp_w2_v': nrm(k[13], (L, CMP_HID, NSA_DH), CMP_HID ** -0.5),
        'w_br_hg': nrm(k[14], (L, HG_DIM, D), HG_DIM ** -0.5),
        'w_br_gla': nrm(k[15], (L, GLA_VDIM, D), GLA_VDIM ** -0.5),
        'w_br_nsa': nrm(k[16], (L, NSA_DIM, D), NSA_DIM ** -0.5),
        'w_out': nrm(k[17], (L, D, D), D ** -0.5),
        'norm2_g': gain(k[18], (L, D)),
        'w_ffn_gate': nrm(k[19], (L, D, FF_DIM), D ** -0.5),
        'w_ffn_up': nrm(k[20], (L, D, FF_DIM), D ** -0.5),
        'w_ffn_down': nrm(k[21], (L, FF_DIM, D), FF_DIM ** -0.5),
        'final_norm_g': gain(k[22], (D,)),
    }

def first_block(x, norm1_g, w_in, hg_lb, hg_norm_g, gla_w2, gla_b, gla_norm_g, cmp_pos_k, cmp_pos_v,
              cmp_w1_k, cmp_w2_k, cmp_w1_v, cmp_w2_v, w_br_hg, w_br_gla, w_br_nsa, w_out,
              norm2_g, w_ffn_gate, w_ffn_up, w_ffn_down, final_norm_g):
    T = x.shape[1]
    pos = jnp.arange(T, dtype=jnp.float32)
    inv_freq = ROPE_THETA ** (-jnp.arange(0, ROT_DIM, 2, dtype=jnp.float32) / ROT_DIM)
    ang = pos[:, None] * inv_freq[None, :]
    cos, sin = jnp.cos(ang), jnp.sin(ang)
    lbs = jnp.cumsum(jax.nn.softmax(hg_lb.astype(jnp.float32), axis=0), axis=0)
    lbs = lbs - lbs[0]
    for l in range(DEPTH):
        h = rmsnorm(x, norm1_g[l])
        x = x + hybrid_mixer(h, lbs[l], w_in[l], hg_norm_g[l], gla_w2[l], gla_b[l], gla_norm_g[l],
                             cmp_pos_k[l], cmp_pos_v[l], cmp_w1_k[l], cmp_w2_k[l], cmp_w1_v[l], cmp_w2_v[l],
                             w_br_hg[l], w_br_gla[l], w_br_nsa[l], w_out[l], cos, sin)
        h = rmsnorm(x, norm2_g[l])
        x = x + swiglu(h, w_ffn_gate[l], w_ffn_up[l], w_ffn_down[l])
    return rmsnorm(x, final_norm_g)


CHUNK = 64
N_EVEN = (DEPTH + 1) // 2
N_ODD = DEPTH // 2

POOL_WIDTH = D_MODEL // 2
POOL_WINDOWS = (2, 4, 8, 16)
POOL_N_GROUPS = len(POOL_WINDOWS)
POOL_GROUP = POOL_WIDTH // POOL_N_GROUPS
ATT_HEAD_DIM = 64
ATT_HEADS = (D_MODEL // 2) // ATT_HEAD_DIM
ATT_WIDTH = ATT_HEADS * ATT_HEAD_DIM
ATT_PREV_CHUNKS = 8
REL_CLIP = 256
MIX_IN = POOL_WIDTH + 3 * ATT_WIDTH
MIX_OUT = POOL_WIDTH + ATT_WIDTH

SSM_EXPAND = 2
SSM_D_INNER = SSM_EXPAND * D_MODEL
SSM_HEAD_DIM = 64
SSM_HEADS = SSM_D_INNER // SSM_HEAD_DIM
SSM_GROUPS = 8
SSM_HEADS_PER_GROUP = SSM_HEADS // SSM_GROUPS
SSM_D_STATE = 128
SSM_D_CONV = 4
SSM_CONV_DIM = SSM_D_INNER + 2 * SSM_GROUPS * SSM_D_STATE
SSM_IN = SSM_D_INNER + SSM_CONV_DIM + SSM_HEADS
DT_MIN = 0.001
DT_MAX = 0.1

MOE_GROUPS = 4
MOE_EXPERTS_PER_GROUP = 8
MOE_EXPERTS = MOE_GROUPS * MOE_EXPERTS_PER_GROUP
MOE_TOP_K = 2
MOE_D_FF = D_MODEL // 8


def rmsnorm_2(x, w):
    xf = x.astype(jnp.float32)
    y = xf * lax.rsqrt(jnp.mean(xf * xf, axis=-1, keepdims=True) + EPS)
    return (y * w.astype(jnp.float32)).astype(x.dtype)

def modulate(h, shift, scale):
    return h * (1 + scale[:, None, :]) + shift[:, None, :]

def pool_mixer(u, pool_w, pool_scale):
    b, s, _ = u.shape
    uf = u.astype(jnp.float32)
    cs = jnp.pad(jnp.cumsum(uf, axis=1), ((0, 0), (1, 0), (0, 0)))
    pos = jnp.arange(1, s + 1, dtype=jnp.float32)
    outs = []
    for g, w in enumerate(POOL_WINDOWS):
        lo, hi = g * POOL_GROUP, (g + 1) * POOL_GROUP
        upper = cs[:, 1:, lo:hi]
        lower = jnp.pad(cs[:, :s + 1 - w, lo:hi], ((0, 0), (w - 1, 0), (0, 0)))
        count = jnp.minimum(pos, w)[None, :, None]
        outs.append((upper - lower) / count - uf[:, :, lo:hi])
    pooled = jnp.stack(outs, axis=2).astype(u.dtype)
    y = jnp.einsum('bsgc,gcd->bsgd', pooled, pool_w).reshape(b, s, POOL_WIDTH)
    return y * pool_scale

def chunk_attention(q, k, v, rel_bias):
    b, s, _ = q.shape
    nc = s // CHUNK
    band = (ATT_PREV_CHUNKS + 1) * CHUNK
    q = q.reshape(b, nc, CHUNK, ATT_HEADS, ATT_HEAD_DIM)
    k = k.reshape(b, nc, CHUNK, ATT_HEADS, ATT_HEAD_DIM)
    v = v.reshape(b, nc, CHUNK, ATT_HEADS, ATT_HEAD_DIM)
    pad = ((0, 0), (ATT_PREV_CHUNKS, 0), (0, 0), (0, 0), (0, 0))
    kp = jnp.pad(k, pad)
    vp = jnp.pad(v, pad)
    k_band = jnp.concatenate([kp[:, j:j + nc] for j in range(ATT_PREV_CHUNKS + 1)], axis=2)
    v_band = jnp.concatenate([vp[:, j:j + nc] for j in range(ATT_PREV_CHUNKS + 1)], axis=2)
    q_off = jnp.arange(CHUNK)[:, None] + ATT_PREV_CHUNKS * CHUNK
    k_off = jnp.arange(band)[None, :]
    rel_idx = jnp.clip(q_off - k_off, -REL_CLIP, REL_CLIP) + REL_CLIP
    bias = rel_bias[:, rel_idx].astype(jnp.float32)
    key_chunk = jnp.arange(nc)[:, None] - ATT_PREV_CHUNKS + jnp.arange(band)[None, :] // CHUNK
    valid = key_chunk >= 0
    scores = jnp.einsum('bclhd,bcshd->bchls', q, k_band).astype(jnp.float32) * (ATT_HEAD_DIM ** -0.5)
    scores = scores + bias[None, None]
    scores = jnp.where(valid[None, :, None, None, :], scores, -1e30)
    p = jax.nn.softmax(scores, axis=-1).astype(v.dtype)
    o = jnp.einsum('bchls,bcshd->bclhd', p, v_band)
    return o.reshape(b, s, ATT_WIDTH)

def mamba2_mixer(h, w_in, conv_w, conv_b, dt_bias, A_log, D_skip, norm_w, w_out):
    b, s, _ = h.shape
    nc = s // CHUNK
    G, R, P, N = SSM_GROUPS, SSM_HEADS_PER_GROUP, SSM_HEAD_DIM, SSM_D_STATE
    f32 = jnp.float32
    zxbcdt = h @ w_in
    z, xbc, dt = jnp.split(zxbcdt, [SSM_D_INNER, SSM_D_INNER + SSM_CONV_DIM], axis=-1)
    xp = jnp.pad(xbc, ((0, 0), (SSM_D_CONV - 1, 0), (0, 0)))
    conv = xp[:, 0:s] * conv_w[0]
    for tap in range(1, SSM_D_CONV):
        conv = conv + xp[:, tap:tap + s] * conv_w[tap]
    xbc = jax.nn.silu(conv + conv_b)
    xs, Bm, Cm = jnp.split(xbc, [SSM_D_INNER, SSM_D_INNER + G * N], axis=-1)
    dt = jax.nn.softplus(dt.astype(f32) + dt_bias.astype(f32))
    A = -jnp.exp(A_log.astype(f32))
    a = (dt * A).reshape(b, nc, CHUNK, G, R)
    xs = xs.astype(f32).reshape(b, nc, CHUNK, G, R, P)
    x_dt = xs * dt.reshape(b, nc, CHUNK, G, R)[..., None]
    Bm = Bm.astype(f32).reshape(b, nc, CHUNK, G, N)
    Cm = Cm.astype(f32).reshape(b, nc, CHUNK, G, N)
    a_cs = jnp.moveaxis(jnp.cumsum(a, axis=2), 2, -1)
    tril = jnp.tril(jnp.ones((CHUNK, CHUNK), dtype=bool))
    seg = jnp.exp(jnp.where(tril, a_cs[..., :, None] - a_cs[..., None, :], -jnp.inf))
    cb = jnp.einsum('bclgn,bcsgn->bcgls', Cm, Bm)
    y_diag = jnp.einsum('bcgls,bcgrls,bcsgrp->bclgrp', cb, seg, x_dt)
    decay_states = jnp.exp(a_cs[..., -1:] - a_cs)
    states = jnp.einsum('bclgn,bcgrl,bclgrp->bcgrpn', Bm, decay_states, x_dt)
    chunk_decay = jnp.exp(a_cs[..., -1])

    def step(carry, inp):
        st, dec = inp
        return carry * dec[..., None, None] + st, carry

    init = jnp.zeros((b, G, R, P, N), f32)
    _, prev = lax.scan(step, init, (jnp.moveaxis(states, 1, 0), jnp.moveaxis(chunk_decay, 1, 0)))
    prev = jnp.moveaxis(prev, 0, 1)
    y_off = jnp.einsum('bclgn,bcgrpn,bcgrl->bclgrp', Cm, prev, jnp.exp(a_cs))
    y = y_diag + y_off + xs * D_skip.astype(f32).reshape(G, R)[:, :, None]
    y = y.reshape(b, s, SSM_D_INNER)
    g = (y * jax.nn.silu(z.astype(f32))).reshape(b, s, G, SSM_D_INNER // G)
    g = g * lax.rsqrt(jnp.mean(g * g, axis=-1, keepdims=True) + EPS)
    g = g.reshape(b, s, SSM_D_INNER) * norm_w.astype(f32)
    return g.astype(h.dtype) @ w_out

def hier_moe(h, w_group, b_group, w_expert, b_expert, w1, w3, w2):
    b, s, d = h.shape
    t = h.reshape(b * s, d)
    tf = t.astype(jnp.float32)
    g_prob = jax.nn.softmax(tf @ w_group.astype(jnp.float32) + b_group.astype(jnp.float32), axis=-1)
    g_val, g_idx = lax.top_k(g_prob, 1)
    e_logits = jnp.einsum('td,dge->tge', tf, w_expert.astype(jnp.float32)) + b_expert.astype(jnp.float32)
    e_logits = e_logits[jnp.arange(b * s), g_idx[:, 0]]
    e_val, e_idx = lax.top_k(jax.nn.softmax(e_logits, axis=-1), MOE_TOP_K)
    e_val = e_val / jnp.sum(e_val, axis=-1, keepdims=True)
    weights = g_val * e_val
    expert_id = g_idx * MOE_EXPERTS_PER_GROUP + e_idx
    combine = jnp.sum(jax.nn.one_hot(expert_id, MOE_EXPERTS, dtype=jnp.float32) * weights[..., None], axis=1)
    hid = jax.nn.silu(jnp.einsum('td,edf->tef', t, w1)) * jnp.einsum('td,edf->tef', t, w3)
    hid = hid * combine.astype(hid.dtype)[:, :, None]
    y = jnp.einsum('tef,efd->td', hid, w2)
    return y.reshape(b, s, d)

def _normal(key, shape, scale):
    return jax.random.normal(key, shape, jnp.float32) * scale

def second_inputs(seed: int = 0) -> dict:
    key = jax.random.key(seed)
    ks = jax.random.split(key, 28)
    D = D_MODEL
    f32 = jnp.float32
    dt0 = jnp.exp(jax.random.uniform(ks[14], (N_ODD, SSM_HEADS), f32) * (math.log(DT_MAX) - math.log(DT_MIN)) + math.log(DT_MIN))
    dt0 = jnp.maximum(dt0, 1e-4)
    return {
        'x': _normal(ks[0], (BATCH, SEQ, D), 1.0),
        'c': _normal(ks[1], (BATCH, D), 1.0),
        'ada_w': _normal(ks[2], (DEPTH, D, 6 * D), 0.5 * D ** -0.5),
        'ada_b': _normal(ks[3], (DEPTH, 6 * D), 0.02),
        'norm1_w': 1.0 + _normal(ks[4], (DEPTH, D), 0.05),
        'norm2_w': 1.0 + _normal(ks[5], (DEPTH, D), 0.05),
        'mix_w_in': _normal(ks[6], (N_EVEN, D, MIX_IN), D ** -0.5),
        'pool_w': _normal(ks[7], (N_EVEN, POOL_N_GROUPS, POOL_GROUP, POOL_GROUP), POOL_GROUP ** -0.5),
        'pool_scale': 1.0 + _normal(ks[8], (N_EVEN, POOL_WIDTH), 0.05),
        'rel_bias': _normal(ks[9], (N_EVEN, ATT_HEADS, 2 * REL_CLIP + 1), 0.2),
        'mix_w_out': _normal(ks[10], (N_EVEN, MIX_OUT, D), MIX_OUT ** -0.5),
        'ssm_w_in': _normal(ks[11], (N_ODD, D, SSM_IN), D ** -0.5),
        'ssm_conv_w': _normal(ks[12], (N_ODD, SSM_D_CONV, SSM_CONV_DIM), SSM_D_CONV ** -0.5),
        'ssm_conv_b': _normal(ks[13], (N_ODD, SSM_CONV_DIM), 0.02),
        'ssm_dt_bias': dt0 + jnp.log(-jnp.expm1(-dt0)),
        'ssm_A_log': jnp.log(jax.random.uniform(ks[15], (N_ODD, SSM_HEADS), f32, 1.0, 16.0)),
        'ssm_D': 1.0 + _normal(ks[16], (N_ODD, SSM_HEADS), 0.1),
        'ssm_norm_w': 1.0 + _normal(ks[17], (N_ODD, SSM_D_INNER), 0.05),
        'ssm_w_out': _normal(ks[18], (N_ODD, SSM_D_INNER, D), SSM_D_INNER ** -0.5),
        'moe_w_group': _normal(ks[19], (DEPTH, D, MOE_GROUPS), D ** -0.5),
        'moe_b_group': _normal(ks[20], (DEPTH, MOE_GROUPS), 0.01),
        'moe_w_expert': _normal(ks[21], (DEPTH, D, MOE_GROUPS, MOE_EXPERTS_PER_GROUP), D ** -0.5),
        'moe_b_expert': _normal(ks[22], (DEPTH, MOE_GROUPS, MOE_EXPERTS_PER_GROUP), 0.01),
        'moe_w1': _normal(ks[23], (DEPTH, MOE_EXPERTS, D, MOE_D_FF), D ** -0.5),
        'moe_w3': _normal(ks[24], (DEPTH, MOE_EXPERTS, D, MOE_D_FF), D ** -0.5),
        'moe_w2': _normal(ks[25], (DEPTH, MOE_EXPERTS, MOE_D_FF, D), MOE_D_FF ** -0.5),
        'final_norm_w': 1.0 + _normal(ks[26], (D,), 0.05),
    }

def second_block(x, c, ada_w, ada_b, norm1_w, norm2_w, mix_w_in, pool_w, pool_scale, rel_bias, mix_w_out,
              ssm_w_in, ssm_conv_w, ssm_conv_b, ssm_dt_bias, ssm_A_log, ssm_D, ssm_norm_w, ssm_w_out,
              moe_w_group, moe_b_group, moe_w_expert, moe_b_expert, moe_w1, moe_w3, moe_w2, final_norm_w):
    c_act = jax.nn.silu(c)
    for layer in range(DEPTH):
        mod = c_act @ ada_w[layer] + ada_b[layer]
        shift1, scale1, gate1, shift2, scale2, gate2 = jnp.split(mod, 6, axis=-1)
        h = modulate(rmsnorm_2(x, norm1_w[layer]), shift1, scale1)
        i = layer // 2
        if layer % 2 == 0:
            proj = h @ mix_w_in[i]
            u, q, k, v = jnp.split(proj, [POOL_WIDTH, POOL_WIDTH + ATT_WIDTH, POOL_WIDTH + 2 * ATT_WIDTH], axis=-1)
            a_out = pool_mixer(u, pool_w[i], pool_scale[i])
            b_out = chunk_attention(q, k, v, rel_bias[i])
            mix = jnp.concatenate([a_out, b_out], axis=-1) @ mix_w_out[i]
        else:
            mix = mamba2_mixer(h, ssm_w_in[i], ssm_conv_w[i], ssm_conv_b[i], ssm_dt_bias[i], ssm_A_log[i],
                               ssm_D[i], ssm_norm_w[i], ssm_w_out[i])
        x = x + gate1[:, None, :] * mix
        h2 = modulate(rmsnorm_2(x, norm2_w[layer]), shift2, scale2)
        ffn = hier_moe(h2, moe_w_group[layer], moe_b_group[layer], moe_w_expert[layer], moe_b_expert[layer],
                       moe_w1[layer], moe_w3[layer], moe_w2[layer])
        x = x + gate2[:, None, :] * ffn
    return rmsnorm_2(x, final_norm_w)


def setup_inputs(seed=0):
    out = dict(first_inputs(seed))
    for name, value in second_inputs(seed + 1).items():
        if name != "x":
            out[name + "_2"] = value
    return out


def reference(
    x, norm1_g, w_in, hg_lb, hg_norm_g, gla_w2, gla_b, gla_norm_g, cmp_pos_k, cmp_pos_v,
    cmp_w1_k, cmp_w2_k, cmp_w1_v, cmp_w2_v, w_br_hg, w_br_gla, w_br_nsa, w_out, norm2_g,
    w_ffn_gate, w_ffn_up, w_ffn_down, final_norm_g, c_2, ada_w_2, ada_b_2, norm1_w_2, norm2_w_2,
    mix_w_in_2, pool_w_2, pool_scale_2, rel_bias_2, mix_w_out_2, ssm_w_in_2, ssm_conv_w_2,
    ssm_conv_b_2, ssm_dt_bias_2, ssm_A_log_2, ssm_D_2, ssm_norm_w_2, ssm_w_out_2, moe_w_group_2,
    moe_b_group_2, moe_w_expert_2, moe_b_expert_2, moe_w1_2, moe_w3_2, moe_w2_2, final_norm_w_2,
):
    x = first_block(
        x, norm1_g, w_in, hg_lb, hg_norm_g, gla_w2, gla_b, gla_norm_g, cmp_pos_k, cmp_pos_v,
        cmp_w1_k, cmp_w2_k, cmp_w1_v, cmp_w2_v, w_br_hg, w_br_gla, w_br_nsa, w_out, norm2_g,
        w_ffn_gate, w_ffn_up, w_ffn_down, final_norm_g,
    )
    return second_block(
        x, c_2, ada_w_2, ada_b_2, norm1_w_2, norm2_w_2, mix_w_in_2, pool_w_2, pool_scale_2,
        rel_bias_2, mix_w_out_2, ssm_w_in_2, ssm_conv_w_2, ssm_conv_b_2, ssm_dt_bias_2,
        ssm_A_log_2, ssm_D_2, ssm_norm_w_2, ssm_w_out_2, moe_w_group_2, moe_b_group_2,
        moe_w_expert_2, moe_b_expert_2, moe_w1_2, moe_w3_2, moe_w2_2, final_norm_w_2,
    )


_drawn_inputs = setup_inputs


def setup_inputs(seed=0):
    import zlib

    import numpy as np

    out = dict(_drawn_inputs(seed))
    spreads = {}
    factors = {'hg_lb': 2.908,
     'hg_norm_g': 4.204,
     'gla_norm_g': 3.474,
     'cmp_pos_k': 22.271,
     'pool_scale_2': 3.583,
     'rel_bias_2': 4.864,
     'ssm_conv_b_2': 5.849,
     'ssm_D_2': 3.702,
     'ssm_norm_w_2': 3.419,
     'moe_b_group_2': 17.644,
     'moe_b_expert_2': 22.626,
     'cmp_pos_v': 2.886,
     'norm2_g': 3.132}
    for name, (base, spread) in spreads.items():
        noise = np.random.default_rng([zlib.crc32(name.encode()), seed]).standard_normal(out[name].shape)
        drawn = base * np.exp(spread * noise) if base else spread * noise
        out[name] = __import__('jax').numpy.asarray(drawn.astype(out[name].dtype))
    for name, factor in factors.items():
        out[name] = (out[name] * factor).astype(out[name].dtype)
    return out
```

```python
from contextlib import ExitStack

import numpy as np

import concourse.bass as bass
from concourse import mybir

ALU = mybir.AluOpType
ACT = mybir.ActivationFunctionType
F32 = mybir.dt.float32
U32 = mybir.dt.uint32
AX_X = mybir.AxisListType.X

P = 128
T = 256
TT = T // P
D = 1024
KD = D // P
DEPTH = 2
EPS = 1e-6
NEG = -1e30
BLOCKS = 16
UNIT = BLOCKS * P
RING = 6
BANK = 512

HG_H, HG_D = 4, 128
GLA_H, GLA_DK, GLA_DV, GLA_RANK = 4, 64, 128, 16
GLA_TAU = 16.0
NSA_H, NSA_G, NSA_DH = 8, 2, 64
CMP_STRIDE, CMP_BLK, CMP_HID = 16, 32, 128
NCMP = T // CMP_STRIDE - 1
ROT = NSA_DH // 4
THETA = 500000.0
N_BR = 3
FF = 2816
KF = FF // P
LEVELS = 7

CHUNK = 64
POOL_WINDOWS = (2, 4, 8, 16)
ATT_H, ATT_DH = 8, 64
REL = 256
SSM_IN = 2048
KS = SSM_IN // P
SSM_H, SSM_P, SSM_G, SSM_N, SSM_CONV = 32, 64, 8, 128, 4
KX = (SSM_IN + 2 * SSM_G * SSM_N) // P
E_G, E_PER = 4, 8
E_N = E_G * E_PER
RT = E_G + E_N



def columns(spec):
    at, out = 0, {}
    for name, n in spec:
        out[name] = (at, n)
        at += n
    return out, at


CONST, N_CONST = columns([
    ("ident", P), ("ones", P), ("upper", P + P), ("rot", P), ("cos", T), ("sin", T),
    ("causal_neg", 3 * P), ("chunk_neg", P), ("cmp_neg", TT * 32), ("cmp_keep", TT * 32), ("ssd", 3 * P),
    ("count", 4 * 16), ("iota4", 4), ("iota8", 8), ("level", LEVELS * P),
])
PAR1, N_PAR1 = columns([
    ("norm1", KD), ("norm2", KD), ("hg_norm", HG_H), ("gla_norm", GLA_H), ("gla_b", 2), ("gla_w2", 2 * P),
    ("pos_k", 16), ("pos_v", 16), ("w2_k", P), ("w2_v", NSA_DH),
])
PAR2, N_PAR2 = columns([
    ("norm1_0", KD), ("norm1_1", KD), ("norm2_0", KD), ("norm2_1", KD), ("final", KD), ("final_1", KD), ("c", KD),
    ("ada_b0", 48), ("ada_b1", 48), ("pool_w", 4 * P), ("pool_scale", 4), ("conv_w", SSM_CONV * KX),
    ("conv_b", KX), ("dt_b", SSM_H), ("a_log", SSM_H), ("d_skip", KS), ("ssm_norm", KS), ("w_dt", KD * SSM_H),
    ("router_0", KD * RT), ("router_1", KD * RT), ("router_b0", RT), ("router_b1", RT),
])

IN_AT = {}
_at = 0
for _n, _w in (("hq", 512), ("hf", 512), ("hi", 512), ("hog", 512), ("gq", 256), ("gk", 256), ("gv", 512),
               ("glr", 16), ("gog", 512), ("nq", 512), ("nkc", 128), ("nvc", 128), ("nks", 128), ("nvs", 128),
               ("nkw", 128), ("nvw", 128), ("ngate", 24), ("mgate", 3072)):
    IN_AT[_n] = (_at, _w)
    _at += _w
IN_COLS = _at

UNITS1 = [("hf", 2), ("hq", 2), ("hi", 2), ("misc", 1), ("gq", 1), ("gk", 1), ("gv", 2), ("nkc", 1), ("nvc", 1),
          ("nks", 1), ("nkw", 1), ("nq", 2), ("nvsw", 1), ("hog", 2), ("gog", 2), ("mgate", 12),
          ("w1k", 1), ("w1v", 1), ("br_hg", 2), ("br_gla", 2), ("br_nsa", 2), ("w_out", 4), ("ffn_gu", 22),
          ("ffn_d", 11)]
N_U1 = sum(n for _, n in UNITS1)
SLOTS1 = -(-N_U1 // RING) * RING
UNITS2 = [("ada0", 24), ("ada1", 24), ("mix_in", 8), ("mix_out", 4), ("moe0", 48), ("ssm_in", 24), ("ssm_out", 8),
          ("pad", 4), ("moe1", 48)]
N_U2 = sum(n for _, n in UNITS2)


def weight_blocks(w):
    k, n = w.shape
    return w.reshape(k // P, P, n // P, P).transpose(2, 0, 1, 3).reshape(-1, P, P)


def units_of(blocks):
    n = len(blocks) // BLOCKS
    return blocks.reshape(n, BLOCKS, P, P).transpose(0, 2, 1, 3).reshape(n, P, UNIT)


def token_major_units(w):
    k, n = w.shape
    per = UNIT // (k // P)
    return w.reshape(k // P, P, n // per, per).transpose(2, 1, 0, 3).reshape(-1, P, UNIT)


def feature_columns(v):
    return v.reshape(-1, P).T


def rows(v):
    return np.broadcast_to(v.reshape(1, -1), (P, v.size))


def pack(spec, total, parts, dtype=np.float32):
    out = np.zeros((P, total), dtype)
    for name, a in parts.items():
        at, n = spec[name]
        a = a.reshape(a.shape[0], -1)
        assert a.shape[1] == n, (name, a.shape, n)
        out[:a.shape[0], at:at + n] = a
    return out


def stream_hybrid(w_in, w1k, w1v, br_hg, br_gla, br_nsa, w_out, wg, wu, wd):
    def cols(name):
        at, n = IN_AT[name]
        return w_in[:, at:at + n]

    def twice(name):
        w = cols(name).reshape(D, NSA_G, 1, NSA_DH)
        return np.concatenate([w, w], axis=2).reshape(D, 2 * P)

    feature = lambda w: units_of(weight_blocks(w))
    misc = np.zeros((D, 2 * P), w_in.dtype)
    misc[:, 0:GLA_RANK] = cols("glr")
    misc[:, P:P + 24] = cols("ngate")
    gu = np.concatenate([wg.reshape(D, -1, 2 * P), wu.reshape(D, -1, 2 * P)], axis=2).reshape(D, 2 * FF)
    one = lambda w: w.reshape(BLOCKS, P, CMP_HID).transpose(1, 0, 2).reshape(1, P, UNIT)
    parts = {"hf": feature(cols("hf")), "hq": feature(cols("hq")), "hi": token_major_units(cols("hi")),
             "misc": token_major_units(misc), "gq": feature(cols("gq")), "gk": feature(cols("gk")),
             "gv": token_major_units(cols("gv")), "nkc": feature(twice("nkc")), "nvc": feature(twice("nvc")),
             "nks": feature(twice("nks")), "nkw": feature(twice("nkw")), "nq": feature(cols("nq")),
             "nvsw": token_major_units(np.concatenate([cols("nvs"), cols("nvw")], axis=1)),
             "hog": feature(cols("hog")), "gog": feature(cols("gog")), "mgate": feature(cols("mgate")),
             "w1k": one(w1k), "w1v": one(w1v), "br_hg": feature(br_hg), "br_gla": feature(br_gla),
             "br_nsa": feature(br_nsa), "w_out": feature(w_out), "ffn_gu": feature(gu), "ffn_d": feature(wd)}
    return [parts[name] for name, n in UNITS1]


def moe_units(w1, w3, w2):
    def up(e):
        return units_of(np.concatenate([weight_blocks(w1[e]), weight_blocks(w3[e])]))

    out = []
    for e in range(0, E_N, 2):
        out += [up(e), up(e + 1), w2[e:e + 2].transpose(1, 0, 2).reshape(1, P, UNIT)]
    return np.concatenate(out)


def constants():
    i = np.arange(P)
    t = np.arange(T)
    s_, t_ = i[:, None], i[None, :]
    upper = (s_ <= t_).astype(np.float32)
    ones = np.ones((P, P), np.float32)
    zeros = np.zeros((P, P), np.float32)
    rot = np.zeros((P, P), np.float32)
    half = ROT // 2
    for base in (0, NSA_DH):
        for j in range(half):
            rot[base + half + j, base + j] = 1.0
            rot[base + j, base + half + j] = 1.0
    inv = np.float32(THETA) ** (-np.arange(0, ROT, 2, dtype=np.float32) / np.float32(ROT))
    ang = np.arange(T, dtype=np.float32)[:, None] * inv.astype(np.float32)[None, :]
    cos, sin = np.cos(ang).T, np.sin(ang).T
    c = np.ones((P, T), np.float32)
    s = np.zeros((P, T), np.float32)
    for base in (0, NSA_DH):
        c[base:base + half], c[base + half:base + ROT] = cos, cos
        s[base:base + half], s[base + half:base + ROT] = -sin, sin
    n = np.arange(32)
    tok = i[:, None, None] + P * np.arange(TT)[None, :, None]
    keep = ((n * CMP_STRIDE + CMP_BLK - 1)[None, None, :] <= tok) & (n < NCMP)[None, None, :]
    count = np.stack([w / np.minimum(np.arange(16) + 1, w) for w in POOL_WINDOWS]).astype(np.float32)
    causal = np.where(t_ <= s_, 0.0, NEG).astype(np.float32)
    level = []
    for lv in range(LEVELS):
        m = 1 << lv
        level.append((s_ // (2 * m) == t_ // (2 * m)) & (s_ // m % 2 == 0) & (t_ // m % 2 == 1))
    return pack(CONST, N_CONST, {
        "ident": np.eye(P, dtype=np.float32), "ones": ones, "upper": np.concatenate([upper, ones], 1),
        "rot": rot, "cos": c, "sin": s,
        "causal_neg": np.concatenate([causal, zeros, causal], 1),
        "chunk_neg": np.where(t_ // CHUNK <= s_ // CHUNK, 0.0, NEG).astype(np.float32),
        "cmp_neg": np.where(keep, 0.0, NEG).astype(np.float32), "cmp_keep": keep.astype(np.float32),
        "ssd": np.concatenate([upper, ones, upper], 1), "count": rows(count), "iota4": rows(np.arange(4.0)),
        "iota8": rows(np.arange(8.0)), "level": np.concatenate(level, 1).astype(np.float32),
    })




class Count:

    def __init__(self, sem):
        self.sem, self.n, self.base = sem, 0, 0

    def one(self):
        self.n += 1
        return 1


class InOrder:

    def __init__(self, eng, count):
        self.eng, self.count = eng, count

    def __call__(self, ins):
        ins.then_inc(self.count.sem, self.count.one())
        self.eng.wait_ge(self.count.sem, self.count.n)


class Ring:

    def __init__(self, dram, buf, slot_full, unit_done):
        self.dram, self.buf, self.slot_full, self.unit_done = dram, buf, slot_full, unit_done
        self.place, self.used, self.index = 0, [0] * RING, None

    def load(self, sp, index, slot):
        src = self.dram[index, :, :] if isinstance(index, int) else \
            self.dram[bass.ds(index, 1), :, :].rearrange("o p n -> p (o n)")
        sp.dma_start(self.buf[:, slot, :], src).then_inc(self.slot_full[slot], 16)

    def claim(self, n):
        return Units(self, n)


class Units:

    def __init__(self, ring, n):
        self.ring, self.first, self.n, self.done0 = ring, ring.place, n, ring.unit_done.n
        self.turn = []
        for i in range(n):
            s = (self.first + i) % RING
            ring.used[s] += 1
            self.turn.append(ring.used[s])
        ring.place += n
        ring.unit_done.n += n

    def arrived(self, pe, i):
        s = (self.first + i) % RING
        pe.wait_ge(self.ring.slot_full[s], 16 * self.turn[i])
        return self.ring.buf[:, s, :]

    def refill(self, sp):
        for i in range(self.n):
            nxt = self.first + i + RING
            if self.ring.index(nxt) is None:
                nxt += RING
            if isinstance(self.ring.index(nxt), str):
                continue
            sp.wait_ge(self.ring.unit_done.sem, self.done0 + i + 1)
            self.ring.load(sp, self.ring.index(nxt), (self.first + i) % RING)


class Product:

    def __init__(self, units, block0, tiles, kt, banks, token_major=False):
        self.units, self.block0, self.kt, self.banks, self.token_major = units, block0, kt, banks, token_major
        self.pairs = []
        n = (tiles + 1) // 2
        for j in range(n):
            last = block0 + min(2 * (j + 1), tiles) * kt - 1
            if last % BLOCKS == BLOCKS - 1:
                done = (units.ring.unit_done.sem, units.done0 + last // BLOCKS + 1)
            else:
                banks.done.n += 1
                done = (banks.done.sem, banks.done.n)
            b = banks.take()
            self.pairs.append((b, banks.reads[b] - 1, done, min(2, tiles - 2 * j)))

    def psum(self, j):
        return self.banks.ps[:, self.pairs[j][0], :]

    def wait(self, eng, j):
        eng.wait_ge(*self.pairs[j][2])
        return self.psum(j)

    def read(self, j):
        return self.banks.read[self.pairs[j][0]]

    def after_read(self, eng, j):
        eng.wait_ge(self.read(j), self.pairs[j][1] + 1)

    def tensor(self, pe, x, j):
        b, before, done, tiles = self.pairs[j]
        if before:
            pe.wait_ge(self.banks.read[b], before)
        blk = self.block0 + 2 * j * self.kt
        for m in range(tiles):
            for k in range(self.kt):
                if blk % BLOCKS == 0 or (m == 0 and k == 0):
                    slot = self.units.arrived(pe, blk // BLOCKS)
                out = self.banks.ps[:, b, m * T:(m + 1) * T]
                if self.token_major:
                    ins = pe.matmul(out, x[:, k, m * P:(m + 1) * P], slot[:, k * 2 * P:(k + 1) * 2 * P],
                                    start=(k == 0), stop=(k == self.kt - 1))
                else:
                    at = blk % BLOCKS * P
                    ins = pe.matmul(out, slot[:, at:at + P], x[:, k, :], start=(k == 0), stop=(k == self.kt - 1))
                if blk % BLOCKS == BLOCKS - 1:
                    ins.then_inc(self.units.ring.unit_done.sem, 1)
                elif m == tiles - 1 and k == self.kt - 1:
                    ins.then_inc(self.banks.done.sem, 1)
                blk += 1


class Banks:

    def __init__(self, ps, read, done, n):
        self.ps, self.read, self.done, self.n = ps, read, done, n
        self.reads, self.turn = [0] * n, 0

    def take(self):
        b = self.turn
        self.turn = (b + 1) % self.n
        self.reads[b] += 1
        return b




def hybrid_and_moe(nc, stream, const_in, par1_in, lb_in, par2_in, bias_in, x_in, out):
    with ExitStack() as everywhere:
        def sem(name):
            return everywhere.enter_context(nc.semaphore(name))

        counts = []

        def signal(name):
            counts.append(Count(sem(name)))
            return counts[-1]

        def sb(name, shape, scope=everywhere, dt=F32):
            return scope.enter_context(nc.sbuf_tensor(name, shape, dt))

        ps = everywhere.enter_context(nc.psum_tensor("ps", [P, 8, BANK], F32))
        ringbuf = sb("weights", [P, RING, UNIT])
        const = sb("const", [P, N_CONST])
        par1 = sb("par1", [P, N_PAR1])
        par2 = sb("par2", [P, N_PAR2])
        xT = sb("xT", [P, KD, T])
        hT = sb("hT", [P, KD, T])
        sq = sb("sq", [P, KD, T])
        stat = sb("stat", [P, 4, T])
        small = sb("small", [P, 2, 8])

        def C(name, lo=0, n=None):
            at, w = CONST[name]
            return const[:, at + lo:at + lo + (w - lo if n is None else n)]

        def P1(name):
            at, w = PAR1[name]
            return par1[:, at:at + w]

        def P2(name):
            at, w = PAR2[name]
            return par2[:, at:at + w]

        ident, ones = C("ident"), C("ones")

        ring = Ring(stream, ringbuf, [sem(f"slot_full{i}") for i in range(RING)], signal("unit_done"))
        banks = Banks(ps, [sem(f"bank_read{i}") for i in range(4)], signal("bank_done"), 4)
        loaded = sem("inputs_loaded")
        par_loaded = sem("layer_parameters_loaded")
        stored = sem("output_stored")
        dve_step, act_step, pool_step = signal("dve_step"), signal("act_step"), signal("pool_step")
        squares, summed, variance, deviation = (signal(n) for n in ("squares", "summed", "variance", "deviation"))
        to_pe, to_pe2, to_act, to_act2, to_dve, to_dve2, to_pool = (
            signal(n) for n in ("for_tensor", "for_tensor2", "for_scalar", "for_scalar2", "for_vector",
                                "for_vector2", "for_gpsimd"))
        pv_done, pt_ready, pt_done, score_done, prob_ready = (
            signal(n) for n in ("values_weighted", "transposed_ready", "transposed", "scores_done", "probs_ready"))

        def new_block():
            for c in counts:
                c.base = c.n
            return nc.Block()

        def tell(ins, count):
            return ins.then_inc(count.sem, count.one())

        def restart_counts():
            with new_block() as block:
                @block.sync
                def _(sp):
                    for c in counts:
                        sp.sem_clear(c.sem)
                    for b in range(banks.n):
                        sp.sem_clear(banks.read[b])
                    sp.sem_clear(par_loaded)
            for c in counts:
                c.n = c.base = 0
            banks.reads, banks.turn = [0] * banks.n, 0

        def restart_ring():
            with new_block() as block:
                @block.sync
                def _(sp):
                    for s in range(RING):
                        sp.wait_ge(ring.slot_full[s], 16 * (ring.used[s] + 1))
            with new_block() as block:
                @block.sync
                def _(sp):
                    for s in range(RING):
                        sp.sem_clear(ring.slot_full[s])
            with new_block() as block:
                @block.sync
                def _(sp):
                    for s in range(RING):
                        sp.sem_inc(ring.slot_full[s], 16)
            ring.used = [0] * RING

        with new_block() as block:
            @block.sync
            def _(sp):
                for s in range(RING):
                    ring.load(sp, s, s)
                sp.wait_ge(loaded, 16 * 3)

            @block.scalar
            def _(act):
                act.dma_start(xT[:, :, :], x_in).then_inc(loaded, 16)
                act.dma_start(const[:, :], const_in).then_inc(loaded, 16)
                act.dma_start(par2[:, :], par2_in).then_inc(loaded, 16)


        def rms_norm(gain, shift=None, out=hT, width=D):
            with new_block() as block:
                @block.scalar
                def _(act):
                    for c in range(4):
                        tell(act.activation(sq[:, 2 * c:2 * c + 2, :], xT[:, 2 * c:2 * c + 2, :], ACT.Square), squares)
                    act.wait_ge(variance.sem, variance.base + 1)
                    tell(act.activation(stat[:, 1, :], stat[:, 0, :], ACT.Sqrt), deviation)

                @block.tensor
                def _(pe):
                    for k in range(KD):
                        if k % 2 == 0:
                            pe.wait_ge(squares.sem, squares.base + k // 2 + 1)
                        ins = pe.matmul(ps[:, 4, 0:T], ones, sq[:, k, :], start=(k == 0), stop=(k == KD - 1))
                    tell(ins, summed)

                @block.vector
                def _(dve):
                    done = InOrder(dve, dve_step)
                    dve.wait_ge(summed.sem, summed.base + 1)
                    tell(dve.tensor_scalar(stat[:, 0, :], ps[:, 4, 0:T], 1.0 / width, EPS, ALU.mult, ALU.add), variance)
                    dve.wait_ge(deviation.sem, deviation.base + 1)
                    done(dve.reciprocal(stat[:, 2, :], stat[:, 1, :]))
                    for k in range(KD):
                        ins = dve.scalar_tensor_tensor(out[:, k, :], xT[:, k, :], gain[:, k:k + 1], stat[:, 2, :],
                                                       ALU.mult, ALU.mult)
                        if shift is not None:
                            done(ins)
                            dve.tensor_scalar(out[:, k, :], out[:, k, :], shift[:, k:k + 1], None, ALU.add)

        def residual_product(n_units, kt, x, gate=None):
            w = ring.claim(n_units)
            prod = Product(w, 0, KD, kt, banks)
            with new_block() as block:
                @block.sync
                def _(sp):
                    w.refill(sp)

                @block.tensor
                def _(pe):
                    for j in range(KD // 2):
                        prod.tensor(pe, x, j)

                @block.vector
                def _(dve):
                    for j in range(KD // 2):
                        acc = prod.wait(dve, j)
                        for m in range(2):
                            k = 2 * j + m
                            if gate is None:
                                ins = dve.tensor_tensor(xT[:, k, :], xT[:, k, :], acc[:, m * T:(m + 1) * T], ALU.add)
                            else:
                                ins = dve.scalar_tensor_tensor(xT[:, k, :], acc[:, m * T:(m + 1) * T],
                                                               gate[:, k:k + 1], xT[:, k, :], ALU.mult, ALU.add)
                        ins.then_inc(prod.read(j), 1)

        hybrid = ExitStack()
        lb = sb("lb", [P, DEPTH * HG_H], hybrid)
        lbw = sb("lbw", [P, 6, HG_H], hybrid)
        ln_lb = sb("ln_lb", [P, DEPTH, HG_H], hybrid)
        ln_1m = sb("ln_1m", [P, DEPTH, HG_H], hybrid)
        lb_now = sb("lb_now", [P, 2, HG_H], hybrid)
        hf = sb("hf", [P, HG_H, T], hybrid)
        hq = sb("hq", [P, HG_H, T], hybrid)
        hk = sb("hk", [P, HG_H, T], hybrid)
        hv = sb("hv", [P, TT, 512], hybrid)
        hog = sb("hog", [P, 4, T], hybrid)
        gq = sb("gq", [P, 2, T], hybrid)
        gk = sb("gk", [P, 2, T], hybrid)
        gg = sb("gg", [P, 2, T], hybrid)
        gv = sb("gv", [P, TT, 512], hybrid)
        glr = sb("glr", [P, T], hybrid)
        gl_tok = sb("gl_tok", [P, TT, GLA_RANK], hybrid)
        gates = sb("gates", [P, TT, 24], hybrid)
        gog = sb("gog", [P, 4, T], hybrid)
        qk = sb("qk", [P, 10, T], hybrid)
        vc = sb("vc", [P, 2, T], hybrid)
        vsw = sb("vsw", [P, TT, 2 * P], hybrid)
        mg = sb("mg", [P, 24, T], hybrid)
        y = sb("y", [P, 3, 4, T], hybrid)
        W = sb("W", [P, 3, 4 * T], hybrid)
        scores = sb("scores", [P, 8, P], hybrid)
        cross = sb("cross", [P, 4, P], hybrid)

        with new_block() as block:
            @block.sync
            def _(sp):
                sp.dma_start(lb[:, :], lb_in).then_inc(loaded, 16)
                sp.wait_ge(loaded, 16 * 4)

            @block.vector
            def _(dve):
                done = InOrder(dve, dve_step)
                dve.wait_ge(loaded, 16 * 4)
                a0, a1 = lb[:, 0:HG_H], lb[:, HG_H:2 * HG_H]
                done(dve.tensor_tensor(lbw[:, 0, :], a0, a1, ALU.max))
                dve.tensor_tensor(lbw[:, 1, :], a0, lbw[:, 0, :], ALU.subtract)
                tell(dve.tensor_tensor(lbw[:, 2, :], a1, lbw[:, 0, :], ALU.subtract), to_act)
                dve.wait_ge(to_dve.sem, to_dve.base + 1)
                done(dve.tensor_tensor(lbw[:, 5, :], lbw[:, 3, :], lbw[:, 4, :], ALU.add))
                dve.memset(ln_lb[:, 0, :], NEG)
                tell(dve.memset(ln_1m[:, 0, :], 0.0), to_act)
                dve.wait_ge(to_dve.sem, to_dve.base + 2)
                dve.tensor_tensor(ln_lb[:, 1, :], lbw[:, 2, :], lbw[:, 0, :], ALU.subtract)
                dve.tensor_tensor(ln_1m[:, 1, :], lbw[:, 1, :], lbw[:, 0, :], ALU.subtract)

            @block.scalar
            def _(act):
                act.wait_ge(to_act.sem, to_act.base + 1)
                act.activation(lbw[:, 3, :], lbw[:, 1, :], ACT.Exp)
                tell(act.activation(lbw[:, 4, :], lbw[:, 2, :], ACT.Exp), to_dve)
                act.wait_ge(to_act.sem, to_act.base + 2)
                tell(act.activation(lbw[:, 0, :], lbw[:, 5, :], ACT.Ln), to_dve)

        def project_all(w):
            def product(at, tiles, token_major=False):
                return Product(w, at * BLOCKS, tiles, KD, banks, token_major)

            at, order = 0, []
            for name, n in UNITS1[:16]:
                order.append((name, product(at, 2 * n, name in ("hi", "misc", "gv", "nvsw")), n))
                at += n
            plain = {"hf": hf, "gk": gk, "nkc": qk[:, 4:6, :], "nks": qk[:, 6:8, :], "nkw": qk[:, 8:10, :],
                     "nq": qk[:, 0:4, :], "nvc": vc, "nvsw": None, "hi": hv, "gv": gv, "gq": gq, "misc": None}
            with new_block() as block:
                @block.sync
                def _(sp):
                    w.refill(sp)

                @block.tensor
                def _(pe):
                    for name, prod, n in order:
                        for j in range(n):
                            prod.tensor(pe, hT, j)

                @block.vector
                def _(dve):
                    for name, prod, n in order:
                        for j in range(n if name in plain else 0):
                            acc = prod.wait(dve, j)
                            if name == "misc":
                                acc3 = acc.rearrange("p (t n) -> p t n", t=TT)
                                dve.tensor_copy(gl_tok[:, :, :], acc3[:, :, 0:GLA_RANK])
                                ins = dve.tensor_copy(gates[:, :, :], acc3[:, :, P:P + 24])
                            elif name == "gq":
                                ins = dve.tensor_scalar(gq[:, :, :], acc.rearrange("p (m t) -> p m t", m=2),
                                                        GLA_DK ** -0.5, None, ALU.mult)
                            elif name == "nvsw":
                                ins = dve.tensor_copy(vsw[:, :, :], acc.rearrange("p (t n) -> p t n", t=TT))
                            elif name in ("hi", "gv"):
                                ins = dve.tensor_copy(plain[name][:, :, j * 2 * P:(j + 1) * 2 * P],
                                                      acc.rearrange("p (t n) -> p t n", t=TT))
                            else:
                                ins = dve.tensor_copy(plain[name][:, 2 * j:2 * j + 2, :],
                                                      acc.rearrange("p (m t) -> p m t", m=2))
                            ins.then_inc(prod.read(j), 1)

                @block.scalar
                def _(act):
                    for name, prod, n in order:
                        if name in plain:
                            continue
                        dst = {"hq": hq, "hog": hog, "gog": gog, "mgate": mg}[name]
                        func = ACT.Sigmoid if name == "mgate" else ACT.Silu
                        for j in range(n):
                            acc = prod.wait(act, j)
                            act.activation(dst[:, 2 * j:2 * j + 2, :], acc.rearrange("p (m t) -> p m t", m=2),
                                           func).then_inc(prod.read(j), 1)


        def log_sigmoid_tail(act, buf, wait_for, tell_to):
            done = InOrder(act, act_step)
            if wait_for is not None:
                act.wait_ge(*wait_for)
            done(act.activation(buf, buf, ACT.Abs))
            done(act.activation(buf, buf, ACT.Exp, scale=-1.0))
            tell(act.activation(buf, buf, ACT.Ln, bias=1.0), tell_to)

        def flat(a):
            return a.rearrange("p a b -> p (a b)")

        def prepare_hgrn(layer):
            c, dist = W[:, 1, :], W[:, 2, :]
            c3, dist3 = (a.rearrange("p (h t) -> p h t", h=HG_H) for a in (c, dist))
            with new_block() as block:
                @block.vector
                def _(dve):
                    done = InOrder(dve, dve_step)
                    dve.tensor_copy(lb_now[:, 0:1, :], ln_lb[:, bass.ds(layer, 1), :])
                    dve.tensor_copy(lb_now[:, 1:2, :], ln_1m[:, bass.ds(layer, 1), :])
                    tell(dve.tensor_copy(dist, flat(hf[:, :, :])), to_act)
                    dve.wait_ge(to_dve.sem, to_dve.base + 1)
                    done(dve.scalar_tensor_tensor(c, flat(hf[:, :, :]), 0.0, dist, ALU.min, ALU.subtract))
                    for h in range(HG_H):
                        ins = dve.tensor_scalar(c3[:, h, :], c3[:, h, :], lb_now[:, 1, h:h + 1], None, ALU.add)
                    done(ins)
                    tell(dve.tensor_tensor(flat(hk[:, :, :]), c, flat(hf[:, :, :]), ALU.subtract), to_act)
                    for h in range(HG_H):
                        ins = dve.tensor_scalar(dist3[:, h, :], c3[:, h, :], lb_now[:, 0, h:h + 1], None, ALU.subtract)
                    tell(ins, to_act)
                    dve.wait_ge(to_dve.sem, to_dve.base + 2)
                    for h in range(HG_H):
                        dve.scalar_tensor_tensor(hf[:, h, :], c3[:, h, :], lb_now[:, 0, h:h + 1], dist3[:, h, :],
                                                 ALU.max, ALU.add)

                @block.scalar
                def _(act):
                    log_sigmoid_tail(act, dist, (to_act.sem, to_act.base + 1), to_dve)
                    act.wait_ge(to_act.sem, to_act.base + 2)
                    act.activation(flat(hk[:, :, :]), flat(hk[:, :, :]), ACT.Exp)
                    log_sigmoid_tail(act, dist, (to_act.sem, to_act.base + 3), to_dve)

        def prepare_gla():
            with new_block() as block:
                @block.tensor
                def _(pe):
                    for t in range(TT):
                        ins = pe.transpose(ps[0:GLA_RANK, 4, t * P:(t + 1) * P], gl_tok[:, t, :], ident)
                    tell(ins, to_dve)
                    pe.wait_ge(to_pe.sem, to_pe.base + 1)
                    for m in range(2):
                        ins = pe.matmul(ps[:, 5, m * T:(m + 1) * T], P1("gla_w2")[0:GLA_RANK, m * P:(m + 1) * P],
                                        glr[0:GLA_RANK, :], start=True, stop=True)
                    tell(ins, to_dve)

                @block.vector
                def _(dve):
                    done = InOrder(dve, dve_step)
                    dve.wait_ge(to_dve.sem, to_dve.base + 1)
                    tell(dve.tensor_copy(glr[0:GLA_RANK, :], ps[0:GLA_RANK, 4, 0:T]), to_pe)
                    dve.wait_ge(to_dve.sem, to_dve.base + 2)
                    for m in range(2):
                        ins = dve.tensor_scalar(gg[:, m, :], ps[:, 5, m * T:(m + 1) * T], P1("gla_b")[:, m:m + 1],
                                                None, ALU.add)
                    done(ins)
                    tell(dve.tensor_copy(W[:, 2, 0:2 * T], flat(gg[:, :, :])), to_act)
                    dve.wait_ge(to_dve2.sem, to_dve2.base + 1)
                    done(dve.scalar_tensor_tensor(flat(gg[:, :, :]), flat(gg[:, :, :]), 0.0, W[:, 2, 0:2 * T],
                                                  ALU.min, ALU.subtract))
                    dve.tensor_scalar(gg[:, :, :], gg[:, :, :], 1.0 / GLA_TAU, None, ALU.mult)

                @block.scalar
                def _(act):
                    log_sigmoid_tail(act, W[:, 2, 0:2 * T], (to_act.sem, to_act.base + 1), to_dve2)

        def linear_attention(q, k, v, g, tiles, dk, gate, gain, branch):
            n = tiles * T
            b = W[:, 0, 0:n]
            b4 = b.rearrange("p (f t s) -> p f t s", f=tiles, t=TT)
            fold = [W[:, 1, 0:n], W[:, 2, 0:n]]
            decay = [flat(sq[:, 4 * i:4 * i + tiles, :]) for i in range(2)]
            qf, kf = flat(q[:, :, :]), flat(k[:, :, :])
            steps = LEVELS + 2
            per_head = P // dk

            def head(buf3, h, t):
                lo = h % per_head * dk
                return buf3[lo:lo + dk, h // per_head, t * P:(t + 1) * P]

            def place(h, t):
                return (t, h) if per_head == 1 else (h % 2, 2 * t + h // 2)

            def cross_place(h):
                return h if per_head == 1 else h % 2 * 2 + h // 2

            with new_block() as block:
                @block.vector
                def _(dve):
                    done = InOrder(dve, dve_step)
                    for f in range(tiles):
                        for t in range(TT):
                            ins = dve.tensor_tensor_scan(b4[:, f, t, :], ones, g[:, f, t * P:(t + 1) * P], 0.0,
                                                         ALU.mult, ALU.add)
                    done(ins)

                    def halves(a, lv):
                        m = 1 << lv
                        v4 = a.rearrange("p (n two m) -> p n two m", two=2, m=m)
                        return v4[:, :, 0, :], v4[:, :, 1, :]

                    def exponents(lv):
                        if lv >= 2:
                            dve.wait_ge(to_pe.sem, to_pe.base + lv - 1)
                        first, second = halves(b, lv)
                        e1, e2 = halves(decay[lv % 2], lv)
                        ref = first[:, :, (1 << lv) - 1:1 << lv].broadcast_to(list(first.shape))
                        dve.tensor_tensor(e1, ref, first, ALU.subtract)
                        if lv < LEVELS:
                            ins = dve.tensor_tensor(e2, second, ref, ALU.subtract)
                        else:
                            ins = dve.tensor_copy(e2, second)
                        tell(ins, to_act)

                    def weigh(lv):
                        dve.wait_ge(to_dve.sem, to_dve.base + lv + 1)
                        if lv >= 2:
                            dve.wait_ge(score_done.sem, score_done.base + lv)
                        e1, e2 = halves(decay[lv % 2], lv)
                        f1, f2 = halves(fold[lv % 2], lv)
                        dve.tensor_tensor(f1, halves(kf, lv)[0], e1, ALU.mult)
                        tell(dve.tensor_tensor(f2, halves(qf, lv)[1], e2, ALU.mult), to_pe)

                    def pick(step):
                        dve.wait_ge(score_done.sem, score_done.base + step + 1)
                        if step:
                            dve.wait_ge(prob_ready.sem, prob_ready.base + step)
                        bank = 4 + step % 2 * 2
                        if step == 0:
                            for i in range(2):
                                ins = dve.tensor_tensor(
                                    scores[:, 4 * i:4 * i + 4, :],
                                    ps[:, bank + i, :].rearrange("p (h t) -> p h t", h=4),
                                    ident.unsqueeze(1).broadcast_to([P, 4, P]), ALU.mult)
                        elif step <= LEVELS:
                            mask = C("level", (step - 1) * P, P).bitcast(U32).unsqueeze(1).broadcast_to([P, 4, P])
                            for i in range(2):
                                ins = dve.copy_predicated(scores[:, 4 * i:4 * i + 4, :], mask,
                                                          ps[:, bank + i, :].rearrange("p (h t) -> p h t", h=4))
                        else:
                            for i in range(per_head):
                                w = 4 // per_head
                                ins = dve.tensor_copy(cross[:, i * w:(i + 1) * w, :],
                                                      ps[:, bank + i, 0:w * P].rearrange("p (h t) -> p h t", h=w))
                        tell(ins, prob_ready)

                    exponents(0)
                    for step in range(steps):
                        if step + 1 < LEVELS + 1:
                            exponents(step + 1)
                        if step < LEVELS + 1:
                            weigh(step)
                        pick(step)
                    dve.wait_ge(to_act.sem, to_act.base + LEVELS + 1)
                    dve.wait_ge(to_pe.sem, to_pe.base + LEVELS + 1)
                    dve.wait_ge(summed.sem, summed.base + 1)
                    for i in range(2):
                        ins = dve.tensor_scalar(W[:, 0, i * BANK:(i + 1) * BANK], ps[:, 6 + i, :], 1.0 / 128, EPS,
                                                ALU.mult, ALU.add)
                    tell(ins, variance)
                    dve.wait_ge(deviation.sem, deviation.base + 1)
                    done(dve.reciprocal(W[:, 0, :], W[:, 0, :]))
                    for h in range(4):
                        ins = dve.scalar_tensor_tensor(
                            W[:, 1, h * T:(h + 1) * T], ps[:, 4 + h // 2, h % 2 * T:(h % 2 + 1) * T],
                            gain[:, h:h + 1], W[:, 0, h * T:(h + 1) * T], ALU.mult, ALU.mult)
                    done(ins)
                    dve.tensor_tensor(flat(y[:, branch, :, :]), W[:, 1, :], flat(gate[:, :, :]), ALU.mult)

                @block.scalar
                def _(act):
                    for lv in range(LEVELS + 1):
                        act.wait_ge(to_act.sem, to_act.base + lv + 1)
                        tell(act.activation(decay[lv % 2], decay[lv % 2], ACT.Exp), to_dve)
                    act.wait_ge(pv_done.sem, pv_done.base + 1)
                    for i in range(2):
                        ins = act.activation(flat(sq[:, 2 * i:2 * i + 2, :]), ps[:, 4 + i, :], ACT.Square)
                    tell(ins, squares)
                    act.wait_ge(variance.sem, variance.base + 1)
                    tell(act.activation(W[:, 0, :], W[:, 0, :], ACT.Sqrt), deviation)

                @block.tensor
                def _(pe):
                    for step in range(steps):
                        if step:
                            pe.wait_ge(to_pe.sem, to_pe.base + step)
                        if step >= 2:
                            pe.wait_ge(prob_ready.sem, prob_ready.base + step - 1)
                        bank = 4 + step % 2 * 2
                        f3 = fold[(step - 1) % 2].rearrange("p (f t) -> p f t", f=tiles)
                        for t in range(TT if step <= LEVELS else 1):
                            for h in range(4):
                                i, c0 = place(h, t)
                                out_ = ps[:, bank + i, c0 * P:(c0 + 1) * P]
                                if step == 0:
                                    a, c = head(k, h, t), head(q, h, t)
                                elif step <= LEVELS:
                                    a = c = head(f3, h, t)
                                else:
                                    a, c = head(f3, h, 0), head(f3, h, 1)
                                ins = pe.matmul(out_, a, c, start=True, stop=True)
                        tell(ins, score_done)
                    pe.wait_ge(prob_ready.sem, prob_ready.base + steps)
                    for h in range(4):
                        o = ps[:, 4 + h // 2, h % 2 * T:(h % 2 + 1) * T]
                        vh = [v[:, t, h * P:(h + 1) * P] for t in range(TT)]
                        own = [scores[:, 4 * place(h, t)[0] + place(h, t)[1], :] for t in range(TT)]
                        pe.matmul(o[:, 0:P], vh[0], own[0], start=True, stop=True)
                        pe.matmul(o[:, P:T], vh[1], own[1], start=True, stop=False)
                        ins = pe.matmul(o[:, P:T], vh[0], cross[:, cross_place(h), :], start=False, stop=True)
                    tell(ins, pv_done)
                    pe.wait_ge(squares.sem, squares.base + 1)
                    for i in range(2):
                        ins = pe.matmul(ps[:, 6 + i, :], ones, flat(sq[:, 2 * i:2 * i + 2, :]), start=True, stop=True)
                    tell(ins, summed)

        def attention(block, items, q_of, k_of, add_of, weight_of, small, prob, turned, values, act_after):
            parts = ((0, P), (P, 3 * P))

            @block.tensor
            def _(pe):
                def score(i):
                    if i >= 2:
                        pe.wait_ge(to_pe.sem, to_pe.base + i - 1)
                    for t, (lo, hi) in enumerate(parts):
                        ins = pe.matmul(ps[:, 4 + i % 2, lo:hi], q_of(i, t), k_of(i, hi - lo), start=True, stop=True)
                    tell(ins, score_done)

                def turn(i):
                    pe.wait_ge(prob_ready.sem, prob_ready.base + i + 1)
                    if i >= 2:
                        pe.wait_ge(pt_ready.sem, pt_ready.base + i - 1)
                    for c in range(3):
                        ins = pe.transpose(ps[:, 6 + i % 2, c * P:(c + 1) * P], prob[i % 2][:, c * P:(c + 1) * P], ident)
                    tell(ins, pt_done)

                score(0)
                score(1)
                for i in range(items):
                    turn(i)
                    if i + 2 < items:
                        score(i + 2)
                    values(pe, i)

            @block.vector
            def _(dve):
                done = InOrder(dve, dve_step)

                def rows_max(i):
                    s = small[:, i % 2, :]
                    dve.wait_ge(score_done.sem, score_done.base + i + 1)
                    if i >= 2:
                        dve.wait_ge(pt_done.sem, pt_done.base + i - 1)
                    tell(dve.scalar_tensor_tensor(prob[i % 2], ps[:, 4 + i % 2, 0:3 * P], NSA_DH ** -0.5, add_of(i),
                                                  ALU.mult, ALU.add), to_pe)
                    dve.wait_ge(to_pe.sem, to_pe.n)
                    for t, (lo, hi) in enumerate(parts):
                        ins = dve.tensor_reduce(s[:, t:t + 1], prob[i % 2][:, lo:hi], AX_X, ALU.max)
                    done(ins)
                    tell(dve.tensor_scalar(s[:, 2:4], s[:, 0:2], -1.0, None, ALU.mult), to_act)

                def normalise(i):
                    s = small[:, i % 2, :]
                    dve.wait_ge(to_dve.sem, to_dve.base + i + 1)
                    done(dve.reciprocal(s[:, 6:8], s[:, 4:6]))
                    if weight_of(i) is not None:
                        done(dve.tensor_tensor(s[:, 6:8], s[:, 6:8], weight_of(i), ALU.mult))
                    for t, (lo, hi) in enumerate(parts):
                        ins = dve.tensor_scalar(prob[i % 2][:, lo:hi], prob[i % 2][:, lo:hi], s[:, 6 + t:7 + t], None,
                                                ALU.mult)
                    tell(ins, prob_ready)

                rows_max(0)
                for i in range(items):
                    if i + 1 < items:
                        rows_max(i + 1)
                    normalise(i)

            @block.scalar
            def _(act):
                def exponentials(i):
                    s = small[:, i % 2, :]
                    act.wait_ge(to_act.sem, to_act.base + i + 1)
                    for t, (lo, hi) in enumerate(parts):
                        ins = act.activation(prob[i % 2][:, lo:hi], prob[i % 2][:, lo:hi], ACT.Exp,
                                             bias=s[:, 2 + t:3 + t], accum_out=s[:, 4 + t:5 + t])
                    tell(ins, to_dve)

                exponentials(0)
                for i in range(items):
                    if i + 1 < items:
                        exponentials(i + 1)
                    act.wait_ge(pt_done.sem, pt_done.base + i + 1)
                    act_after(act, i)
                    tell(act.copy(turned(i), ps[:, 6 + i % 2, 0:3 * P]), pt_ready)
                act_after(act, items)

        cstat = sb("cstat", [P, 4, 16], hybrid)
        kcd = sb("kcd", [P, 2 * NCMP], hybrid)
        vcm = sb("vcm", [P, NSA_G * NSA_DH], hybrid)
        hid = sb("hid", [P, 2, 2 * NCMP], hybrid)

        def rope():
            with new_block() as block:
                @block.tensor
                def _(pe):
                    for j in range(5):
                        if j == 4:
                            pe.wait_ge(to_pe.sem, to_pe.base + 1)
                        tell(pe.matmul(ps[:, 4 + j % 4, :], C("rot"), flat(qk[:, 2 * j:2 * j + 2, :]), start=True,
                                       stop=True), to_dve)

                @block.vector
                def _(dve):
                    done = InOrder(dve, dve_step)
                    cos, sin = (C(n).unsqueeze(1).broadcast_to([P, 2, T]) for n in ("cos", "sin"))
                    for j in range(5):
                        x = qk[:, 2 * j:2 * j + 2, :]
                        turned = W[:, j % 2, 0:BANK].rearrange("p (m t) -> p m t", m=2)
                        dve.wait_ge(to_dve.sem, to_dve.base + j + 1)
                        ins = dve.tensor_tensor(turned, ps[:, 4 + j % 4, :].rearrange("p (m t) -> p m t", m=2), sin,
                                                ALU.mult)
                        if j == 0:
                            tell(ins, to_pe)
                        done(dve.tensor_tensor(x, x, cos, ALU.mult))
                        done(dve.tensor_tensor(x, x, turned, ALU.add))

        def compress(w):
            kd = [W[:, 0, i * 2 * T:(i + 1) * 2 * T].rearrange("p (g t) -> p g t", g=2) for i in range(2)]
            with new_block() as block:
                @block.sync
                def _(sp):
                    w.refill(sp)

                @block.vector
                def _(dve):
                    for i, src in enumerate((qk[:, 4:6, :], vc[:, :, :])):
                        dve.tensor_copy(kd[i][0:NSA_DH, :, :], src[0:NSA_DH, :, :])
                        ins = dve.tensor_copy(kd[i][NSA_DH:P, :, 0:T - 1], src[NSA_DH:P, :, 1:T])
                        tell(ins, to_pe)
                    for i in range(2):
                        dve.wait_ge(ring.unit_done.sem, w.done0 + i + 1)
                        tell(dve.tensor_copy(cstat[:, 0, i:i + 1], ps[:, 4 + i, 64:65]), to_act)
                    dve.wait_ge(to_dve.sem, to_dve.base + 1)
                    dve.tensor_copy(kcd[:, :], ps[:, 6, 0:2 * NCMP])
                    for i in range(4):
                        dve.tensor_copy(vcm[32 * i:32 * i + NCMP, :], ps[32 * i:32 * i + NCMP, 7, 0:NSA_G * NSA_DH])

                @block.tensor
                def _(pe):
                    for i, pos in enumerate(("pos_k", "pos_v")):
                        slot = w.arrived(pe, i)
                        pe.wait_ge(to_pe.sem, to_pe.base + i + 1)
                        for what in range(2):
                            for j in range(BLOCKS):
                                if what:
                                    x, o = P1(pos)[:, j:j + 1], ps[:, 4 + i, 64:65]
                                else:
                                    x = kd[i][:, :, 2 * j:2 * j + CMP_STRIDE * (NCMP - 1) + 1:CMP_STRIDE]
                                    o = ps[:, 4 + i, 0:2 * NCMP].rearrange("p (g n) -> p g n", g=2)
                                ins = pe.matmul(o, slot[:, j * P:(j + 1) * P], x, start=(j == 0), stop=(j == BLOCKS - 1))
                        ins.then_inc(ring.unit_done.sem, 1)
                    pe.wait_ge(to_pe2.sem, to_pe2.base + 1)
                    pe.matmul(ps[:, 6, 0:2 * NCMP], P1("w2_k"), hid[:, 0, :], start=True, stop=True)
                    for i in range(4):
                        for g in range(NSA_G):
                            ins = pe.matmul(ps[32 * i:32 * i + NCMP, 7, g * NSA_DH:(g + 1) * NSA_DH],
                                            hid[:, 1, g * NCMP:(g + 1) * NCMP], P1("w2_v"), start=True, stop=True,
                                            tile_position=(0, 32 * i))
                    tell(ins, to_dve)

                @block.scalar
                def _(act):
                    for i in range(2):
                        act.wait_ge(to_act.sem, to_act.base + i + 1)
                        ins = act.activation(hid[:, i, :], ps[:, 4 + i, 0:2 * NCMP], ACT.Gelu_apprx_tanh,
                                             bias=cstat[:, 0, i:i + 1])
                    tell(ins, to_pe2)
                    act.activation(flat(gates[:, :, :]), flat(gates[:, :, :]), ACT.Sigmoid)

        def query_half(h, buf, t):
            lo = h % 2 * NSA_DH
            return buf[lo:lo + NSA_DH, h // 2, t * P:(t + 1) * P]

        pc = W[:, 1, 0:BANK].rearrange("p (t h n) -> p t h n", t=TT, h=NSA_H)
        ptc = W[:, 2, 0:BANK].rearrange("p (i t) -> p i t", i=4)

        def compressed_probabilities():
            def over_heads(name, n):
                return C(name).rearrange("p (t n) -> p t n", t=TT)[:, :, 0:n].unsqueeze(2) \
                    .broadcast_to([P, TT, NSA_H, n])

            def over_keys(a, n):
                return a.rearrange("p (t h) -> p t h", t=TT).unsqueeze(3).broadcast_to([P, TT, NSA_H, n])

            with new_block() as block:
                @block.tensor
                def _(pe):
                    for t in range(TT):
                        for h in range(NSA_H):
                            lo, g = h % 2 * NSA_DH, h // 4
                            at = t * P + h // 2 * 32
                            ins = pe.matmul(ps[:, 4 + h % 2, at:at + NCMP], query_half(h, qk, t),
                                            kcd[lo:lo + NSA_DH, g * NCMP:(g + 1) * NCMP], start=True, stop=True)
                    tell(ins, score_done)
                    pe.wait_ge(prob_ready.sem, prob_ready.base + 1)
                    for i in range(4):
                        ins = pe.transpose(ps[:, 6, i * P:(i + 1) * P], W[:, 1, i * P:(i + 1) * P], ident)
                    tell(ins, pt_done)

                @block.vector
                def _(dve):
                    done = InOrder(dve, dve_step)
                    done(dve.memset(W[:, 1, 0:BANK], 0.0))
                    dve.wait_ge(score_done.sem, score_done.base + 1)
                    pairs = pc.rearrange("p t (h two) n -> p t h two n", two=2)
                    for i in range(2):
                        s4 = ps[:, 4 + i, 0:T].rearrange("p (t h n) -> p t h n", t=TT, h=NSA_H // 2)
                        ins = dve.tensor_tensor(pairs[:, :, :, i, 0:NCMP], s4[:, :, :, 0:NCMP],
                                                over_heads("cmp_neg", NCMP)[:, :, 0:NSA_H // 2, :], ALU.add)
                    done(ins)
                    done(dve.tensor_reduce(cstat[:, 1, :].rearrange("p (t h) -> p t h", t=TT), pc[:, :, :, 0:NCMP], AX_X,
                                           ALU.max))
                    tell(dve.tensor_tensor(pc[:, :, :, 0:NCMP], pc[:, :, :, 0:NCMP], over_keys(cstat[:, 1, :], NCMP),
                                           ALU.subtract), to_act)
                    dve.wait_ge(to_dve.sem, to_dve.base + 1)
                    done(dve.tensor_reduce(cstat[:, 2, :].rearrange("p (t h) -> p t h", t=TT), pc[:, :, :, 0:NCMP], AX_X,
                                           ALU.add))
                    done(dve.reciprocal(cstat[:, 3, :], cstat[:, 2, :]))
                    gate = gates[:, :, :].rearrange("p t (h k) -> p t h k", k=3)[:, :, :, 0]
                    rec = cstat[:, 3, :].rearrange("p (t h) -> p t h", t=TT)
                    dve.tensor_tensor(rec, rec, gate, ALU.mult)
                    done(dve.tensor_tensor(pc, pc, over_heads("cmp_keep", 32), ALU.mult))
                    tell(dve.tensor_tensor(pc, pc, over_keys(cstat[:, 3, :], 32), ALU.mult), prob_ready)
                    dve.wait_ge(pt_done.sem, pt_done.base + 1)
                    dve.tensor_copy(W[:, 2, 0:BANK], ps[:, 6, :])

                @block.scalar
                def _(act):
                    act.wait_ge(to_act.sem, to_act.base + 1)
                    tell(act.activation(W[:, 1, 0:BANK], W[:, 1, 0:BANK], ACT.Exp, scale=NSA_DH ** -0.5), to_dve)

        def sparse_attention():
            sqf = flat(sq[:, :, :])
            turned = lambda i: sqf[:, i % 4 * BANK:i % 4 * BANK + 3 * P]
            prob = [W[:, 0, 0:3 * P], W[:, 0, BANK:BANK + 3 * P]]
            gate4 = gates[:, :, :].rearrange("p t (h k) -> p t h k", k=3)

            def values(pe, i):
                if i % 2 == 0:
                    return
                h = i // 2
                g, lo, c32 = h // 4, h % 2 * NSA_DH, 32 * (h % 4)
                pe.wait_ge(pt_ready.sem, pt_ready.base + i + 1)
                for t in range(TT):
                    o = ps[lo:lo + NSA_DH, h // 2, t * P:(t + 1) * P]
                    pe.matmul(o, vcm[c32:c32 + NCMP, g * NSA_DH:(g + 1) * NSA_DH],
                              ptc[c32:c32 + NCMP, 2 * t + h // 4, :], start=True, stop=False, tile_position=(c32, lo))
                    for b in range(2):
                        for s in range(t + 1):
                            ins = pe.matmul(o, vsw[:, s, b * P + g * NSA_DH:b * P + (g + 1) * NSA_DH],
                                            turned(2 * h + b)[:, (t + s) * P:(t + s + 1) * P], start=False,
                                            stop=(b == 1 and s == t))
                tell(ins, pv_done)

            def act_after(act, i):
                if 4 <= i < 2 * NSA_H:
                    act.wait_ge(pv_done.sem, pv_done.base + (i - 4) // 2 + 1)
                if i == 2 * NSA_H:
                    act.wait_ge(pv_done.sem, pv_done.base + NSA_H)
                    for m in range(4):
                        act.copy(y[:, 2, m, :], ps[:, m, 0:T])

            with new_block() as block:
                attention(block, 2 * NSA_H, lambda i, t: query_half(i // 2, qk, t),
                          lambda i, n: qk[i // 2 % 2 * NSA_DH:(i // 2 % 2 + 1) * NSA_DH, 6 + 2 * (i % 2) + i // 8, 0:n],
                          lambda i: C("causal_neg"), lambda i: gate4[:, :, i // 2, 1 + i % 2],
                          small, prob, turned, values, act_after)

        def mix_branches():
            w = ring.claim(6)
            prods = [Product(w, 2 * BLOCKS * b, KD, 4, banks) for b in range(N_BR)]
            with new_block() as block:
                @block.sync
                def _(sp):
                    w.refill(sp)

                @block.tensor
                def _(pe):
                    for b in range(N_BR):
                        for j in range(KD // 2):
                            prods[b].tensor(pe, y[:, b, :, :], j)

                @block.vector
                def _(dve):
                    done = InOrder(dve, dve_step)
                    for b in range(N_BR):
                        for j in range(KD // 2):
                            acc = prods[b].wait(dve, j)
                            gate = flat(mg[:, 8 * b + 2 * j:8 * b + 2 * j + 2, :])
                            m = flat(hT[:, 2 * j:2 * j + 2, :])
                            if b == 0:
                                dve.tensor_tensor(m, acc, gate, ALU.mult).then_inc(prods[b].read(j), 1)
                            else:
                                part = W[:, j % 2, 0:BANK]
                                dve.tensor_tensor(part, acc, gate, ALU.mult).then_inc(prods[b].read(j), 1)
                                prods[b].after_read(dve, j)
                                done(dve.tensor_tensor(m, m, part, ALU.add))

        def swiglu_hidden():
            w = ring.claim(22)
            prod = Product(w, 0, 2 * KF, KD, banks)
            sqf = flat(sq[:, :, :])
            with new_block() as block:
                @block.sync
                def _(sp):
                    w.refill(sp)

                @block.tensor
                def _(pe):
                    for j in range(KF):
                        prod.tensor(pe, hT, j)

                @block.scalar
                def _(act):
                    for i in range(KF // 2):
                        acc = prod.wait(act, 2 * i)
                        if i >= 4:
                            prod.after_read(act, 2 * i - 7)
                        act.activation(sqf[:, i % 4 * BANK:(i % 4 + 1) * BANK], acc, ACT.Silu) \
                            .then_inc(prod.read(2 * i), 1)

                @block.vector
                def _(dve):
                    for i in range(KF // 2):
                        acc = prod.wait(dve, 2 * i + 1)
                        prod.after_read(dve, 2 * i)
                        dve.tensor_tensor(flat(mg[:, 2 * i:2 * i + 2, :]), sqf[:, i % 4 * BANK:(i % 4 + 1) * BANK],
                                          acc, ALU.mult).then_inc(prod.read(2 * i + 1), 1)

        def unit1(layer):
            def index(place):
                if place < N_U1:
                    return layer * N_U1 + place
                return None if place < SLOTS1 else (layer + 1) * N_U1 + place - SLOTS1
            return index

        restart_counts()
        with nc.Fori(0, DEPTH) as layer:
            ring.place, ring.index = 0, unit1(layer)
            with new_block() as block:
                @block.scalar
                def _(act):
                    act.dma_start(par1[:, :], par1_in[bass.ds(layer, 1), :, :].rearrange("o p n -> p (o n)")) \
                        .then_inc(par_loaded, 16)
                    act.wait_ge(par_loaded, 16)
            rms_norm(P1("norm1"))
            project_all(ring.claim(34))
            prepare_hgrn(layer)
            linear_attention(hq, hk, hv, hf, HG_H, HG_D, hog, P1("hg_norm"), 0)
            prepare_gla()
            linear_attention(gq, gk, gv, gg, GLA_H * GLA_DK // P, GLA_DK, gog, P1("gla_norm"), 1)
            rope()
            compress(ring.claim(2))
            compressed_probabilities()
            sparse_attention()
            mix_branches()
            residual_product(4, KD, hT)
            rms_norm(P1("norm2"))
            swiglu_hidden()
            residual_product(11, KF, mg)
            restart_counts()
            restart_ring()
        rms_norm(P2("final_1"), out=xT)
        hybrid.close()

        def index2(place):
            first_pad = 140
            if place < first_pad:
                return DEPTH * N_U1 + place
            if place < first_pad + 4:
                return None
            return DEPTH * N_U1 + place - 4 if place < N_U2 else "end"

        ring.place, ring.index = 0, index2
        adaln = everywhere.enter_context(ExitStack())
        cact = sb("cact", [P, KD], adaln)
        mod = sb("mod", [P, 2, 48], adaln)
        mgain = sb("mgain", [P, 4, KD], adaln)
        logits = sb("logits", [P, TT, RT], adaln)
        rtmp = sb("rtmp", [P, TT, 80], adaln)
        combine = sb("combine", [P, TT, E_N], adaln)
        ccol = sb("ccol", [P, TT, 4], adaln)

        def modulation():
            with new_block() as block:
                @block.scalar
                def _(act):
                    act.activation(cact[:, :], P2("c"), ACT.Silu)
            for l in range(2):
                w = ring.claim(24)
                with new_block() as block:
                    @block.sync
                    def _(sp):
                        w.refill(sp)

                    @block.tensor
                    def _(pe):
                        for i in range(24):
                            slot = w.arrived(pe, i)
                            for m in range(2):
                                for k in range(KD):
                                    at = (m * KD + k) * P
                                    ins = pe.matmul(ps[:, 4 + l, 2 * i + m:2 * i + m + 1], slot[:, at:at + P],
                                                    cact[:, k:k + 1], start=(k == 0), stop=(k == KD - 1))
                            ins.then_inc(ring.unit_done.sem, 1)

                    @block.vector
                    def _(dve):
                        done = InOrder(dve, dve_step)
                        dve.wait_ge(ring.unit_done.sem, w.done0 + 24)
                        done(dve.tensor_tensor(mod[:, l, :], ps[:, 4 + l, 0:48], P2(f"ada_b{l}"), ALU.add))
                        for i, scale_at in enumerate((8, 32)):
                            dve.scalar_tensor_tensor(mgain[:, 2 * l + i, :], mod[:, l, scale_at:scale_at + 8], 1.0,
                                                     P2(f"norm{i + 1}_{l}"), ALU.add, ALU.mult)

        def shift(l, i):
            return mod[:, l, 24 * i:24 * i + 8]

        def gate(l, i):
            return mod[:, l, 24 * i + 16:24 * i + 24]

        def pool_and_chunk_attention():
            pa = ExitStack()
            u = sb("u", [P, 3, 4, T], pa)
            q = sb("q", [P, 4, T], pa)
            k = sb("k", [P, 4, T], pa)
            v = sb("v", [P, TT, 512], pa)
            cat = sb("cat", [P, KD, T], pa)
            bias = sb("bias", [P, ATT_H, 3 * P], pa)
            rev = sb("rev", [P, ATT_H, 3 * P], pa)
            probs = sb("probs", [P, 2, 3 * P], pa)
            w = ring.claim(8)
            prods = [Product(w, 2 * BLOCKS * i, 4, KD, banks, token_major=(i == 3)) for i in range(4)]
            with new_block() as block:
                @block.sync
                def _(sp):
                    w.refill(sp)

                @block.tensor
                def _(pe):
                    for prod in prods:
                        for j in range(2):
                            prod.tensor(pe, hT, j)

                @block.vector
                def _(dve):
                    for prod, dst in zip(prods, (u[:, 0, :, :], q, k, v)):
                        for j in range(2):
                            acc = prod.wait(dve, j).rearrange("p (m t) -> p m t", m=2)
                            to = dst[:, :, j * T:(j + 1) * T] if dst is v else dst[:, 2 * j:2 * j + 2, :]
                            dve.tensor_copy(to, acc).then_inc(prod.read(j), 1)

                @block.scalar
                def _(act):
                    for h in range(ATT_H):
                        for lo, n, first in ((0, P, REL - (P - 1)), (P, 2 * P, REL + P - (T - 1))):
                            row = bias_in[h, first:first + P + n - 1]
                            src = bass.AP(tensor=row.tensor, offset=row.offset, ap=[[1, P], [1, n]])
                            act.dma_start(rev[:, h, lo:lo + n], src).then_inc(loaded, 16)
                    act.wait_ge(loaded, 16 * (4 + 2 * ATT_H))
            with new_block() as block:
                @block.vector
                def _(dve):
                    done = InOrder(dve, dve_step)
                    for lo, n in ((0, P), (P, 2 * P)):
                        ins = dve.tensor_copy(bias[:, :, lo:lo + n], rev[:, :, lo:lo + n][:, :, ::-1])
                    done(ins)
                    for lo in (0, 2 * P):
                        dve.tensor_tensor(bias[:, :, lo:lo + P], bias[:, :, lo:lo + P],
                                          C("chunk_neg").unsqueeze(1).broadcast_to([P, ATT_H, P]), ALU.add)
                    for d in range(4):
                        s = 1 << d
                        src, dst = u[:, 0 if d == 0 else 1 + (d - 1) % 2, :, :], u[:, 1 + d % 2, :, :]
                        dve.tensor_tensor(dst[:, d:4, s:T], src[:, d:4, s:T], src[:, d:4, 0:T - s], ALU.add)
                        done(dve.tensor_copy(dst[:, d:4, 0:s], src[:, d:4, 0:s]))
                        win = dst[:, d, :]
                        done(dve.tensor_tensor(cat[:, d, 0:16], win[:, 0:16], C("count", 16 * d, 16), ALU.mult))
                        done(dve.tensor_copy(cat[:, d, 16:T], win[:, 16:T]))
                        done(dve.scalar_tensor_tensor(cat[:, 4 + d, :], cat[:, d, :], 1.0 / POOL_WINDOWS[d],
                                                      u[:, 0, d, :], ALU.mult, ALU.subtract))
                    tell(dve.memset(small[:, 0, 0:1], 0.0), to_pe)
                    dve.wait_ge(to_dve.sem, to_dve.base + 1)
                    for d in range(4):
                        dve.tensor_scalar(cat[:, d, :], ps[:, 4 + d // 2, d % 2 * T:(d % 2 + 1) * T],
                                          P2("pool_scale")[:, d:d + 1], None, ALU.mult)

                @block.tensor
                def _(pe):
                    pe.wait_ge(to_pe.sem, to_pe.base + 1)
                    for d in range(4):
                        ins = pe.matmul(ps[:, 4 + d // 2, d % 2 * T:(d % 2 + 1) * T], P2("pool_w")[:, d * P:(d + 1) * P],
                                        cat[:, 4 + d, :], start=True, stop=True)
                    tell(ins, to_dve)
            sqf = flat(sq[:, :, :])
            turned = lambda i: sqf[:, i % 4 * BANK:i % 4 * BANK + 3 * P]

            def values(pe, h):
                lo = h % 2 * ATT_DH
                pe.wait_ge(pt_ready.sem, pt_ready.base + h + 1)
                for t in range(TT):
                    for s in range(t + 1):
                        ins = pe.matmul(ps[lo:lo + ATT_DH, h // 2, t * P:(t + 1) * P], v[:, s, h * ATT_DH:(h + 1) * ATT_DH],
                                        turned(h)[:, (t + s) * P:(t + s + 1) * P], start=(s == 0), stop=(s == t))
                tell(ins, pv_done)

            def act_after(act, i):
                if 4 <= i < ATT_H:
                    act.wait_ge(pv_done.sem, pv_done.base + i - 3)
                if i == ATT_H:
                    act.wait_ge(pv_done.sem, pv_done.base + ATT_H)
                    for m in range(4):
                        act.copy(cat[:, 4 + m, :], ps[:, m, 0:T])

            with new_block() as block:
                attention(block, ATT_H, lambda i, t: query_half(i, q, t),
                          lambda i, n: k[i % 2 * ATT_DH:(i % 2 + 1) * ATT_DH, i // 2, 0:n],
                          lambda i: bias[:, i, :], lambda i: None, small, [probs[:, 0, :], probs[:, 1, :]], turned,
                          values, act_after)
            residual_product(4, KD, cat, gate(0, 0))
            pa.close()

        def router(l):
            parts = [0]

            def scratch(n):
                parts[0] += n
                return rtmp[:, :, parts[0] - n:parts[0]]

            glog, elog = logits[:, :, 0:E_G], logits[:, :, E_G:RT]
            gmax, gexp, gsum, gcand, gleast, ghot = (scratch(n) for n in (1, E_G, 1, E_G, 1, E_G))
            esel, emax, cand, least, hot1, hot2, rest, top1, top2, share = (
                scratch(n) for n in (E_PER, 1, E_PER, 1, E_PER, E_PER, E_PER, 1, 1, 1))
            weigh, weigh2 = scratch(E_PER), scratch(E_PER)

            def wide(a, n):
                return a.broadcast_to([P, TT, n])

            with new_block() as block:
                @block.tensor
                def _(pe):
                    for t in range(TT):
                        for k in range(KD):
                            ins = pe.matmul(ps[:, 4, t * RT:(t + 1) * RT], hT[:, k, t * P:(t + 1) * P],
                                            P2(f"router_{l}")[:, k * RT:(k + 1) * RT], start=(k == 0), stop=(k == KD - 1))
                    tell(ins, to_dve)

                @block.scalar
                def _(act):
                    act.wait_ge(to_act.sem, to_act.base + 1)
                    tell(act.activation(gexp, gexp, ACT.Exp), to_dve)
                    act.wait_ge(to_act.sem, to_act.base + 2)
                    tell(act.activation(esel, esel, ACT.Exp), to_dve)

                @block.vector
                def _(dve):
                    done = InOrder(dve, dve_step)

                    def first_maximum(a, most, candidates, smallest, onehot, n):
                        done(dve.tensor_reduce(most, a, AX_X, ALU.max))
                        done(dve.tensor_tensor(candidates, a, wide(most, n), ALU.is_equal))
                        iota = C(f"iota{n}").unsqueeze(1).broadcast_to([P, TT, n])
                        done(dve.scalar_tensor_tensor(candidates, candidates, -64.0, iota, ALU.mult, ALU.add))
                        done(dve.tensor_reduce(smallest, candidates, AX_X, ALU.min))
                        done(dve.tensor_tensor(onehot, candidates, wide(smallest, n), ALU.is_equal))

                    dve.wait_ge(to_dve.sem, to_dve.base + 1)
                    done(dve.tensor_tensor(logits[:, :, :], ps[:, 4, 0:TT * RT].rearrange("p (t n) -> p t n", t=TT),
                                           P2(f"router_b{l}").unsqueeze(1).broadcast_to([P, TT, RT]), ALU.add))
                    done(dve.tensor_reduce(gmax, glog, AX_X, ALU.max))
                    tell(dve.tensor_tensor(gexp, glog, wide(gmax, E_G), ALU.subtract), to_act)
                    dve.wait_ge(to_dve.sem, to_dve.base + 2)
                    done(dve.tensor_reduce(gsum, gexp, AX_X, ALU.add))
                    first_maximum(gexp, gmax, gcand, gleast, ghot, E_G)
                    chosen = combine[:, :, :].rearrange("p t (g e) -> p t g e", g=E_G)
                    done(dve.tensor_tensor(chosen, elog.rearrange("p t (g e) -> p t g e", g=E_G),
                                           ghot.unsqueeze(3).broadcast_to([P, TT, E_G, E_PER]), ALU.mult))
                    done(dve.tensor_reduce(esel, chosen.rearrange("p t g e -> p t e g"), AX_X, ALU.add))
                    done(dve.tensor_reduce(emax, esel, AX_X, ALU.max))
                    tell(dve.tensor_tensor(esel, esel, wide(emax, E_PER), ALU.subtract), to_act)
                    dve.wait_ge(to_dve.sem, to_dve.base + 3)
                    first_maximum(esel, top1, cand, least, hot1, E_PER)
                    done(dve.scalar_tensor_tensor(rest, hot1, -2.0, esel, ALU.mult, ALU.add))
                    first_maximum(rest, top2, cand, least, hot2, E_PER)
                    done(dve.tensor_tensor(share, top1, top2, ALU.add))
                    done(dve.tensor_tensor(share, share, gsum, ALU.mult))
                    done(dve.reciprocal(share, share))
                    done(dve.tensor_tensor(share, share, gmax, ALU.mult))
                    dve.tensor_tensor(weigh, hot1, wide(top1, E_PER), ALU.mult)
                    done(dve.tensor_tensor(weigh2, hot2, wide(top2, E_PER), ALU.mult))
                    done(dve.tensor_tensor(weigh, weigh, weigh2, ALU.add))
                    done(dve.tensor_tensor(weigh, weigh, wide(share, E_PER), ALU.mult))
                    dve.tensor_tensor(chosen, ghot.unsqueeze(3).broadcast_to([P, TT, E_G, E_PER]),
                                      weigh.unsqueeze(2).broadcast_to([P, TT, E_G, E_PER]), ALU.mult)

        hid_free, silu_done, column_ready, even_down, product_step = (
            signal(n) for n in ("hidden_done", "silu_done", "combine_columns_ready", "even_expert_down", "silu_times_up"))

        def experts(l, last):
            assert ring.place % RING == 0
            turns = E_N // 4
            first, used = ring.place, list(ring.used)
            unit0, hid0, silu0 = ring.unit_done.n, hid_free.n, silu_done.n
            col0, even0, prod0 = column_ready.n, even_down.n, product_step.n
            up_slot, down_slot = (0, 1, 3, 4), (2, 2, 5, 5)
            silu_buf = [sq[:, j, :] for j in range(2)]
            hidden = [sq[:, 2 + j, :] for j in range(2)]
            with new_block() as block:
                @block.sync
                def _(sp):
                    with sp.Fori(0, turns - 1 if last else turns) as i:
                        for s in range(RING):
                            sp.wait_ge(ring.unit_done.sem, i * RING + (unit0 + s + 1))
                            ring.load(sp, i * RING + (index2(first) + RING + s), s)

                @block.tensor
                def _(pe):
                    pe.wait_ge(column_ready.sem, col0 + 1)
                    for b in range(4):
                        pe.matmul(ps[:, 4 + b, :], ones, flat(sq[:, 4:6, :]), start=True, stop=True,
                                  skip_group_check=True)
                    with pe.Fori(0, turns) as i:
                        def up(j):
                            pe.wait_ge(hid_free.sem, i * 4 + (hid0 + j + 1))
                            if j == 0:
                                pe.wait_ge(column_ready.sem, i + (col0 + 2))
                            for t in range(TT):
                                pe.matmul(ps[:, 2 + j % 2, t * P:(t + 1) * P],
                                          ccol[:, t, j:j + 1].broadcast_to([P, P]), ident, start=True, stop=True)
                            s = up_slot[j]
                            pe.wait_ge(ring.slot_full[s], i * 16 + 16 * (used[s] + 1))
                            for m in range(2):
                                for k in range(KD):
                                    at = (m * KD + k) * P
                                    ins = pe.matmul(ps[:, j % 2, m * T:(m + 1) * T], ringbuf[:, s, at:at + P],
                                                    hT[:, k, :], start=(k == 0), stop=(k == KD - 1))
                            ins.then_inc(ring.unit_done.sem, 1)

                        def down(j):
                            s = down_slot[j]
                            pe.wait_ge(hid_free.sem, i * 4 + (hid0 + 2 + j + 1))
                            if j % 2 == 0:
                                pe.wait_ge(ring.slot_full[s], i * 16 + 16 * (used[s] + 1))
                            for m in range(KD):
                                at = j % 2 * D + m * P
                                ins = pe.matmul(ps[:, 4 + m // 2, m % 2 * T:(m % 2 + 1) * T], ringbuf[:, s, at:at + P],
                                                hidden[j % 2], start=False, stop=False, skip_group_check=True)
                            ins.then_inc((ring.unit_done if j % 2 else even_down).sem, 1)

                        for j in (0, 2):
                            up(j)
                            up(j + 1)
                            down(j)
                            down(j + 1)

                @block.scalar
                def _(act):
                    with act.Fori(0, turns) as i:
                        for j in range(4):
                            act.wait_ge(ring.unit_done.sem, i * RING + (unit0 + up_slot[j] + 1))
                            act.wait_ge(hid_free.sem, i * 4 + (hid0 + j + 1))
                            act.activation(silu_buf[j % 2], ps[:, j % 2, 0:T], ACT.Silu).then_inc(silu_done.sem, 1)

                @block.vector
                def _(dve):
                    dve.memset(sq[:, 4:6, :], 0.0).then_inc(column_ready.sem, 1)
                    dve.memset(small[:, 0, 0:1], 0.0).then_inc(hid_free.sem, 1)
                    dve.memset(small[:, 0, 1:2], 0.0).then_inc(hid_free.sem, 1)
                    dve.memset(small[:, 0, 2:3], 0.0).then_inc(even_down.sem, 1)
                    with dve.Fori(0, turns) as i:
                        dve.tensor_copy(ccol[:, :, :], combine[:, :, bass.ds(i * 4, 4)]).then_inc(column_ready.sem, 1)
                        for j in range(4):
                            dve.wait_ge(silu_done.sem, i * 4 + (silu0 + j + 1))
                            dve.tensor_tensor(silu_buf[j % 2], silu_buf[j % 2], ps[:, j % 2, T:2 * T], ALU.mult) \
                                .then_inc(product_step.sem, 1)
                            dve.wait_ge(product_step.sem, i * 4 + (prod0 + j + 1))
                            if j % 2 == 0:
                                dve.wait_ge(even_down.sem, i * 2 + (even0 + j // 2 + 1))
                            else:
                                dve.wait_ge(ring.unit_done.sem, i * RING + (unit0 + 3 * (j // 2)))
                            dve.tensor_tensor(hidden[j % 2], silu_buf[j % 2], ps[:, 2 + j % 2, 0:T], ALU.mult) \
                                .then_inc(hid_free.sem, 1)
                    dve.wait_ge(ring.unit_done.sem, unit0 + turns * RING)
                    for m in range(KD):
                        dve.scalar_tensor_tensor(xT[:, m, :], ps[:, 4 + m // 2, m % 2 * T:(m % 2 + 1) * T],
                                                 gate(l, 1)[:, m:m + 1], xT[:, m, :], ALU.mult, ALU.add)
            for count, n in ((ring.unit_done, turns * RING), (hid_free, 2 + E_N), (silu_done, E_N),
                             (column_ready, 1 + turns), (even_down, 1 + E_N // 2), (product_step, E_N)):
                count.n += n
            ring.place += turns * RING
            ring.used = [n + turns for n in used]

        def mamba():
            mb = ExitStack()
            z = sb("z", [P, KS, T], mb)
            xbc = sb("xbc", [P, KX, T], mb)
            xdt = sb("xdt", [P, TT, SSM_IN], mb)
            cv = sb("cv", [P, 2, 2, T], mb)
            dt = sb("dt", [P, TT, SSM_H], mb)
            a = sb("a", [P, TT, SSM_H], mb)
            acs = sb("acs", [P, TT, SSM_H], mb)
            soft = sb("soft", [P, TT * SSM_H], mb)
            cbm = sb("cbm", [P, 2, 3 * P], mb)
            seg = sb("seg", [P, 4, 3 * P], mb)
            yt = sb("yt", [P, 2, T], mb)
            w = ring.claim(24)
            prod = Product(w, 0, KS + KX, KD, banks)
            conv_w = P2("conv_w").rearrange("p (i c) -> p i c", i=SSM_CONV)
            with new_block() as block:
                @block.sync
                def _(sp):
                    w.refill(sp)

                @block.tensor
                def _(pe):
                    for j in range(24):
                        prod.tensor(pe, hT, j)

                @block.vector
                def _(dve):
                    done = InOrder(dve, dve_step)
                    for j in range(KX // 2):
                        acc = prod.wait(dve, 8 + j)
                        buf = cv[:, j % 2, :, :]
                        if j >= 2:
                            dve.wait_ge(to_dve.sem, to_dve.base + j - 1)
                        for m in range(2):
                            ins = dve.tensor_scalar(buf[:, m, :], acc[:, m * T:(m + 1) * T],
                                                    conv_w[:, SSM_CONV - 1, 2 * j + m:2 * j + m + 1], None, ALU.mult)
                        for s in range(1, SSM_CONV):
                            done(ins)
                            for m in range(2):
                                ins = dve.scalar_tensor_tensor(
                                    buf[:, m, s:T], acc[:, m * T:(m + 1) * T - s],
                                    conv_w[:, SSM_CONV - 1 - s, 2 * j + m:2 * j + m + 1], buf[:, m, s:T],
                                    ALU.mult, ALU.add)
                        ins.then_inc(prod.read(8 + j), 1)

                @block.scalar
                def _(act):
                    for j in range(8):
                        acc = prod.wait(act, j)
                        act.activation(flat(z[:, 2 * j:2 * j + 2, :]), acc, ACT.Silu).then_inc(prod.read(j), 1)
                    for j in range(KX // 2):
                        prod.after_read(act, 8 + j)
                        for m in range(2):
                            c = 2 * j + m
                            ins = act.activation(xbc[:, c, :], cv[:, j % 2, m, :], ACT.Silu,
                                                 bias=P2("conv_b")[:, c:c + 1])
                        tell(ins, to_dve)

            with new_block() as block:
                @block.tensor
                def _(pe):
                    for t in range(TT):
                        for k in range(KD):
                            ins = pe.matmul(ps[:, 4, t * SSM_H:(t + 1) * SSM_H], hT[:, k, t * P:(t + 1) * P],
                                            P2("w_dt")[:, k * SSM_H:(k + 1) * SSM_H], start=(k == 0), stop=(k == KD - 1))
                    tell(ins, to_dve)
                    pe.wait_ge(to_pe.sem, to_pe.base + 1)
                    pe.matmul(ps[:, 5, 0:SSM_H], C("upper", 0, P), a[:, 0, :], start=True, stop=True)
                    pe.matmul(ps[:, 5, SSM_H:2 * SSM_H], ones, a[:, 0, :], start=True, stop=False)
                    ins = pe.matmul(ps[:, 5, SSM_H:2 * SSM_H], C("upper", 0, P), a[:, 1, :], start=False, stop=True)
                    tell(ins, to_dve)

                @block.scalar
                def _(act):
                    log_sigmoid_tail(act, soft[:, :], (to_act.sem, to_act.base + 1), to_dve2)
                    tell(act.activation(acs[:, 0, :], P2("a_log"), ACT.Exp), to_dve2)

                @block.vector
                def _(dve):
                    done = InOrder(dve, dve_step)
                    dve.wait_ge(to_dve.sem, to_dve.base + 1)
                    for t in range(TT):
                        ins = dve.tensor_tensor(dt[:, t, :], ps[:, 4, t * SSM_H:(t + 1) * SSM_H], P2("dt_b"), ALU.add)
                    done(ins)
                    tell(dve.tensor_copy(soft[:, :], flat(dt[:, :, :])), to_act)
                    dve.wait_ge(to_dve2.sem, to_dve2.base + 2)
                    done(dve.scalar_tensor_tensor(flat(dt[:, :, :]), flat(dt[:, :, :]), 0.0, soft[:, :], ALU.max, ALU.add))
                    for t in range(TT):
                        ins = dve.scalar_tensor_tensor(a[:, t, :], dt[:, t, :], -1.0, acs[:, 0, :], ALU.mult, ALU.mult)
                    tell(ins, to_pe)
                    dve.wait_ge(to_dve.sem, to_dve.base + 2)
                    dve.tensor_copy(flat(acs[:, :, :]), ps[:, 5, 0:2 * SSM_H])

            rounds = [(c4, t) for c4 in range(KS // 4) for t in range(TT)]
            with new_block() as block:
                @block.tensor
                def _(pe):
                    for n, (c4, t) in enumerate(rounds):
                        if n >= 4:
                            pe.wait_ge(to_pe.sem, to_pe.base + n - 3)
                        for m in range(4):
                            ins = pe.transpose(ps[:, 4 + n % 4, m * P:(m + 1) * P],
                                               xbc[:, 4 * c4 + m, t * P:(t + 1) * P], ident)
                        tell(ins, to_dve)

                @block.vector
                def _(dve):
                    for n, (c4, t) in enumerate(rounds):
                        dve.wait_ge(to_dve.sem, to_dve.base + n + 1)
                        heads = BANK // SSM_P
                        tell(dve.tensor_tensor(
                            xdt[:, t, c4 * BANK:(c4 + 1) * BANK].rearrange("p (h n) -> p h n", n=SSM_P),
                            ps[:, 4 + n % 4, :].rearrange("p (h n) -> p h n", n=SSM_P),
                            dt[:, t, c4 * heads:(c4 + 1) * heads].unsqueeze(2).broadcast_to([P, heads, SSM_P]),
                            ALU.mult), to_pe)

            per = SSM_H // SSM_G
            cb_done, cb_read, bc_done, seg_ready, exp_done, m_ready, y_done, y_read = (
                pt_done, pt_ready, score_done, to_act, to_dve, prob_ready, pv_done, to_pe2)
            with new_block() as block:
                @block.tensor
                def _(pe):
                    def group(g):
                        if g >= 2:
                            pe.wait_ge(cb_read.sem, cb_read.base + g - 1)
                        B, Cm = xbc[:, KS + g, :], xbc[:, KS + SSM_G + g, :]
                        pe.matmul(ps[:, 4 + g % 2, 0:T], B[:, 0:P], Cm, start=True, stop=True)
                        tell(pe.matmul(ps[:, 4 + g % 2, T:T + P], B[:, P:T], Cm[:, P:T], start=True, stop=True), cb_done)

                    def running_sum(h):
                        if h >= 2:
                            pe.wait_ge(seg_ready.sem, seg_ready.base + h - 1)
                        o = ps[:, 6 + h % 2, :]
                        pe.matmul(o[:, 0:T], a[:, 0, h:h + 1].broadcast_to([P, P]), C("upper"), start=True, stop=False)
                        tell(pe.matmul(o[:, P:T], a[:, 1, h:h + 1].broadcast_to([P, P]), C("upper", 0, P), start=False,
                                       stop=True), bc_done)

                    def outputs(h):
                        ct, lo = h // 2, h % 2 * SSM_P
                        if ct >= 4 and h % 2 == 0:
                            pe.wait_ge(y_read.sem, y_read.base + ct - 3)
                        pe.wait_ge(m_ready.sem, m_ready.base + h + 1)
                        o = ps[lo:lo + SSM_P, ct % 4, 0:T]
                        cols = slice(h * SSM_P, (h + 1) * SSM_P)
                        pe.matmul(o, xdt[:, 0, cols], seg[:, h % 4, 0:T], start=True, stop=False)
                        tell(pe.matmul(o[:, P:T], xdt[:, 1, cols], seg[:, h % 4, T:T + P], start=False, stop=True), y_done)

                    group(0)
                    running_sum(0)
                    running_sum(1)
                    for h in range(SSM_H):
                        if h + 2 < SSM_H:
                            if (h + 2) % per == 0:
                                group((h + 2) // per)
                            running_sum(h + 2)
                        outputs(h)

                @block.vector
                def _(dve):
                    done = InOrder(dve, dve_step)

                    def exponents(h):
                        g = h // per
                        if h % per == 0:
                            dve.wait_ge(cb_done.sem, cb_done.base + g + 1)
                            if g >= 2:
                                dve.wait_ge(m_ready.sem, m_ready.base + per * (g - 1))
                            tell(dve.tensor_tensor(cbm[:, g % 2, :], ps[:, 4 + g % 2, 0:3 * P], C("ssd"), ALU.mult),
                                 cb_read)
                        dve.wait_ge(bc_done.sem, bc_done.base + h + 1)
                        if h >= 4:
                            dve.wait_ge(y_done.sem, y_done.base + h - 3)
                        o = ps[:, 6 + h % 2, :]
                        dve.tensor_scalar(seg[:, h % 4, 0:T], o[:, 0:T], acs[:, 0, h:h + 1], 0.0, ALU.subtract, ALU.min)
                        tell(dve.tensor_scalar(seg[:, h % 4, T:T + P], o[:, P:T], acs[:, 1, h:h + 1], 0.0, ALU.subtract,
                                               ALU.min), seg_ready)

                    def gated(ct):
                        dve.wait_ge(y_done.sem, y_done.base + 2 * ct + 2)
                        tell(dve.scalar_tensor_tensor(yt[:, ct % 2, :], xbc[:, ct, :], P2("d_skip")[:, ct:ct + 1],
                                                      ps[:, ct % 4, 0:T], ALU.mult, ALU.add), y_read)
                        dve.wait_ge(y_read.sem, y_read.base + ct + 1)
                        done(dve.tensor_tensor(z[:, ct, :], z[:, ct, :], yt[:, ct % 2, :], ALU.mult))

                    exponents(0)
                    for h in range(SSM_H):
                        if h + 1 < SSM_H:
                            exponents(h + 1)
                        dve.wait_ge(exp_done.sem, exp_done.base + h + 1)
                        if h % per == 0:
                            dve.wait_ge(cb_read.sem, cb_read.base + h // per + 1)
                        tell(dve.tensor_tensor(seg[:, h % 4, :], seg[:, h % 4, :], cbm[:, h // per % 2, :], ALU.mult), m_ready)
                        if h % 2 and h >= 3:
                            gated(h // 2 - 1)
                    gated(KS - 1)

                @block.scalar
                def _(act):
                    for h in range(SSM_H):
                        act.wait_ge(seg_ready.sem, seg_ready.base + h + 1)
                        tell(act.activation(seg[:, h % 4, :], seg[:, h % 4, :], ACT.Exp), exp_done)

            sqz = xdt[:, :, :].rearrange("p a b -> p (a b)")
            var = flat(xbc[:, 0:SSM_G, :])
            with new_block() as block:
                @block.scalar
                def _(act):
                    for c in range(4):
                        tell(act.activation(sqz[:, c * 4 * T:(c + 1) * 4 * T], flat(z[:, 4 * c:4 * c + 4, :]), ACT.Square),
                             squares)
                    act.wait_ge(variance.sem, variance.base + 1)
                    tell(act.activation(var, var, ACT.Sqrt), deviation)

                @block.tensor
                def _(pe):
                    for g in range(SSM_G):
                        if g % 2 == 0:
                            pe.wait_ge(squares.sem, squares.base + g // 2 + 1)
                        for m in range(2):
                            ins = pe.matmul(ps[:, 4 + g // 2, g % 2 * T:(g % 2 + 1) * T], ones,
                                            sqz[:, (2 * g + m) * T:(2 * g + m + 1) * T], start=(m == 0), stop=(m == 1))
                    tell(ins, summed)

                @block.vector
                def _(dve):
                    done = InOrder(dve, dve_step)
                    dve.wait_ge(summed.sem, summed.base + 1)
                    for b in range(4):
                        ins = dve.tensor_scalar(var[:, b * BANK:(b + 1) * BANK], ps[:, 4 + b, :], 1.0 / (2 * P), EPS,
                                                ALU.mult, ALU.add)
                    tell(ins, variance)
                    dve.wait_ge(deviation.sem, deviation.base + 1)
                    done(dve.reciprocal(var, var))
                    for c in range(KS):
                        dve.scalar_tensor_tensor(z[:, c, :], z[:, c, :], P2("ssm_norm")[:, c:c + 1],
                                                 var[:, c // 2 * T:(c // 2 + 1) * T], ALU.mult, ALU.mult)
            residual_product(8, KS, z, gate(1, 0))
            mb.close()

        modulation()
        rms_norm(mgain[:, 0, :], shift(0, 0))
        pool_and_chunk_attention()
        rms_norm(mgain[:, 1, :], shift(0, 1))
        router(0)
        experts(0, False)
        rms_norm(mgain[:, 2, :], shift(1, 0))
        mamba()
        rms_norm(mgain[:, 3, :], shift(1, 1))
        router(1)
        assert ring.place == 140
        ring.place += 4
        experts(1, True)
        rms_norm(P2("final"), out=xT)
        with new_block() as block:
            @block.sync
            def _(sp):
                sp.dma_start(out, xT[:, :, :]).then_inc(stored, 16)
                sp.wait_ge(stored, 16)




def kernel(x, norm1_g, w_in, hg_lb, hg_norm_g, gla_w2, gla_b, gla_norm_g, cmp_pos_k, cmp_pos_v,
           cmp_w1_k, cmp_w2_k, cmp_w1_v, cmp_w2_v, w_br_hg, w_br_gla, w_br_nsa, w_out, norm2_g,
           w_ffn_gate, w_ffn_up, w_ffn_down, final_norm_g, c_2, ada_w_2, ada_b_2, norm1_w_2, norm2_w_2,
           mix_w_in_2, pool_w_2, pool_scale_2, rel_bias_2, mix_w_out_2, ssm_w_in_2, ssm_conv_w_2,
           ssm_conv_b_2, ssm_dt_bias_2, ssm_A_log_2, ssm_D_2, ssm_norm_w_2, ssm_w_out_2, moe_w_group_2,
           moe_b_group_2, moe_w_expert_2, moe_b_expert_2, moe_w1_2, moe_w3_2, moe_w2_2, final_norm_w_2):
    import concourse.bacc as bacc
    from concourse.bass_utils import run_bass_kernel_spmd

    A = np.asarray
    fc = lambda v: feature_columns(A(v))
    units = []
    for l in range(DEPTH):
        units += stream_hybrid(*(A(w[l]) for w in (w_in, cmp_w1_k, cmp_w1_v, w_br_hg, w_br_gla, w_br_nsa, w_out,
                                                   w_ffn_gate, w_ffn_up, w_ffn_down)))
    feature = lambda w: units_of(weight_blocks(A(w)))
    mix = A(mix_w_in_2[0])
    ssm = A(ssm_w_in_2[0])
    units += [feature(ada_w_2[0]), feature(ada_w_2[1]), feature(mix[:, :1536]), token_major_units(mix[:, 1536:]),
              feature(mix_w_out_2[0]), moe_units(A(moe_w1_2[0]), A(moe_w3_2[0]), A(moe_w2_2[0])),
              feature(ssm[:, :SSM_IN + KX * P]), feature(ssm_w_out_2[0]),
              moe_units(A(moe_w1_2[1]), A(moe_w3_2[1]), A(moe_w2_2[1]))]
    stream = np.concatenate(units)

    def pos(v):
        return A(v).reshape(BLOCKS, 2, NSA_DH).transpose(1, 2, 0).reshape(P, BLOCKS)

    par1 = np.stack([pack(PAR1, N_PAR1, {
        "norm1": fc(norm1_g[l]), "norm2": fc(norm2_g[l]), "hg_norm": fc(hg_norm_g[l]), "gla_norm": fc(gla_norm_g[l]),
        "gla_b": fc(gla_b[l]), "gla_w2": A(gla_w2[l]), "pos_k": pos(cmp_pos_k[l]), "pos_v": pos(cmp_pos_v[l]),
        "w2_k": np.concatenate([A(cmp_w2_k[l])] * 2, 1), "w2_v": A(cmp_w2_v[l])}) for l in range(DEPTH)])

    def k_major(w):
        return w.reshape(KD, P, -1).transpose(1, 0, 2)

    def router(l):
        return k_major(np.concatenate([A(moe_w_group_2[l]), A(moe_w_expert_2[l]).reshape(D, E_N)], 1))

    def router_bias(l):
        return rows(np.concatenate([A(moe_b_group_2[l]), A(moe_b_expert_2[l]).reshape(-1)]))

    par2 = pack(PAR2, N_PAR2, {
        "norm1_0": fc(norm1_w_2[0]), "norm1_1": fc(norm1_w_2[1]), "norm2_0": fc(norm2_w_2[0]),
        "norm2_1": fc(norm2_w_2[1]), "final": fc(final_norm_w_2), "final_1": fc(final_norm_g), "c": fc(c_2),
        "ada_b0": fc(ada_b_2[0]), "ada_b1": fc(ada_b_2[1]), "pool_w": A(pool_w_2[0]).transpose(1, 0, 2),
        "pool_scale": fc(pool_scale_2[0]), "conv_w": np.stack([fc(ssm_conv_w_2[0][i]) for i in range(SSM_CONV)], 1),
        "conv_b": fc(ssm_conv_b_2[0]), "dt_b": rows(A(ssm_dt_bias_2[0])), "a_log": rows(A(ssm_A_log_2[0])),
        "d_skip": fc(np.repeat(A(ssm_D_2[0]), SSM_P)), "ssm_norm": fc(ssm_norm_w_2[0]),
        "w_dt": k_major(ssm[:, SSM_IN + KX * P:]), "router_0": router(0), "router_1": router(1),
        "router_b0": router_bias(0), "router_b1": router_bias(1)})
    arrays = {"stream": stream, "const": constants(), "par1": par1, "par2": par2,
              "lb": np.concatenate([fc(hg_lb[l]) for l in range(DEPTH)], 1), "bias": A(rel_bias_2[0]),
              "xT": A(x)[0].T.reshape(KD, P, T).transpose(1, 0, 2)}
    nc = bacc.Bacc("TRN2", target_bir_lowering=False, num_devices=1)
    arrays = {f"in_{n}": np.ascontiguousarray(a) for n, a in arrays.items()}
    aps = {n: nc.dram_tensor(n, a.shape, mybir.dt.from_np(a.dtype), kind="ExternalInput").ap()
           for n, a in arrays.items()}
    out = nc.dram_tensor("out", (P, KD, T), F32, kind="ExternalOutput").ap()
    hybrid_and_moe(nc, aps["in_stream"], aps["in_const"], aps["in_par1"], aps["in_lb"], aps["in_par2"], aps["in_bias"],
                   aps["in_xT"], out)
    r = run_bass_kernel_spmd(nc, [arrays], core_ids=[0])
    return np.ascontiguousarray(r.results[0]["out"].transpose(2, 1, 0).reshape(1, T, D))
```

```python
from contextlib import ExitStack

import numpy as np

import concourse.bass as bass
from concourse import mybir

ALU = mybir.AluOpType
ACT = mybir.ActivationFunctionType
F32 = mybir.dt.float32
U32 = mybir.dt.uint32
AX_X = mybir.AxisListType.X

P = 128
T = 256
TT = T // P
D = 1024
KD = D // P
DEPTH = 2
EPS = 1e-6
NEG = -1e30
F32R = mybir.dt.float32r
BLOCKS = 8
UNIT = BLOCKS * P
RING = 4
BANK = 512

HG_H, HG_D = 4, 128
GLA_H, GLA_DK, GLA_DV, GLA_RANK = 4, 64, 128, 16
GLA_TAU = 16.0
NSA_H, NSA_G, NSA_DH = 8, 2, 64
CMP_STRIDE, CMP_BLK, CMP_HID = 16, 32, 128
NCMP = T // CMP_STRIDE - 1
ROT = NSA_DH // 4
THETA = 500000.0
N_BR = 3
FF = 2816
KF = FF // P
LEVELS = 7

CHUNK = 64
POOL_WINDOWS = (2, 4, 8, 16)
ATT_H, ATT_DH = 8, 64
REL = 256
SSM_IN = 2048
KS = SSM_IN // P
SSM_H, SSM_P, SSM_G, SSM_N, SSM_CONV = 32, 64, 8, 128, 4
KX = (SSM_IN + 2 * SSM_G * SSM_N) // P
E_G, E_PER = 4, 8
E_N = E_G * E_PER
RT = E_G + E_N



def columns(spec):
    at, out = 0, {}
    for name, n in spec:
        out[name] = (at, n)
        at += n
    return out, at


CONST, N_CONST = columns([
    ("ident", P), ("ones", P), ("upper", P + P), ("rot", P), ("cos", T), ("sin", T),
    ("causal_neg", 3 * P), ("chunk_neg", P), ("cmp_neg", TT * 32), ("cmp_keep", TT * 32), ("ssd", 3 * P),
    ("count", 4 * 16), ("iota4", 4), ("iota8", 8), ("level", LEVELS * P),
])
PAR1, N_PAR1 = columns([
    ("norm1", KD), ("norm2", KD), ("hg_norm", HG_H), ("gla_norm", GLA_H), ("gla_b", 2), ("gla_w2", 2 * P),
    ("pos_k", 16), ("pos_v", 16), ("w2_k", P), ("w2_v", NSA_DH),
])
PAR2, N_PAR2 = columns([
    ("norm1_0", KD), ("norm1_1", KD), ("norm2_0", KD), ("norm2_1", KD), ("final", KD), ("final_1", KD),
    ("ada_b0", 48), ("ada_b1", 48), ("pool_w", 4 * P), ("pool_scale", 4), ("conv_w", SSM_CONV * KX),
    ("conv_b", KX), ("dt_b", SSM_H), ("a_log", SSM_H), ("d_skip", KS), ("ssm_norm", KS), ("w_dt", KD * SSM_H),
    ("router_0", KD * RT), ("router_1", KD * RT), ("router_b0", RT), ("router_b1", RT),
])

IN_AT = {}
_at = 0
for _n, _w in (("hq", 512), ("hf", 512), ("hi", 512), ("hog", 512), ("gq", 256), ("gk", 256), ("gv", 512),
               ("glr", 16), ("gog", 512), ("nq", 512), ("nkc", 128), ("nvc", 128), ("nks", 128), ("nvs", 128),
               ("nkw", 128), ("nvw", 128), ("ngate", 24), ("mgate", 3072)):
    IN_AT[_n] = (_at, _w)
    _at += _w
IN_COLS = _at

UNITS1 = [("hf", 4), ("hq", 4), ("hi", 4), ("hog", 4), ("gq", 2), ("gk", 2), ("gv", 4), ("misc", 1), ("gog", 4),
          ("nkc", 2), ("nvc", 2), ("nks", 2), ("nkw", 2), ("nq", 4), ("nvsw", 2), ("w1k", 2), ("w1v", 2),
          ("mix", 36), ("w_out", 8), ("ffn_gu", 44), ("ffn_d", 22), ("filler", 3)]
N_U1 = sum(n for _, n in UNITS1)
assert N_U1 % RING == 0
UNITS2 = [("mix_in", 16), ("mix_out", 8), ("moe0", 96), ("ssm_in", 48), ("ssm_out", 16), ("moe1", 96)]
N_U2 = sum(n for _, n in UNITS2)
N_UNITS = DEPTH * N_U1 + N_U2


def weight_blocks(w):
    k, n = w.shape
    return w.reshape(k // P, P, n // P, P).transpose(2, 0, 1, 3).reshape(-1, P, P)


def units_of(blocks):
    n = len(blocks) // BLOCKS
    return blocks.reshape(n, BLOCKS, P, P).transpose(0, 2, 1, 3).reshape(n, P, UNIT)


def feature_columns(v):
    return v.reshape(-1, P).T


def rows(v):
    return np.broadcast_to(v.reshape(1, -1), (P, v.size))


def pack(spec, total, parts, dtype=np.float32):
    out = np.zeros((P, total), dtype)
    for name, a in parts.items():
        at, n = spec[name]
        a = a.reshape(a.shape[0], -1)
        assert a.shape[1] == n, (name, a.shape, n)
        out[:a.shape[0], at:at + n] = a
    return out


def stream_hybrid(w_in, w1k, w1v, br_hg, br_gla, br_nsa, w_out, wg, wu, wd):
    def cols(name):
        at, n = IN_AT[name]
        return w_in[:, at:at + n]

    def twice(name):
        w = cols(name).reshape(D, NSA_G, 1, NSA_DH)
        return np.concatenate([w, w], axis=2).reshape(D, 2 * P)

    feature = lambda w: units_of(weight_blocks(w))
    misc = np.zeros((D, P), w_in.dtype)
    misc[:, 0:GLA_RANK] = cols("glr")
    misc[:, 32:32 + 24] = cols("ngate")
    gu = np.concatenate([wg.reshape(D, -1, 2 * P), wu.reshape(D, -1, 2 * P)], axis=2).reshape(D, 2 * FF)
    mgate, mix = feature(cols("mgate")), []
    for b, w in enumerate((br_hg, br_gla, br_nsa)):
        branch = feature(w)
        for j in range(KD // 2):
            mix += [mgate[8 * b + 2 * j:8 * b + 2 * j + 2], branch[j:j + 1]]
    parts = {n: feature(cols(n)) for n in ("hf", "hq", "hi", "gq", "gk", "gv", "nq", "hog", "gog")}
    parts.update({n: feature(twice(n)) for n in ("nkc", "nvc", "nks", "nkw")})
    parts.update({
        "misc": feature(misc), "nvsw": feature(np.concatenate([cols("nvs"), cols("nvw")], axis=1)),
        "w1k": units_of(w1k.reshape(-1, P, CMP_HID)), "w1v": units_of(w1v.reshape(-1, P, CMP_HID)),
        "mix": np.concatenate(mix), "w_out": feature(w_out), "ffn_gu": feature(gu), "ffn_d": feature(wd),
        "filler": np.zeros((3, P, UNIT), w_in.dtype)})
    for name, n in UNITS1:
        assert len(parts[name]) == n, (name, len(parts[name]))
    return [parts[name] for name, n in UNITS1]


def moe_units(w1, w3, w2):
    out = []
    for e in range(0, E_N, 2):
        for i in (e, e + 1):
            out += [units_of(weight_blocks(w1[i])), units_of(weight_blocks(w3[i]))]
        out += [w2[e:e + 2]]
    return np.concatenate(out)


def constants():
    i = np.arange(P)
    t = np.arange(T)
    s_, t_ = i[:, None], i[None, :]
    upper = (s_ <= t_).astype(np.float32)
    ones = np.ones((P, P), np.float32)
    zeros = np.zeros((P, P), np.float32)
    rot = np.zeros((P, P), np.float32)
    half = ROT // 2
    for base in (0, NSA_DH):
        for j in range(half):
            rot[base + half + j, base + j] = 1.0
            rot[base + j, base + half + j] = 1.0
    inv = np.float32(THETA) ** (-np.arange(0, ROT, 2, dtype=np.float32) / np.float32(ROT))
    ang = np.arange(T, dtype=np.float32)[:, None] * inv.astype(np.float32)[None, :]
    cos, sin = np.cos(ang).T, np.sin(ang).T
    c = np.ones((P, T), np.float32)
    s = np.zeros((P, T), np.float32)
    for base in (0, NSA_DH):
        c[base:base + half], c[base + half:base + ROT] = cos, cos
        s[base:base + half], s[base + half:base + ROT] = -sin, sin
    n = np.arange(32)
    tok = i[:, None, None] + P * np.arange(TT)[None, :, None]
    keep = ((n * CMP_STRIDE + CMP_BLK - 1)[None, None, :] <= tok) & (n < NCMP)[None, None, :]
    count = np.stack([w / np.minimum(np.arange(16) + 1, w) for w in POOL_WINDOWS]).astype(np.float32)
    causal = np.where(t_ <= s_, 0.0, NEG).astype(np.float32)
    level = []
    for lv in range(LEVELS):
        m = 1 << lv
        level.append((s_ // (2 * m) == t_ // (2 * m)) & (s_ // m % 2 == 0) & (t_ // m % 2 == 1))
    return pack(CONST, N_CONST, {
        "ident": np.eye(P, dtype=np.float32), "ones": ones, "upper": np.concatenate([upper, ones], 1),
        "rot": rot, "cos": c, "sin": s,
        "causal_neg": np.concatenate([causal, zeros, causal], 1),
        "chunk_neg": np.where(t_ // CHUNK <= s_ // CHUNK, 0.0, NEG).astype(np.float32),
        "cmp_neg": np.where(keep, 0.0, NEG).astype(np.float32), "cmp_keep": keep.astype(np.float32),
        "ssd": np.concatenate([upper, ones, upper], 1), "count": rows(count), "iota4": rows(np.arange(4.0)),
        "iota8": rows(np.arange(8.0)), "level": np.concatenate(level, 1).astype(np.float32),
    })




class Count:

    def __init__(self, sem):
        self.sem, self.n, self.base = sem, 0, 0

    def one(self):
        self.n += 1
        return 1


class InOrder:

    def __init__(self, eng, count):
        self.eng, self.count = eng, count

    def __call__(self, ins):
        ins.then_inc(self.count.sem, self.count.one())
        self.eng.wait_ge(self.count.sem, self.count.n)


class Ring:

    def __init__(self, dram, raw, high, low, raw_full, unit_done, high_done, split):
        self.dram, self.raw, self.high, self.low, self.raw_full = dram, raw, high, low, raw_full
        self.unit_done, self.high_done, self.split = unit_done, high_done, split
        self.place, self.loads, self.base, self.limit = 0, [0] * RING, 0, None

    def load(self, sp, index, slot):
        src = self.dram[index, :, :] if isinstance(index, int) else \
            self.dram[bass.ds(index, 1), :, :].rearrange("o p n -> p (o n)")
        sp.dma_start(self.raw[:, slot, :], src).then_inc(self.raw_full[slot], 16)

    def round_high(self, act, slot):
        return act.copy(self.high[:, slot, :], self.raw[:, slot, :])

    def take_low(self, dve, slot):
        return dve.tensor_tensor(self.low[:, slot, :], self.raw[:, slot, :], self.high[:, slot, :].bitcast(F32),
                                 ALU.subtract)

    def claim(self, n):
        return Units(self, n)


class Units:

    def __init__(self, ring, n):
        self.ring, self.first, self.n = ring, ring.place, n
        self.done0, self.split0, self.high0 = ring.unit_done.n, ring.split.n, ring.high_done.n
        self.turn = []
        for i in range(n):
            s = (self.first + i) % RING
            ring.loads[s] += 1
            self.turn.append(ring.loads[s])
        self.more = [ring.limit is None or self.first + i + RING < ring.limit for i in range(n)]
        self.load_more = [ring.limit is None or self.first + i + 2 * RING < ring.limit for i in range(n)]
        ring.place += n
        ring.unit_done.n += n
        ring.split.n += n
        ring.high_done.n += n

    def done(self, i):
        return self.ring.unit_done.sem, self.done0 + i + 1

    def arrived(self, pe, i):
        s = (self.first + i) % RING
        pe.wait_ge(self.ring.split.sem, self.split0 - RING + i + 1)
        return self.ring.high[:, s, :], self.ring.low[:, s, :]

    def scalar(self, act, i):
        if self.more[i]:
            s = (self.first + i) % RING
            act.wait_ge(*self.done(i))
            act.wait_ge(self.ring.raw_full[s], 16 * self.turn[i])
            self.ring.round_high(act, s).then_inc(self.ring.high_done.sem, 1)

    def vector(self, dve, i):
        if self.more[i]:
            dve.wait_ge(self.ring.high_done.sem, self.high0 + i + 1)
            self.ring.take_low(dve, (self.first + i) % RING).then_inc(self.ring.split.sem, 1)

    def sync(self, sp, which=None):
        for i in range(self.n) if which is None else which:
            if self.load_more[i]:
                sp.wait_ge(self.ring.split.sem, self.split0 + i + 1)
                self.ring.load(sp, self.ring.base + (self.first + i + 2 * RING), (self.first + i) % RING)


def three_products(pe, out, stationary, moving, start, stop, **more):
    (sh, sl), (mh, ml) = stationary, moving
    pe.matmul(out, sh, mh, start=start, stop=False, **more)
    pe.matmul(out, sl, mh, start=False, stop=False, **more)
    return pe.matmul(out, sh, ml, start=False, stop=stop, **more)


class Product:

    def __init__(self, units, block0, tiles, kt, banks, token_major=False):
        self.units, self.block0, self.kt, self.banks, self.token_major = units, block0, kt, banks, token_major
        self.pairs = []
        for j in range((tiles + 1) // 2):
            last = block0 + min(2 * (j + 1), tiles) * kt - 1
            if last % BLOCKS == BLOCKS - 1:
                done = units.done(last // BLOCKS)
            else:
                banks.done.n += 1
                done = (banks.done.sem, banks.done.n)
            b = banks.take()
            self.pairs.append((b, banks.reads[b] - 1, done, min(2, tiles - 2 * j)))

    def units_of(self, j):
        lo = self.block0 + 2 * j * self.kt
        hi = lo + self.pairs[j][3] * self.kt
        return range(lo // BLOCKS, hi // BLOCKS)

    def psum(self, j):
        return self.banks.ps[:, self.pairs[j][0], :]

    def wait(self, eng, j):
        eng.wait_ge(*self.pairs[j][2])
        return self.psum(j)

    def read(self, j):
        return self.banks.read[self.pairs[j][0]]

    def after_read(self, eng, j):
        eng.wait_ge(self.read(j), self.pairs[j][1] + 1)

    def tensor(self, pe, x, j):
        b, before, done, tiles = self.pairs[j]
        if before:
            pe.wait_ge(self.banks.read[b], before)
        blk = self.block0 + 2 * j * self.kt
        xh, xl = x
        for m in range(tiles):
            if self.token_major:
                high, low = self.units.arrived(pe, blk // BLOCKS)
                for t in range(TT):
                    for k in range(self.kt):
                        w = (a[:, k * P:(k + 1) * P] for a in (high, low))
                        ins = three_products(pe, self.banks.ps[:, b, t * T + m * P:t * T + (m + 1) * P],
                                             (xh[:, k, t * P:(t + 1) * P], xl[:, k, t * P:(t + 1) * P]), tuple(w),
                                             k == 0, k == self.kt - 1)
                ins.then_inc(self.units.ring.unit_done.sem, 1)
                blk += self.kt
                continue
            for k in range(self.kt):
                if blk % BLOCKS == 0 or (m == 0 and k == 0):
                    high, low = self.units.arrived(pe, blk // BLOCKS)
                at = blk % BLOCKS * P
                ins = three_products(pe, self.banks.ps[:, b, m * T:(m + 1) * T], (high[:, at:at + P], low[:, at:at + P]),
                                     (xh[:, k, :], xl[:, k, :]), k == 0, k == self.kt - 1)
                if blk % BLOCKS == BLOCKS - 1:
                    ins.then_inc(self.units.ring.unit_done.sem, 1)
                elif m == tiles - 1 and k == self.kt - 1:
                    ins.then_inc(self.banks.done.sem, 1)
                blk += 1


class Banks:

    def __init__(self, ps, read, done, n):
        self.ps, self.read, self.done, self.n = ps, read, done, n
        self.reads, self.turn = [0] * n, 0

    def take(self):
        b = self.turn
        self.turn = (b + 1) % self.n
        self.reads[b] += 1
        return b




def hybrid_and_moe(nc, stream, const_in, par1_in, lb_in, par2_in, ada_in, c_in, bias_in, x_in, out):
    with ExitStack() as everywhere:
        def sem(name):
            return everywhere.enter_context(nc.semaphore(name))

        counts = []

        def signal(name):
            counts.append(Count(sem(name)))
            return counts[-1]

        def sb(name, shape, scope=everywhere, dt=F32):
            return scope.enter_context(nc.sbuf_tensor(name, shape, dt))

        ps = everywhere.enter_context(nc.psum_tensor("ps", [P, 8, BANK], F32))
        raw = sb("raw", [P, RING, UNIT])
        high = sb("high", [P, RING, UNIT], dt=F32R)
        low = sb("low", [P, RING, UNIT], dt=F32R)
        const = sb("const", [P, N_CONST])
        par1 = sb("par1", [P, N_PAR1])
        par2 = sb("par2", [P, N_PAR2])
        xT = sb("xT", [P, KD, T])
        hh = sb("hh", [P, KD, T], dt=F32R)
        hl = sb("hl", [P, KD, T], dt=F32R)
        h = (hh, hl)
        mod = sb("mod", [P, 2, 48])
        sq = sb("sq", [P, KD, T])
        stat = sb("stat", [P, 4, T])
        small = sb("small", [P, 2, 8])

        def C(name, lo=0, n=None):
            at, w = CONST[name]
            return const[:, at + lo:at + lo + (w - lo if n is None else n)]

        def P1(name):
            at, w = PAR1[name]
            return par1[:, at:at + w]

        def P2(name):
            at, w = PAR2[name]
            return par2[:, at:at + w]

        ident, ones = C("ident"), C("ones")

        ring = Ring(stream, raw, high, low, [sem(f"raw_full{i}") for i in range(RING)], signal("unit_done"),
                    signal("high_done"), signal("unit_split"))
        banks = Banks(ps, [sem(f"bank_read{i}") for i in range(4)], signal("bank_done"), 4)
        loaded = sem("inputs_loaded")
        par_loaded = sem("layer_parameters_loaded")
        stored = sem("output_stored")
        dve_step, act_step, pool_step = signal("dve_step"), signal("act_step"), signal("pool_step")
        squares, summed, variance, deviation = (signal(n) for n in ("squares", "summed", "variance", "deviation"))
        to_pe, to_pe2, to_act, to_act2, to_dve, to_dve2, to_pool = (
            signal(n) for n in ("for_tensor", "for_tensor2", "for_scalar", "for_scalar2", "for_vector",
                                "for_vector2", "for_gpsimd"))
        pv_done, pt_ready, pt_done, score_done, prob_ready = (
            signal(n) for n in ("values_weighted", "transposed_ready", "transposed", "scores_done", "probs_ready"))

        def new_block():
            for c in counts:
                c.base = c.n
            return nc.Block()

        def tell(ins, count):
            return ins.then_inc(count.sem, count.one())

        def restart_counts():
            with new_block() as block:
                @block.sync
                def _(sp):
                    for c in counts:
                        sp.sem_clear(c.sem)
                    for b in range(banks.n):
                        sp.sem_clear(banks.read[b])
                    for s in (par_loaded, c_loaded, *ada_full):
                        sp.sem_clear(s)
            for c in counts:
                c.n = c.base = 0
            banks.reads, banks.turn = [0] * banks.n, 0

        def restart_ring():
            with new_block() as block:
                @block.sync
                def _(sp):
                    for s in range(RING):
                        sp.wait_ge(ring.raw_full[s], 16 * (ring.loads[s] + 1))
            with new_block() as block:
                @block.sync
                def _(sp):
                    for s in range(RING):
                        sp.sem_clear(ring.raw_full[s])
            with new_block() as block:
                @block.sync
                def _(sp):
                    for s in range(RING):
                        sp.sem_inc(ring.raw_full[s], 16)
                    sp.sem_inc(ring.high_done.sem, RING)
                    sp.sem_inc(ring.split.sem, RING)
            ring.loads = [0] * RING
            ring.high_done.n = ring.split.n = RING

        with new_block() as block:
            @block.sync
            def _(sp):
                for s in range(RING):
                    ring.load(sp, s, s)
                for s in range(RING):
                    sp.wait_ge(ring.split.sem, s + 1)
                    ring.load(sp, RING + s, s)
                sp.wait_ge(loaded, 16 * 3)

            @block.scalar
            def _(act):
                act.dma_start(xT[:, :, :], x_in).then_inc(loaded, 16)
                act.dma_start(const[:, :], const_in).then_inc(loaded, 16)
                act.dma_start(par2[:, :], par2_in).then_inc(loaded, 16)
                for s in range(RING):
                    act.wait_ge(ring.raw_full[s], 16)
                    ring.round_high(act, s).then_inc(ring.high_done.sem, 1)

            @block.vector
            def _(dve):
                for s in range(RING):
                    dve.wait_ge(ring.high_done.sem, s + 1)
                    ring.take_low(dve, s).then_inc(ring.split.sem, 1)
        ring.loads = [1] * RING
        ring.high_done.n = ring.split.n = RING


        def rms_norm(gain, shift=None, out=None, width=D):
            out, halves = (sq if out is None else out), out is not xT
            with new_block() as block:
                @block.scalar
                def _(act):
                    for c in range(4):
                        tell(act.activation(sq[:, 2 * c:2 * c + 2, :], xT[:, 2 * c:2 * c + 2, :], ACT.Square), squares)
                    act.wait_ge(variance.sem, variance.base + 1)
                    tell(act.activation(stat[:, 1, :], stat[:, 0, :], ACT.Sqrt), deviation)
                    for k in range(0, KD if halves else 0, 2):
                        act.wait_ge(to_act.sem, to_act.base + k // 2 + 1)
                        tell(act.copy(hh[:, k:k + 2, :], out[:, k:k + 2, :]), to_dve)

                @block.tensor
                def _(pe):
                    for k in range(KD):
                        if k % 2 == 0:
                            pe.wait_ge(squares.sem, squares.base + k // 2 + 1)
                        ins = pe.matmul(ps[:, 4, 0:T], ones, sq[:, k, :], start=(k == 0), stop=(k == KD - 1))
                    tell(ins, summed)

                @block.vector
                def _(dve):
                    done = InOrder(dve, dve_step)
                    dve.wait_ge(summed.sem, summed.base + 1)
                    tell(dve.tensor_scalar(stat[:, 0, :], ps[:, 4, 0:T], 1.0 / width, EPS, ALU.mult, ALU.add), variance)
                    dve.wait_ge(deviation.sem, deviation.base + 1)
                    done(dve.reciprocal(stat[:, 2, :], stat[:, 1, :]))
                    for k in range(KD):
                        ins = dve.scalar_tensor_tensor(out[:, k, :], xT[:, k, :], gain[:, k:k + 1], stat[:, 2, :],
                                                       ALU.mult, ALU.mult)
                        if shift is not None:
                            done(ins)
                            ins = dve.tensor_scalar(out[:, k, :], out[:, k, :], shift[:, k:k + 1], None, ALU.add)
                        if halves and k % 2:
                            tell(ins, to_act)
                        if halves and k % 2 and k > 1:
                            low_half(dve, k // 2 - 1, out)
                    if halves:
                        low_half(dve, KD // 2 - 1, out)

        def low_half(dve, c, x):
            dve.wait_ge(to_dve.sem, to_dve.base + c + 1)
            dve.tensor_tensor(hl[:, 2 * c:2 * c + 2, :], x[:, 2 * c:2 * c + 2, :], hh[:, 2 * c:2 * c + 2, :].bitcast(F32),
                              ALU.subtract)

        def residual_product(n_units, kt, x, gate=None, mods=None):
            w = ring.claim(n_units)
            prod = Product(w, 0, KD, kt, banks)

            def modulate(dve, i):
                if mods is not None:
                    mods.vector(dve, IN_SWIGLU + i + 1)

            with new_block() as block:
                @block.sync
                def _(sp):
                    for i in range(n_units):
                        if mods is not None:
                            mods.sync(sp, IN_SWIGLU + i)
                        w.sync(sp, [i])

                @block.tensor
                def _(pe):
                    for j in range(KD // 2):
                        prod.tensor(pe, x, j)

                @block.scalar
                def _(act):
                    for i in range(n_units):
                        w.scalar(act, i)

                @block.vector
                def _(dve):
                    for j in range(KD // 2):
                        for i in list(prod.units_of(j))[:-1]:
                            w.vector(dve, i)
                            modulate(dve, i)
                        acc = prod.wait(dve, j)
                        for m in range(2):
                            k = 2 * j + m
                            if gate is None:
                                ins = dve.tensor_tensor(xT[:, k, :], xT[:, k, :], acc[:, m * T:(m + 1) * T], ALU.add)
                            else:
                                ins = dve.scalar_tensor_tensor(xT[:, k, :], acc[:, m * T:(m + 1) * T],
                                                               gate[:, k:k + 1], xT[:, k, :], ALU.mult, ALU.add)
                        ins.then_inc(prod.read(j), 1)
                        for i in list(prod.units_of(j))[-1:]:
                            w.vector(dve, i)
                            modulate(dve, i)
                    if mods is not None:
                        mods.finish(dve)

        hybrid = ExitStack()
        lb = sb("lb", [P, DEPTH * HG_H], hybrid)
        lbw = sb("lbw", [P, 6, HG_H], hybrid)
        ln_lb = sb("ln_lb", [P, DEPTH, HG_H], hybrid)
        ln_1m = sb("ln_1m", [P, DEPTH, HG_H], hybrid)
        lb_now = sb("lb_now", [P, 2, HG_H], hybrid)
        branches = ExitStack()
        hf = sb("hf", [P, HG_H, T], branches)
        hq = sb("hq", [P, HG_H, T], branches)
        hk = sb("hk", [P, HG_H, T], branches)
        hv = sb("hv", [P, TT, 512], branches)
        hog = sb("hog", [P, 4, T], branches)
        gq = sb("gq", [P, 2, T], branches)
        gk = sb("gk", [P, 2, T], branches)
        gg = sb("gg", [P, 2, T], branches)
        gv = sb("gv", [P, TT, 512], branches)
        glr = sb("glr", [P, T], branches)
        gl_tok = sb("gl_tok", [P, TT, GLA_RANK], branches)
        gates = sb("gates", [P, TT, 24], branches)
        gog = sb("gog", [P, 4, T], branches)
        qk = sb("qk", [P, 10, T], branches)
        vc = sb("vc", [P, 2, T], branches)
        vsw = sb("vsw", [P, TT, 2 * P], branches)
        yh = sb("yh", [P, 3, 4, T], branches, F32R)
        yl = sb("yl", [P, 3, 4, T], branches, F32R)
        W = sb("W", [P, 3, 4 * T], branches)
        scores = sb("scores", [P, 8, P], branches)
        cross = sb("cross", [P, 4, P], branches)

        with new_block() as block:
            @block.sync
            def _(sp):
                sp.dma_start(lb[:, :], lb_in).then_inc(loaded, 16)
                sp.wait_ge(loaded, 16 * 4)

            @block.vector
            def _(dve):
                done = InOrder(dve, dve_step)
                dve.wait_ge(loaded, 16 * 4)
                a0, a1 = lb[:, 0:HG_H], lb[:, HG_H:2 * HG_H]
                done(dve.tensor_tensor(lbw[:, 0, :], a0, a1, ALU.max))
                dve.tensor_tensor(lbw[:, 1, :], a0, lbw[:, 0, :], ALU.subtract)
                tell(dve.tensor_tensor(lbw[:, 2, :], a1, lbw[:, 0, :], ALU.subtract), to_act)
                dve.wait_ge(to_dve.sem, to_dve.base + 1)
                done(dve.tensor_tensor(lbw[:, 5, :], lbw[:, 3, :], lbw[:, 4, :], ALU.add))
                dve.memset(ln_lb[:, 0, :], NEG)
                tell(dve.memset(ln_1m[:, 0, :], 0.0), to_act)
                dve.wait_ge(to_dve.sem, to_dve.base + 2)
                dve.tensor_tensor(ln_lb[:, 1, :], lbw[:, 2, :], lbw[:, 0, :], ALU.subtract)
                dve.tensor_tensor(ln_1m[:, 1, :], lbw[:, 1, :], lbw[:, 0, :], ALU.subtract)

            @block.scalar
            def _(act):
                act.wait_ge(to_act.sem, to_act.base + 1)
                act.activation(lbw[:, 3, :], lbw[:, 1, :], ACT.Exp)
                tell(act.activation(lbw[:, 4, :], lbw[:, 2, :], ACT.Exp), to_dve)
                act.wait_ge(to_act.sem, to_act.base + 2)
                tell(act.activation(lbw[:, 0, :], lbw[:, 5, :], ACT.Ln), to_dve)

        class Projections:

            def __init__(self):
                self.w = ring.claim(sum(n for _, n in UNITS1[:15]))
                self.pairs, at = [], 0
                for name, n in UNITS1[:15]:
                    prod = Product(self.w, at * BLOCKS, n, KD, banks, name in ("hi", "misc", "gv", "nvsw"))
                    self.pairs += [(name, prod, j) for j in range((n + 1) // 2)]
                    at += n
                self.mine = range(0)

            def take(self, n):
                self.mine = range(self.mine.stop, self.mine.stop + n)
                return self.mine

            def units(self, p):
                return list(self.pairs[p][1].units_of(self.pairs[p][2]))

            def sync(self, sp):
                for p in self.mine:
                    self.w.sync(sp, self.units(p))

            def tensor(self, pe, p):
                _, prod, j = self.pairs[p]
                prod.tensor(pe, h, j)

            def scalar(self, act, p):
                name, prod, j = self.pairs[p]
                units = self.units(p)
                for i in units[:-1]:
                    self.w.scalar(act, i)
                if name in ("hq", "hog", "gog"):
                    dst = {"hq": hq, "hog": hog, "gog": gog}[name]
                    acc = prod.wait(act, j)
                    act.activation(dst[:, 2 * j:2 * j + 2, :], acc.rearrange("p (m t) -> p m t", m=2), ACT.Silu) \
                        .then_inc(prod.read(j), 1)
                self.w.scalar(act, units[-1])

            def vector(self, dve, p):
                name, prod, j = self.pairs[p]
                units = self.units(p)
                for i in units[:-1]:
                    self.w.vector(dve, i)
                if name not in ("hq", "hog", "gog"):
                    acc = prod.wait(dve, j)
                    acc3 = acc.rearrange("p (m t) -> p m t", m=2)
                    if name == "misc":
                        dve.tensor_copy(gl_tok[:, :, :], acc3[:, :, 0:GLA_RANK])
                        ins = dve.tensor_copy(gates[:, :, :], acc3[:, :, 32:32 + 24])
                    elif name == "gq":
                        ins = dve.tensor_scalar(gq[:, :, :], acc3, GLA_DK ** -0.5, None, ALU.mult)
                    elif name in ("hi", "gv", "nvsw"):
                        dst = {"hi": hv, "gv": gv, "nvsw": vsw}[name]
                        ins = dve.tensor_copy(dst[:, :, j * 2 * P:(j + 1) * 2 * P], acc3)
                    else:
                        dst = {"hf": hf, "gk": gk, "nkc": qk[:, 4:6, :], "nks": qk[:, 6:8, :], "nkw": qk[:, 8:10, :],
                               "nq": qk[:, 0:4, :], "nvc": vc}[name]
                        ins = dve.tensor_copy(dst[:, 2 * j:2 * j + 2, :], acc3)
                    ins.then_inc(prod.read(j), 1)
                self.w.vector(dve, units[-1])

        def project(proj, n):
            mine = proj.take(n)
            with new_block() as block:
                @block.sync
                def _(sp):
                    proj.sync(sp)

                @block.tensor
                def _(pe):
                    for p in mine:
                        proj.tensor(pe, p)

                @block.scalar
                def _(act):
                    for p in mine:
                        proj.scalar(act, p)

                @block.vector
                def _(dve):
                    for p in mine:
                        proj.vector(dve, p)


        def log_sigmoid_tail(act, buf, wait_for, tell_to):
            done = InOrder(act, act_step)
            if wait_for is not None:
                act.wait_ge(*wait_for)
            done(act.activation(buf, buf, ACT.Abs))
            done(act.activation(buf, buf, ACT.Exp, scale=-1.0))
            tell(act.activation(buf, buf, ACT.Ln, bias=1.0), tell_to)

        def flat(a):
            return a.rearrange("p a b -> p (a b)")

        def prepare_hgrn(layer, proj, n):
            c, dist = W[:, 1, :], W[:, 2, :]
            c3, dist3 = (a.rearrange("p (h t) -> p h t", h=HG_H) for a in (c, dist))
            mine = proj.take(n)
            with new_block() as block:
                @block.sync
                def _(sp):
                    proj.sync(sp)

                @block.tensor
                def _(pe):
                    for p in mine:
                        proj.tensor(pe, p)

                @block.vector
                def _(dve):
                    done = InOrder(dve, dve_step)
                    dve.tensor_copy(lb_now[:, 0:1, :], ln_lb[:, bass.ds(layer, 1), :])
                    dve.tensor_copy(lb_now[:, 1:2, :], ln_1m[:, bass.ds(layer, 1), :])
                    tell(dve.tensor_copy(dist, flat(hf[:, :, :])), to_act)
                    dve.wait_ge(to_dve.sem, to_dve.base + 1)
                    done(dve.scalar_tensor_tensor(c, flat(hf[:, :, :]), 0.0, dist, ALU.min, ALU.subtract))
                    for h in range(HG_H):
                        ins = dve.tensor_scalar(c3[:, h, :], c3[:, h, :], lb_now[:, 1, h:h + 1], None, ALU.add)
                    done(ins)
                    tell(dve.tensor_tensor(flat(hk[:, :, :]), c, flat(hf[:, :, :]), ALU.subtract), to_act)
                    for h in range(HG_H):
                        ins = dve.tensor_scalar(dist3[:, h, :], c3[:, h, :], lb_now[:, 0, h:h + 1], None, ALU.subtract)
                    tell(ins, to_act)
                    proj.vector(dve, mine[0])
                    dve.wait_ge(to_dve.sem, to_dve.base + 2)
                    for h in range(HG_H):
                        dve.scalar_tensor_tensor(hf[:, h, :], c3[:, h, :], lb_now[:, 0, h:h + 1], dist3[:, h, :],
                                                 ALU.max, ALU.add)
                    for p in mine[1:]:
                        proj.vector(dve, p)

                @block.scalar
                def _(act):
                    log_sigmoid_tail(act, dist, (to_act.sem, to_act.base + 1), to_dve)
                    proj.scalar(act, mine[0])
                    act.wait_ge(to_act.sem, to_act.base + 2)
                    act.activation(flat(hk[:, :, :]), flat(hk[:, :, :]), ACT.Exp)
                    log_sigmoid_tail(act, dist, (to_act.sem, to_act.base + 3), to_dve)
                    for p in mine[1:]:
                        proj.scalar(act, p)

        def prepare_gla(proj, n):
            mine = proj.take(n)
            with new_block() as block:
                @block.sync
                def _(sp):
                    proj.sync(sp)

                @block.tensor
                def _(pe):
                    for t in range(TT):
                        ins = pe.transpose(ps[0:GLA_RANK, 4, t * P:(t + 1) * P], gl_tok[:, t, :], ident)
                    tell(ins, to_dve)
                    for p in mine:
                        proj.tensor(pe, p)
                    pe.wait_ge(to_pe.sem, to_pe.base + 1)
                    for m in range(2):
                        ins = pe.matmul(ps[:, 5, m * T:(m + 1) * T], P1("gla_w2")[0:GLA_RANK, m * P:(m + 1) * P],
                                        glr[0:GLA_RANK, :], start=True, stop=True)
                    tell(ins, to_dve)

                @block.vector
                def _(dve):
                    done = InOrder(dve, dve_step)
                    dve.wait_ge(to_dve.sem, to_dve.base + 1)
                    tell(dve.tensor_copy(glr[0:GLA_RANK, :], ps[0:GLA_RANK, 4, 0:T]), to_pe)
                    for p in mine:
                        proj.vector(dve, p)
                    dve.wait_ge(to_dve.sem, to_dve.base + 2)
                    for m in range(2):
                        ins = dve.tensor_scalar(gg[:, m, :], ps[:, 5, m * T:(m + 1) * T], P1("gla_b")[:, m:m + 1],
                                                None, ALU.add)
                    done(ins)
                    tell(dve.tensor_copy(W[:, 2, 0:2 * T], flat(gg[:, :, :])), to_act)
                    dve.wait_ge(to_dve2.sem, to_dve2.base + 1)
                    done(dve.scalar_tensor_tensor(flat(gg[:, :, :]), flat(gg[:, :, :]), 0.0, W[:, 2, 0:2 * T],
                                                  ALU.min, ALU.subtract))
                    dve.tensor_scalar(gg[:, :, :], gg[:, :, :], 1.0 / GLA_TAU, None, ALU.mult)

                @block.scalar
                def _(act):
                    for p in mine:
                        proj.scalar(act, p)
                    log_sigmoid_tail(act, W[:, 2, 0:2 * T], (to_act.sem, to_act.base + 1), to_dve2)

        def linear_attention(q, k, v, g, tiles, dk, gate, gain, branch, proj, n_proj):
            mine = list(proj.take(n_proj))
            n = tiles * T
            b = W[:, 0, 0:n]
            b4 = b.rearrange("p (f t s) -> p f t s", f=tiles, t=TT)
            fold = [W[:, 1, 0:n], W[:, 2, 0:n]]
            decay = [flat(sq[:, 4 * i:4 * i + tiles, :]) for i in range(2)]
            qf, kf = flat(q[:, :, :]), flat(k[:, :, :])
            steps = LEVELS + 2
            per_head = P // dk

            def head(buf3, h, t):
                lo = h % per_head * dk
                return buf3[lo:lo + dk, h // per_head, t * P:(t + 1) * P]

            def place(h, t):
                return (t, h) if per_head == 1 else (h % 2, 2 * t + h // 2)

            def cross_place(h):
                return h if per_head == 1 else h % 2 * 2 + h // 2

            with new_block() as block:
                @block.sync
                def _(sp):
                    proj.sync(sp)

                @block.vector
                def _(dve):
                    done = InOrder(dve, dve_step)
                    for f in range(tiles):
                        for t in range(TT):
                            ins = dve.tensor_tensor_scan(b4[:, f, t, :], ones, g[:, f, t * P:(t + 1) * P], 0.0,
                                                         ALU.mult, ALU.add)
                    done(ins)

                    def halves(a, lv):
                        m = 1 << lv
                        v4 = a.rearrange("p (n two m) -> p n two m", two=2, m=m)
                        return v4[:, :, 0, :], v4[:, :, 1, :]

                    def exponents(lv):
                        if lv >= 2:
                            dve.wait_ge(to_pe.sem, to_pe.base + lv - 1)
                        first, second = halves(b, lv)
                        e1, e2 = halves(decay[lv % 2], lv)
                        ref = first[:, :, (1 << lv) - 1:1 << lv].broadcast_to(list(first.shape))
                        dve.tensor_tensor(e1, ref, first, ALU.subtract)
                        if lv < LEVELS:
                            ins = dve.tensor_tensor(e2, second, ref, ALU.subtract)
                        else:
                            ins = dve.tensor_copy(e2, second)
                        tell(ins, to_act)

                    def weigh(lv):
                        dve.wait_ge(to_dve.sem, to_dve.base + lv + 1)
                        if lv >= 2:
                            dve.wait_ge(score_done.sem, score_done.base + lv)
                        e1, e2 = halves(decay[lv % 2], lv)
                        f1, f2 = halves(fold[lv % 2], lv)
                        dve.tensor_tensor(f1, halves(kf, lv)[0], e1, ALU.mult)
                        tell(dve.tensor_tensor(f2, halves(qf, lv)[1], e2, ALU.mult), to_pe)

                    def pick(step):
                        dve.wait_ge(score_done.sem, score_done.base + step + 1)
                        if step:
                            dve.wait_ge(prob_ready.sem, prob_ready.base + step)
                        bank = 4 + step % 2 * 2
                        if step == 0:
                            for i in range(2):
                                ins = dve.tensor_tensor(
                                    scores[:, 4 * i:4 * i + 4, :],
                                    ps[:, bank + i, :].rearrange("p (h t) -> p h t", h=4),
                                    ident.unsqueeze(1).broadcast_to([P, 4, P]), ALU.mult)
                        elif step <= LEVELS:
                            mask = C("level", (step - 1) * P, P).bitcast(U32).unsqueeze(1).broadcast_to([P, 4, P])
                            for i in range(2):
                                ins = dve.copy_predicated(scores[:, 4 * i:4 * i + 4, :], mask,
                                                          ps[:, bank + i, :].rearrange("p (h t) -> p h t", h=4))
                        else:
                            for i in range(per_head):
                                w = 4 // per_head
                                ins = dve.tensor_copy(cross[:, i * w:(i + 1) * w, :],
                                                      ps[:, bank + i, 0:w * P].rearrange("p (h t) -> p h t", h=w))
                        tell(ins, prob_ready)

                    exponents(0)
                    for step in range(steps):
                        if step + 1 < LEVELS + 1:
                            exponents(step + 1)
                        if step < LEVELS + 1:
                            weigh(step)
                        pick(step)
                        if step:
                            for p in mine[step - 1:step]:
                                proj.vector(dve, p)
                    dve.wait_ge(to_act.sem, to_act.base + LEVELS + 1)
                    dve.wait_ge(to_pe.sem, to_pe.base + LEVELS + 1)
                    dve.wait_ge(summed.sem, summed.base + 1)
                    for i in range(2):
                        ins = dve.tensor_scalar(W[:, 0, i * BANK:(i + 1) * BANK], ps[:, 6 + i, :], 1.0 / 128, EPS,
                                                ALU.mult, ALU.add)
                    tell(ins, variance)
                    dve.wait_ge(deviation.sem, deviation.base + 1)
                    done(dve.reciprocal(W[:, 0, :], W[:, 0, :]))
                    for h in range(4):
                        ins = dve.scalar_tensor_tensor(
                            W[:, 1, h * T:(h + 1) * T], ps[:, 4 + h // 2, h % 2 * T:(h % 2 + 1) * T],
                            gain[:, h:h + 1], W[:, 0, h * T:(h + 1) * T], ALU.mult, ALU.mult)
                    done(ins)
                    tell(dve.tensor_tensor(W[:, 1, :], W[:, 1, :], flat(gate[:, :, :]), ALU.mult), to_act)
                    dve.wait_ge(to_dve.sem, to_dve.base + LEVELS + 2)
                    dve.tensor_tensor(flat(yl[:, branch, :, :]), W[:, 1, :], flat(yh[:, branch, :, :]).bitcast(F32),
                                      ALU.subtract)

                @block.scalar
                def _(act):
                    for lv in range(LEVELS + 1):
                        act.wait_ge(to_act.sem, to_act.base + lv + 1)
                        tell(act.activation(decay[lv % 2], decay[lv % 2], ACT.Exp), to_dve)
                        if lv >= 2:
                            for p in mine[lv - 2:lv - 1]:
                                proj.scalar(act, p)
                    for p in mine[LEVELS - 1:]:
                        proj.scalar(act, p)
                    act.wait_ge(pv_done.sem, pv_done.base + 1)
                    for i in range(2):
                        ins = act.activation(flat(sq[:, 2 * i:2 * i + 2, :]), ps[:, 4 + i, :], ACT.Square)
                    tell(ins, squares)
                    act.wait_ge(variance.sem, variance.base + 1)
                    tell(act.activation(W[:, 0, :], W[:, 0, :], ACT.Sqrt), deviation)
                    act.wait_ge(to_act.sem, to_act.base + LEVELS + 2)
                    tell(act.copy(flat(yh[:, branch, :, :]), W[:, 1, :]), to_dve)

                @block.tensor
                def _(pe):
                    for step in range(steps):
                        if step:
                            pe.wait_ge(to_pe.sem, to_pe.base + step)
                        if step >= 2:
                            pe.wait_ge(prob_ready.sem, prob_ready.base + step - 1)
                        bank = 4 + step % 2 * 2
                        f3 = fold[(step - 1) % 2].rearrange("p (f t) -> p f t", f=tiles)
                        for t in range(TT if step <= LEVELS else 1):
                            for h in range(4):
                                i, c0 = place(h, t)
                                out_ = ps[:, bank + i, c0 * P:(c0 + 1) * P]
                                if step == 0:
                                    a, c = head(k, h, t), head(q, h, t)
                                elif step <= LEVELS:
                                    a = c = head(f3, h, t)
                                else:
                                    a, c = head(f3, h, 0), head(f3, h, 1)
                                ins = pe.matmul(out_, a, c, start=True, stop=True)
                        tell(ins, score_done)
                        for p in mine[step:step + 1]:
                            proj.tensor(pe, p)
                    pe.wait_ge(prob_ready.sem, prob_ready.base + steps)
                    for h in range(4):
                        o = ps[:, 4 + h // 2, h % 2 * T:(h % 2 + 1) * T]
                        vh = [v[:, t, h * P:(h + 1) * P] for t in range(TT)]
                        own = [scores[:, 4 * place(h, t)[0] + place(h, t)[1], :] for t in range(TT)]
                        pe.matmul(o[:, 0:P], vh[0], own[0], start=True, stop=True)
                        pe.matmul(o[:, P:T], vh[1], own[1], start=True, stop=False)
                        ins = pe.matmul(o[:, P:T], vh[0], cross[:, cross_place(h), :], start=False, stop=True)
                    tell(ins, pv_done)
                    pe.wait_ge(squares.sem, squares.base + 1)
                    for i in range(2):
                        ins = pe.matmul(ps[:, 6 + i, :], ones, flat(sq[:, 2 * i:2 * i + 2, :]), start=True, stop=True)
                    tell(ins, summed)

        def attention(block, items, q_of, k_of, add_of, weight_of, small, prob, turned, values, act_after,
                      dve_after):
            parts = ((0, P), (P, 3 * P))

            @block.tensor
            def _(pe):
                def score(i):
                    if i >= 2:
                        pe.wait_ge(to_pe.sem, to_pe.base + i - 1)
                    for t, (lo, hi) in enumerate(parts):
                        ins = pe.matmul(ps[:, 4 + i % 2, lo:hi], q_of(i, t), k_of(i, hi - lo), start=True, stop=True)
                    tell(ins, score_done)

                def turn(i):
                    pe.wait_ge(prob_ready.sem, prob_ready.base + i + 1)
                    if i >= 2:
                        pe.wait_ge(pt_ready.sem, pt_ready.base + i - 1)
                    for c in range(3):
                        ins = pe.transpose(ps[:, 6 + i % 2, c * P:(c + 1) * P], prob[i % 2][:, c * P:(c + 1) * P], ident)
                    tell(ins, pt_done)

                score(0)
                score(1)
                for i in range(items):
                    turn(i)
                    if i + 2 < items:
                        score(i + 2)
                    values(pe, i)

            @block.vector
            def _(dve):
                done = InOrder(dve, dve_step)

                def rows_max(i):
                    s = small[:, i % 2, :]
                    dve.wait_ge(score_done.sem, score_done.base + i + 1)
                    if i >= 2:
                        dve.wait_ge(pt_done.sem, pt_done.base + i - 1)
                    tell(dve.scalar_tensor_tensor(prob[i % 2], ps[:, 4 + i % 2, 0:3 * P], NSA_DH ** -0.5, add_of(i),
                                                  ALU.mult, ALU.add), to_pe)
                    dve.wait_ge(to_pe.sem, to_pe.n)
                    for t, (lo, hi) in enumerate(parts):
                        ins = dve.tensor_reduce(s[:, t:t + 1], prob[i % 2][:, lo:hi], AX_X, ALU.max)
                    done(ins)
                    tell(dve.tensor_scalar(s[:, 2:4], s[:, 0:2], -1.0, None, ALU.mult), to_act)

                def normalise(i):
                    s = small[:, i % 2, :]
                    dve.wait_ge(to_dve.sem, to_dve.base + i + 1)
                    done(dve.reciprocal(s[:, 6:8], s[:, 4:6]))
                    if weight_of(i) is not None:
                        done(dve.tensor_tensor(s[:, 6:8], s[:, 6:8], weight_of(i), ALU.mult))
                    for t, (lo, hi) in enumerate(parts):
                        ins = dve.tensor_scalar(prob[i % 2][:, lo:hi], prob[i % 2][:, lo:hi], s[:, 6 + t:7 + t], None,
                                                ALU.mult)
                    tell(ins, prob_ready)

                rows_max(0)
                for i in range(items):
                    if i + 1 < items:
                        rows_max(i + 1)
                    normalise(i)
                dve_after(dve)

            @block.scalar
            def _(act):
                def exponentials(i):
                    s = small[:, i % 2, :]
                    act.wait_ge(to_act.sem, to_act.base + i + 1)
                    for t, (lo, hi) in enumerate(parts):
                        ins = act.activation(prob[i % 2][:, lo:hi], prob[i % 2][:, lo:hi], ACT.Exp,
                                             bias=s[:, 2 + t:3 + t], accum_out=s[:, 4 + t:5 + t])
                    tell(ins, to_dve)

                exponentials(0)
                for i in range(items):
                    if i + 1 < items:
                        exponentials(i + 1)
                    act.wait_ge(pt_done.sem, pt_done.base + i + 1)
                    act_after(act, i)
                    tell(act.copy(turned(i), ps[:, 6 + i % 2, 0:3 * P]), pt_ready)
                act_after(act, items)

        cstat = sb("cstat", [P, 4, 16], branches)
        kcd = sb("kcd", [P, 2 * NCMP], branches)
        vcm = sb("vcm", [P, NSA_G * NSA_DH], branches)
        hid = sb("hid", [P, 2, 2 * NCMP], branches)
        posh = sb("posh", [P, 32], branches, F32R)
        posl = sb("posl", [P, 32], branches, F32R)

        def rope():
            with new_block() as block:
                @block.tensor
                def _(pe):
                    for j in range(5):
                        if j == 4:
                            pe.wait_ge(to_pe.sem, to_pe.base + 1)
                        tell(pe.matmul(ps[:, 4 + j % 4, :], C("rot"), flat(qk[:, 2 * j:2 * j + 2, :]), start=True,
                                       stop=True), to_dve)

                @block.vector
                def _(dve):
                    done = InOrder(dve, dve_step)
                    cos, sin = (C(n).unsqueeze(1).broadcast_to([P, 2, T]) for n in ("cos", "sin"))
                    for j in range(5):
                        x = qk[:, 2 * j:2 * j + 2, :]
                        turned = W[:, j % 2, 0:BANK].rearrange("p (m t) -> p m t", m=2)
                        dve.wait_ge(to_dve.sem, to_dve.base + j + 1)
                        ins = dve.tensor_tensor(turned, ps[:, 4 + j % 4, :].rearrange("p (m t) -> p m t", m=2), sin,
                                                ALU.mult)
                        if j == 0:
                            tell(ins, to_pe)
                        done(dve.tensor_tensor(x, x, cos, ALU.mult))
                        done(dve.tensor_tensor(x, x, turned, ALU.add))

        def compress(w):
            kd = [W[:, 0, i * 2 * T:(i + 1) * 2 * T].rearrange("p (g t) -> p g t", g=2) for i in range(2)]
            kh, kl = ([a[:, 2, 2 * i:2 * i + 2, :] for i in range(2)] for a in (yh, yl))
            at, _ = PAR1["pos_k"]
            pos = par1[:, at:at + 32]
            rows_ = ((slice(0, NSA_DH), T), (slice(NSA_DH, P), T - 1))
            with new_block() as block:
                @block.sync
                def _(sp):
                    w.sync(sp)

                @block.vector
                def _(dve):
                    for i, src in enumerate((qk[:, 4:6, :], vc[:, :, :])):
                        dve.tensor_copy(kd[i][0:NSA_DH, :, :], src[0:NSA_DH, :, :])
                        ins = dve.tensor_copy(kd[i][NSA_DH:P, :, 0:T - 1], src[NSA_DH:P, :, 1:T])
                        tell(ins, to_act)
                    for i in range(2):
                        dve.wait_ge(to_dve.sem, to_dve.base + i + 1)
                        if i == 0:
                            dve.tensor_tensor(posl[:, :], pos, posh[:, :].bitcast(F32), ALU.subtract)
                        for r, n in rows_:
                            ins = dve.tensor_tensor(kl[i][r, :, 0:n], kd[i][r, :, 0:n], kh[i][r, :, 0:n].bitcast(F32),
                                                    ALU.subtract)
                        tell(ins, to_pe)
                    for i in range(2):
                        w.vector(dve, 2 * i)
                        dve.wait_ge(*w.done(2 * i + 1))
                        tell(dve.tensor_copy(cstat[:, 0, i:i + 1], ps[:, 4 + i, 64:65]), to_act)
                        w.vector(dve, 2 * i + 1)
                    dve.wait_ge(to_dve.sem, to_dve.base + 3)
                    dve.tensor_copy(kcd[:, :], ps[:, 6, 0:2 * NCMP])
                    for i in range(4):
                        dve.tensor_copy(vcm[32 * i:32 * i + NCMP, :], ps[32 * i:32 * i + NCMP, 7, 0:NSA_G * NSA_DH])

                @block.tensor
                def _(pe):
                    for i in range(2):
                        pe.wait_ge(to_pe.sem, to_pe.base + i + 1)
                        halves = [w.arrived(pe, 2 * i + u) for u in range(2)]
                        for what in range(2):
                            for j in range(2 * BLOCKS):
                                if what:
                                    x = [a[:, 16 * i + j:16 * i + j + 1].broadcast_to([P, 2]) for a in (posh, posl)]
                                    o = ps[:, 4 + i, 64:66]
                                else:
                                    x = [a[i][:, :, 2 * j:2 * j + CMP_STRIDE * (NCMP - 1) + 1:CMP_STRIDE]
                                         .rearrange("p g n -> p n g") for a in (kh, kl)]
                                    o = ps[:, 4 + i, 0:2 * NCMP].rearrange("p (n g) -> p n g", g=2)
                                at = j % BLOCKS * P
                                ins = three_products(pe, o, [a[:, at:at + P] for a in halves[j // BLOCKS]], x, j == 0,
                                                     j == 2 * BLOCKS - 1)
                                if what and j % BLOCKS == BLOCKS - 1:
                                    ins.then_inc(ring.unit_done.sem, 1)
                    pe.wait_ge(to_pe2.sem, to_pe2.base + 2)
                    pe.matmul(ps[:, 6, 0:2 * NCMP], P1("w2_k"), hid[:, 0, :], start=True, stop=True)
                    for i in range(4):
                        for g in range(NSA_G):
                            ins = pe.matmul(ps[32 * i:32 * i + NCMP, 7, g * NSA_DH:(g + 1) * NSA_DH],
                                            hid[:, 1, g * NCMP:(g + 1) * NCMP], P1("w2_v"), start=True, stop=True,
                                            tile_position=(0, 32 * i))
                    tell(ins, to_dve)

                @block.scalar
                def _(act):
                    act.copy(posh[:, :], pos)
                    for i in range(2):
                        act.wait_ge(to_act.sem, to_act.base + i + 1)
                        for r, n in rows_:
                            ins = act.copy(kh[i][r, :, 0:n], kd[i][r, :, 0:n])
                        tell(ins, to_dve)
                    for i in range(2):
                        w.scalar(act, 2 * i)
                        act.wait_ge(to_act.sem, to_act.base + i + 3)
                        ins = act.activation(hid[:, i, :].rearrange("p (g n) -> p g n", g=2),
                                             ps[:, 4 + i, 0:2 * NCMP].rearrange("p (n g) -> p g n", g=2), ACT.Gelu_apprx_tanh,
                                             bias=cstat[:, 0, i:i + 1])
                        tell(ins, to_pe2)
                        w.scalar(act, 2 * i + 1)
                    act.activation(flat(gates[:, :, :]), flat(gates[:, :, :]), ACT.Sigmoid)

        def query_half(h, buf, t):
            lo = h % 2 * NSA_DH
            return buf[lo:lo + NSA_DH, h // 2, t * P:(t + 1) * P]

        pc = W[:, 1, 0:BANK].rearrange("p (t h n) -> p t h n", t=TT, h=NSA_H)
        ptc = W[:, 2, 0:BANK].rearrange("p (i t) -> p i t", i=4)

        def compressed_probabilities():
            def over_heads(name, n):
                return C(name).rearrange("p (t n) -> p t n", t=TT)[:, :, 0:n].unsqueeze(2) \
                    .broadcast_to([P, TT, NSA_H, n])

            def over_keys(a, n):
                return a.rearrange("p (t h) -> p t h", t=TT).unsqueeze(3).broadcast_to([P, TT, NSA_H, n])

            with new_block() as block:
                @block.tensor
                def _(pe):
                    for t in range(TT):
                        for h in range(NSA_H):
                            lo, g = h % 2 * NSA_DH, h // 4
                            at = t * P + h // 2 * 32
                            ins = pe.matmul(ps[:, 4 + h % 2, at:at + NCMP], query_half(h, qk, t),
                                            kcd[lo:lo + NSA_DH, g * NCMP:(g + 1) * NCMP], start=True, stop=True)
                    tell(ins, score_done)
                    pe.wait_ge(prob_ready.sem, prob_ready.base + 1)
                    for i in range(4):
                        ins = pe.transpose(ps[:, 6, i * P:(i + 1) * P], W[:, 1, i * P:(i + 1) * P], ident)
                    tell(ins, pt_done)

                @block.vector
                def _(dve):
                    done = InOrder(dve, dve_step)
                    done(dve.memset(W[:, 1, 0:BANK], 0.0))
                    dve.wait_ge(score_done.sem, score_done.base + 1)
                    pairs = pc.rearrange("p t (h two) n -> p t h two n", two=2)
                    for i in range(2):
                        s4 = ps[:, 4 + i, 0:T].rearrange("p (t h n) -> p t h n", t=TT, h=NSA_H // 2)
                        ins = dve.tensor_tensor(pairs[:, :, :, i, 0:NCMP], s4[:, :, :, 0:NCMP],
                                                over_heads("cmp_neg", NCMP)[:, :, 0:NSA_H // 2, :], ALU.add)
                    done(ins)
                    done(dve.tensor_reduce(cstat[:, 1, :].rearrange("p (t h) -> p t h", t=TT), pc[:, :, :, 0:NCMP], AX_X,
                                           ALU.max))
                    tell(dve.tensor_tensor(pc[:, :, :, 0:NCMP], pc[:, :, :, 0:NCMP], over_keys(cstat[:, 1, :], NCMP),
                                           ALU.subtract), to_act)
                    dve.wait_ge(to_dve.sem, to_dve.base + 1)
                    done(dve.tensor_reduce(cstat[:, 2, :].rearrange("p (t h) -> p t h", t=TT), pc[:, :, :, 0:NCMP], AX_X,
                                           ALU.add))
                    done(dve.reciprocal(cstat[:, 3, :], cstat[:, 2, :]))
                    gate = gates[:, :, :].rearrange("p t (h k) -> p t h k", k=3)[:, :, :, 0]
                    rec = cstat[:, 3, :].rearrange("p (t h) -> p t h", t=TT)
                    dve.tensor_tensor(rec, rec, gate, ALU.mult)
                    done(dve.tensor_tensor(pc, pc, over_heads("cmp_keep", 32), ALU.mult))
                    tell(dve.tensor_tensor(pc, pc, over_keys(cstat[:, 3, :], 32), ALU.mult), prob_ready)
                    dve.wait_ge(pt_done.sem, pt_done.base + 1)
                    dve.tensor_copy(W[:, 2, 0:BANK], ps[:, 6, :])

                @block.scalar
                def _(act):
                    act.wait_ge(to_act.sem, to_act.base + 1)
                    tell(act.activation(W[:, 1, 0:BANK], W[:, 1, 0:BANK], ACT.Exp, scale=NSA_DH ** -0.5), to_dve)

        def sparse_attention():
            sqf = flat(sq[:, :, :])
            turned = lambda i: sqf[:, i % 4 * BANK:i % 4 * BANK + 3 * P]
            prob = [W[:, 0, 0:3 * P], W[:, 0, BANK:BANK + 3 * P]]
            gate4 = gates[:, :, :].rearrange("p t (h k) -> p t h k", k=3)

            def values(pe, i):
                if i % 2 == 0:
                    return
                h = i // 2
                g, lo, c32 = h // 4, h % 2 * NSA_DH, 32 * (h % 4)
                pe.wait_ge(pt_ready.sem, pt_ready.base + i + 1)
                for t in range(TT):
                    o = ps[lo:lo + NSA_DH, h // 2, t * P:(t + 1) * P]
                    pe.matmul(o, vcm[c32:c32 + NCMP, g * NSA_DH:(g + 1) * NSA_DH],
                              ptc[c32:c32 + NCMP, 2 * t + h // 4, :], start=True, stop=False, tile_position=(c32, lo))
                    for b in range(2):
                        for s in range(t + 1):
                            ins = pe.matmul(o, vsw[:, s, b * P + g * NSA_DH:b * P + (g + 1) * NSA_DH],
                                            turned(2 * h + b)[:, (t + s) * P:(t + s + 1) * P], start=False,
                                            stop=(b == 1 and s == t))
                tell(ins, pv_done)

            def act_after(act, i):
                if 4 <= i < 2 * NSA_H:
                    act.wait_ge(pv_done.sem, pv_done.base + (i - 4) // 2 + 1)
                if i == 2 * NSA_H:
                    act.wait_ge(pv_done.sem, pv_done.base + NSA_H)
                    for m in range(4):
                        ins = act.copy(yh[:, 2, m, :], ps[:, m, 0:T])
                    tell(ins, to_dve2)

            def dve_after(dve):
                dve.wait_ge(to_dve2.sem, to_dve2.base + 1)
                for m in range(4):
                    dve.tensor_tensor(yl[:, 2, m, :], ps[:, m, 0:T], yh[:, 2, m, :].bitcast(F32), ALU.subtract)

            with new_block() as block:
                attention(block, 2 * NSA_H, lambda i, t: query_half(i // 2, qk, t),
                          lambda i, n: qk[i // 2 % 2 * NSA_DH:(i // 2 % 2 + 1) * NSA_DH, 6 + 2 * (i % 2) + i // 8, 0:n],
                          lambda i: C("causal_neg"), lambda i: gate4[:, :, i // 2, 1 + i % 2],
                          small, prob, turned, values, act_after, dve_after)

        def mix_branches():
            w = ring.claim(9 * KD // 2)
            turns = N_BR * KD // 2
            gates_of, branch_of = [], []
            for n in range(turns):
                gates_of.append(Product(w, 3 * n * BLOCKS, 2, KD, banks))
                branch_of.append(Product(w, (3 * n + 2) * BLOCKS, 2, 4, banks))
            sig = lambda n: W[:, 2, n % 2 * BANK:(n % 2 + 1) * BANK]
            with new_block() as block:
                @block.sync
                def _(sp):
                    w.sync(sp)

                @block.tensor
                def _(pe):
                    for n in range(turns):
                        b = n // (KD // 2)
                        gates_of[n].tensor(pe, h, 0)
                        branch_of[n].tensor(pe, (yh[:, b, :, :], yl[:, b, :, :]), 0)

                @block.scalar
                def _(act):
                    for n in range(turns):
                        w.scalar(act, 3 * n)
                        acc = gates_of[n].wait(act, 0)
                        if n >= 2:
                            branch_of[n - 2].after_read(act, 0)
                        act.activation(sig(n), acc, ACT.Sigmoid).then_inc(gates_of[n].read(0), 1)
                        w.scalar(act, 3 * n + 1)
                        w.scalar(act, 3 * n + 2)

                @block.vector
                def _(dve):
                    done = InOrder(dve, dve_step)
                    for n in range(turns):
                        b, j = n // (KD // 2), n % (KD // 2)
                        w.vector(dve, 3 * n)
                        w.vector(dve, 3 * n + 1)
                        acc = branch_of[n].wait(dve, 0)
                        gates_of[n].after_read(dve, 0)
                        m = flat(sq[:, 2 * j:2 * j + 2, :])
                        if b == 0:
                            dve.tensor_tensor(m, acc, sig(n), ALU.mult).then_inc(branch_of[n].read(0), 1)
                        else:
                            part = W[:, j % 2, 0:BANK]
                            dve.tensor_tensor(part, acc, sig(n), ALU.mult).then_inc(branch_of[n].read(0), 1)
                            branch_of[n].after_read(dve, 0)
                            done(dve.tensor_tensor(m, m, part, ALU.add))
                        w.vector(dve, 3 * n + 2)
            split_into_h(sq)

        def split_into_h(x):
            with new_block() as block:
                @block.scalar
                def _(act):
                    for c in range(KD // 2):
                        tell(act.copy(hh[:, 2 * c:2 * c + 2, :], x[:, 2 * c:2 * c + 2, :]), to_dve)

                @block.vector
                def _(dve):
                    for c in range(KD // 2):
                        low_half(dve, c, x)

        ada_full = [sem(f"ada_full{i}") for i in range(2)]
        c_loaded = sem("c_loaded")
        ada_used = signal("ada_used")
        ADA = 6 * KD

        class Modulation:

            def __init__(self, layer, scope):
                self.layer = layer
                self.rows = sb("ada_rows", [P, 2, D], scope)
                self.c = sb("c_act", [P, D], scope)
                self.now = sb("mod_now", [P, ADA], scope)
                self.dealt = self.loads = 0

            def sync(self, sp, upto):
                if self.loads == 0:
                    sp.dma_start(self.c[:, :], c_in).then_inc(c_loaded, 16)
                for i in range(self.loads, min(upto + 2, ADA)):
                    self.loads = i + 1
                    if i >= 2:
                        sp.wait_ge(ada_used.sem, i - 1)
                    sp.dma_start(self.rows[:, i % 2, :], ada_in[bass.ds(self.layer * ADA + i, 1), :, :]
                                   .rearrange("o p n -> p (o n)")).then_inc(ada_full[i % 2], 16)

            def scalar(self, act):
                act.wait_ge(c_loaded, 16)
                tell(act.activation(self.c[:, :], self.c[:, :], ACT.Silu), to_pool)

            def vector(self, dve, upto):
                for i in range(self.dealt, min(upto, ADA)):
                    if i == 0:
                        dve.wait_ge(to_pool.sem, to_pool.base + 1)
                    dve.wait_ge(ada_full[i % 2], 16 * (i // 2 + 1))
                    r = self.rows[:, i % 2, :]
                    dve.scalar_tensor_tensor(r, r, 1.0, self.c[:, :], ALU.mult, ALU.mult,
                                             accum_out=self.now[:, i:i + 1]).then_inc(ada_used.sem, ada_used.one())
                    self.dealt = i + 1

            def finish(self, dve):
                dve.wait_ge(ada_used.sem, ADA)
                at, _ = PAR2["ada_b0"]
                both = par2[:, at:at + 2 * ADA].rearrange("p (l n) -> p l n", l=2)
                dve.tensor_tensor(mod[:, bass.ds(self.layer, 1), :], self.now[:, :].unsqueeze(1),
                                  both[:, bass.ds(self.layer, 1), :], ALU.add)

        IN_SWIGLU = 32

        def swiglu_hidden(fh, fl, mods):
            w = ring.claim(2 * KF)
            prod = Product(w, 0, 2 * KF, KD, banks)
            sqf = flat(sq[:, :, :])
            buf = lambda i: sqf[:, i % 4 * BANK:(i % 4 + 1) * BANK]
            with new_block() as block:
                @block.sync
                def _(sp):
                    for i in range(w.n):
                        mods.sync(sp, min(i // 4 * 3 + min(i % 4, 2), IN_SWIGLU))
                        w.sync(sp, [i])

                @block.tensor
                def _(pe):
                    for j in range(KF):
                        prod.tensor(pe, h, j)

                @block.scalar
                def _(act):
                    mods.scalar(act)
                    for i in range(KF // 2):
                        w.scalar(act, 4 * i)
                        acc = prod.wait(act, 2 * i)
                        if i >= 4:
                            act.wait_ge(to_act.sem, to_act.base + i - 3)
                        act.activation(buf(i), acc, ACT.Silu).then_inc(prod.read(2 * i), 1)
                        for u in range(1, 4):
                            w.scalar(act, 4 * i + u)
                        prod.after_read(act, 2 * i + 1)
                        tell(act.copy(flat(fh[:, 2 * i:2 * i + 2, :]), buf(i)), to_dve)

                @block.vector
                def _(dve):
                    for i in range(KF // 2):
                        for u in range(3):
                            w.vector(dve, 4 * i + u)
                            mods.vector(dve, min(3 * i + u, IN_SWIGLU))
                        acc = prod.wait(dve, 2 * i + 1)
                        prod.after_read(dve, 2 * i)
                        dve.tensor_tensor(buf(i), buf(i), acc, ALU.mult).then_inc(prod.read(2 * i + 1), 1)
                        w.vector(dve, 4 * i + 3)
                        dve.wait_ge(to_dve.sem, to_dve.base + i + 1)
                        tell(dve.tensor_tensor(flat(fl[:, 2 * i:2 * i + 2, :]), buf(i),
                                               flat(fh[:, 2 * i:2 * i + 2, :]).bitcast(F32), ALU.subtract), to_act)
                    mods.vector(dve, IN_SWIGLU)

        def skip_fillers():
            w = ring.claim(3)
            with new_block() as block:
                @block.sync
                def _(sp):
                    w.sync(sp)

                @block.tensor
                def _(pe):
                    for i in range(w.n):
                        hi, _ = w.arrived(pe, i)
                        pe.matmul(ps[:, 4, 0:P], hi[:, 0:P], hi[:, 0:P], start=True, stop=True) \
                            .then_inc(ring.unit_done.sem, 1)

                @block.scalar
                def _(act):
                    for i in range(w.n):
                        w.scalar(act, i)

                @block.vector
                def _(dve):
                    for i in range(w.n):
                        w.vector(dve, i)

        restart_counts()
        restart_ring()
        with nc.Fori(0, DEPTH) as layer:
            ring.place, ring.base = 0, layer * N_U1
            with new_block() as block:
                @block.scalar
                def _(act):
                    act.dma_start(par1[:, :], par1_in[bass.ds(layer, 1), :, :].rearrange("o p n -> p (o n)")) \
                        .then_inc(par_loaded, 16)
                    act.wait_ge(par_loaded, 16)
            rms_norm(P1("norm1"))
            proj = Projections()
            project(proj, 6)
            prepare_hgrn(layer, proj, 3)
            linear_attention(hq, hk, hv, hf, HG_H, HG_D, hog, P1("hg_norm"), 0, proj, 7)
            prepare_gla(proj, 1)
            linear_attention(gq, gk, gv, gg, GLA_H * GLA_DK // P, GLA_DK, gog, P1("gla_norm"), 1, proj, 5)
            assert proj.mine.stop == len(proj.pairs)
            rope()
            compress(ring.claim(4))
            compressed_probabilities()
            sparse_attention()
            mix_branches()
            branches.close()
            ffn = ExitStack()
            fh = sb("ffn_high", [P, KF, T], ffn, F32R)
            fl = sb("ffn_low", [P, KF, T], ffn, F32R)
            mods = Modulation(layer, ffn)
            residual_product(8, KD, h)
            rms_norm(P1("norm2"))
            swiglu_hidden(fh, fl, mods)
            residual_product(22, KF, (fh, fl), mods=mods)
            skip_fillers()
            ffn.close()
            restart_counts()
            restart_ring()
        rms_norm(P2("final_1"), out=xT)
        hybrid.close()

        ring.place, ring.base, ring.limit = 0, DEPTH * N_U1, N_U2
        adaln = everywhere.enter_context(ExitStack())
        hT = sb("hT", [P, KD, T], adaln)
        mgain = sb("mgain", [P, 4, KD], adaln)
        logits = sb("logits", [P, TT, RT], adaln)
        rtmp = sb("rtmp", [P, TT, 80], adaln)
        combine = sb("combine", [P, TT, E_N], adaln)
        ccol = sb("ccol", [P, TT, 4], adaln)

        def modulated_gains():
            with new_block() as block:
                @block.vector
                def _(dve):
                    for l in range(2):
                        for i, scale_at in enumerate((8, 32)):
                            dve.scalar_tensor_tensor(mgain[:, 2 * l + i, :], mod[:, l, scale_at:scale_at + 8], 1.0,
                                                     P2(f"norm{i + 1}_{l}"), ALU.add, ALU.mult)

        def shift(l, i):
            return mod[:, l, 24 * i:24 * i + 8]

        def gate(l, i):
            return mod[:, l, 24 * i + 16:24 * i + 24]

        def pool_and_chunk_attention():
            pa = ExitStack()
            u = sb("u", [P, 3, 4, T], pa)
            q = sb("q", [P, 4, T], pa)
            k = sb("k", [P, 4, T], pa)
            v = sb("v", [P, TT, 512], pa)
            mean = sb("mean", [P, 2, 4, T], pa)
            cath = sb("cat_high", [P, KD, T], pa, F32R)
            catl = sb("cat_low", [P, KD, T], pa, F32R)
            bias = sb("bias", [P, ATT_H, 3 * P], pa)
            rev = sb("rev", [P, ATT_H, 3 * P], pa)
            probs = sb("probs", [P, 2, 3 * P], pa)
            w = ring.claim(16)
            prods = [Product(w, 4 * BLOCKS * i, 4, KD, banks, token_major=(i == 3)) for i in range(4)]
            with new_block() as block:
                @block.sync
                def _(sp):
                    w.sync(sp)

                @block.tensor
                def _(pe):
                    for prod in prods:
                        for j in range(2):
                            prod.tensor(pe, h, j)

                @block.vector
                def _(dve):
                    for prod, dst in zip(prods, (u[:, 0, :, :], q, k, v)):
                        for j in range(2):
                            units = list(prod.units_of(j))
                            w.vector(dve, units[0])
                            acc = prod.wait(dve, j).rearrange("p (m t) -> p m t", m=2)
                            to = dst[:, :, j * T:(j + 1) * T] if dst is v else dst[:, 2 * j:2 * j + 2, :]
                            dve.tensor_copy(to, acc).then_inc(prod.read(j), 1)
                            w.vector(dve, units[1])

                @block.scalar
                def _(act):
                    for h in range(ATT_H):
                        for lo, n, first in ((0, P, REL - (P - 1)), (P, 2 * P, REL + P - (T - 1))):
                            row = bias_in[h, first:first + P + n - 1]
                            src = bass.AP(tensor=row.tensor, offset=row.offset, ap=[[1, P], [1, n]])
                            act.dma_start(rev[:, h, lo:lo + n], src).then_inc(loaded, 16)
                    for i in range(w.n):
                        w.scalar(act, i)
                    act.wait_ge(loaded, 16 * (4 + 2 * ATT_H))
            with new_block() as block:
                @block.vector
                def _(dve):
                    done = InOrder(dve, dve_step)
                    for lo, n in ((0, P), (P, 2 * P)):
                        ins = dve.tensor_copy(bias[:, :, lo:lo + n], rev[:, :, lo:lo + n][:, :, ::-1])
                    done(ins)
                    for lo in (0, 2 * P):
                        dve.tensor_tensor(bias[:, :, lo:lo + P], bias[:, :, lo:lo + P],
                                          C("chunk_neg").unsqueeze(1).broadcast_to([P, ATT_H, P]), ALU.add)
                    for d in range(4):
                        s = 1 << d
                        src, dst = u[:, 0 if d == 0 else 1 + (d - 1) % 2, :, :], u[:, 1 + d % 2, :, :]
                        dve.tensor_tensor(dst[:, d:4, s:T], src[:, d:4, s:T], src[:, d:4, 0:T - s], ALU.add)
                        done(dve.tensor_copy(dst[:, d:4, 0:s], src[:, d:4, 0:s]))
                        win = dst[:, d, :]
                        done(dve.tensor_tensor(mean[:, 0, d, 0:16], win[:, 0:16], C("count", 16 * d, 16), ALU.mult))
                        done(dve.tensor_copy(mean[:, 0, d, 16:T], win[:, 16:T]))
                        done(dve.scalar_tensor_tensor(mean[:, 1, d, :], mean[:, 0, d, :], 1.0 / POOL_WINDOWS[d],
                                                      u[:, 0, d, :], ALU.mult, ALU.subtract))
                    tell(dve.memset(small[:, 0, 0:1], 0.0), to_pe)
                    dve.wait_ge(to_dve.sem, to_dve.base + 1)
                    for d in range(4):
                        tell(dve.tensor_scalar(mean[:, 0, d, :], ps[:, 4 + d // 2, d % 2 * T:(d % 2 + 1) * T],
                                               P2("pool_scale")[:, d:d + 1], None, ALU.mult), to_act)
                    for d in range(4):
                        dve.wait_ge(to_dve.sem, to_dve.base + d + 2)
                        dve.tensor_tensor(catl[:, d, :], mean[:, 0, d, :], cath[:, d, :].bitcast(F32), ALU.subtract)

                @block.scalar
                def _(act):
                    for d in range(4):
                        act.wait_ge(to_act.sem, to_act.base + d + 1)
                        tell(act.copy(cath[:, d, :], mean[:, 0, d, :]), to_dve)

                @block.tensor
                def _(pe):
                    pe.wait_ge(to_pe.sem, to_pe.base + 1)
                    for d in range(4):
                        ins = pe.matmul(ps[:, 4 + d // 2, d % 2 * T:(d % 2 + 1) * T], P2("pool_w")[:, d * P:(d + 1) * P],
                                        mean[:, 1, d, :], start=True, stop=True)
                    tell(ins, to_dve)
            sqf = flat(sq[:, :, :])
            turned = lambda i: sqf[:, i % 4 * BANK:i % 4 * BANK + 3 * P]

            def values(pe, h):
                lo = h % 2 * ATT_DH
                pe.wait_ge(pt_ready.sem, pt_ready.base + h + 1)
                for t in range(TT):
                    for s in range(t + 1):
                        ins = pe.matmul(ps[lo:lo + ATT_DH, h // 2, t * P:(t + 1) * P], v[:, s, h * ATT_DH:(h + 1) * ATT_DH],
                                        turned(h)[:, (t + s) * P:(t + s + 1) * P], start=(s == 0), stop=(s == t))
                tell(ins, pv_done)

            def act_after(act, i):
                if 4 <= i < ATT_H:
                    act.wait_ge(pv_done.sem, pv_done.base + i - 3)
                if i == ATT_H:
                    act.wait_ge(pv_done.sem, pv_done.base + ATT_H)
                    for m in range(4):
                        ins = act.copy(cath[:, 4 + m, :], ps[:, m, 0:T])
                    tell(ins, to_dve2)

            def dve_after(dve):
                dve.wait_ge(to_dve2.sem, to_dve2.base + 1)
                for m in range(4):
                    dve.tensor_tensor(catl[:, 4 + m, :], ps[:, m, 0:T], cath[:, 4 + m, :].bitcast(F32), ALU.subtract)

            with new_block() as block:
                attention(block, ATT_H, lambda i, t: query_half(i, q, t),
                          lambda i, n: k[i % 2 * ATT_DH:(i % 2 + 1) * ATT_DH, i // 2, 0:n],
                          lambda i: bias[:, i, :], lambda i: None, small, [probs[:, 0, :], probs[:, 1, :]], turned,
                          values, act_after, dve_after)
            residual_product(8, KD, (cath, catl), gate(0, 0))
            pa.close()

        def router(l):
            parts = [0]

            def scratch(n):
                parts[0] += n
                return rtmp[:, :, parts[0] - n:parts[0]]

            glog, elog = logits[:, :, 0:E_G], logits[:, :, E_G:RT]
            gmax, gexp, gsum, gcand, gleast, ghot = (scratch(n) for n in (1, E_G, 1, E_G, 1, E_G))
            esel, emax, cand, least, hot1, hot2, rest, top1, top2, share = (
                scratch(n) for n in (E_PER, 1, E_PER, 1, E_PER, E_PER, E_PER, 1, 1, 1))
            weigh, weigh2 = scratch(E_PER), scratch(E_PER)

            def wide(a, n):
                return a.broadcast_to([P, TT, n])

            with new_block() as block:
                @block.tensor
                def _(pe):
                    for t in range(TT):
                        for k in range(KD):
                            ins = pe.matmul(ps[:, 4, t * RT:(t + 1) * RT], hT[:, k, t * P:(t + 1) * P],
                                            P2(f"router_{l}")[:, k * RT:(k + 1) * RT], start=(k == 0), stop=(k == KD - 1))
                    tell(ins, to_dve)

                @block.scalar
                def _(act):
                    act.wait_ge(to_act.sem, to_act.base + 1)
                    tell(act.activation(gexp, gexp, ACT.Exp), to_dve)
                    act.wait_ge(to_act.sem, to_act.base + 2)
                    tell(act.activation(esel, esel, ACT.Exp), to_dve)

                @block.vector
                def _(dve):
                    done = InOrder(dve, dve_step)

                    def first_maximum(a, most, candidates, smallest, onehot, n):
                        done(dve.tensor_reduce(most, a, AX_X, ALU.max))
                        done(dve.tensor_tensor(candidates, a, wide(most, n), ALU.is_equal))
                        iota = C(f"iota{n}").unsqueeze(1).broadcast_to([P, TT, n])
                        done(dve.scalar_tensor_tensor(candidates, candidates, -64.0, iota, ALU.mult, ALU.add))
                        done(dve.tensor_reduce(smallest, candidates, AX_X, ALU.min))
                        done(dve.tensor_tensor(onehot, candidates, wide(smallest, n), ALU.is_equal))

                    dve.wait_ge(to_dve.sem, to_dve.base + 1)
                    done(dve.tensor_tensor(logits[:, :, :], ps[:, 4, 0:TT * RT].rearrange("p (t n) -> p t n", t=TT),
                                           P2(f"router_b{l}").unsqueeze(1).broadcast_to([P, TT, RT]), ALU.add))
                    done(dve.tensor_reduce(gmax, glog, AX_X, ALU.max))
                    tell(dve.tensor_tensor(gexp, glog, wide(gmax, E_G), ALU.subtract), to_act)
                    dve.wait_ge(to_dve.sem, to_dve.base + 2)
                    done(dve.tensor_reduce(gsum, gexp, AX_X, ALU.add))
                    first_maximum(gexp, gmax, gcand, gleast, ghot, E_G)
                    chosen = combine[:, :, :].rearrange("p t (g e) -> p t g e", g=E_G)
                    done(dve.tensor_tensor(chosen, elog.rearrange("p t (g e) -> p t g e", g=E_G),
                                           ghot.unsqueeze(3).broadcast_to([P, TT, E_G, E_PER]), ALU.mult))
                    done(dve.tensor_reduce(esel, chosen.rearrange("p t g e -> p t e g"), AX_X, ALU.add))
                    done(dve.tensor_reduce(emax, esel, AX_X, ALU.max))
                    tell(dve.tensor_tensor(esel, esel, wide(emax, E_PER), ALU.subtract), to_act)
                    dve.wait_ge(to_dve.sem, to_dve.base + 3)
                    first_maximum(esel, top1, cand, least, hot1, E_PER)
                    done(dve.scalar_tensor_tensor(rest, hot1, -2.0, esel, ALU.mult, ALU.add))
                    first_maximum(rest, top2, cand, least, hot2, E_PER)
                    done(dve.tensor_tensor(share, top1, top2, ALU.add))
                    done(dve.tensor_tensor(share, share, gsum, ALU.mult))
                    done(dve.reciprocal(share, share))
                    done(dve.tensor_tensor(share, share, gmax, ALU.mult))
                    dve.tensor_tensor(weigh, hot1, wide(top1, E_PER), ALU.mult)
                    done(dve.tensor_tensor(weigh2, hot2, wide(top2, E_PER), ALU.mult))
                    done(dve.tensor_tensor(weigh, weigh, weigh2, ALU.add))
                    done(dve.tensor_tensor(weigh, weigh, wide(share, E_PER), ALU.mult))
                    dve.tensor_tensor(chosen, ghot.unsqueeze(3).broadcast_to([P, TT, E_G, E_PER]),
                                      weigh.unsqueeze(2).broadcast_to([P, TT, E_G, E_PER]), ALU.mult)

        hidden_done, silu_done, column_ready, product_step, weighed, hidden_high = (
            signal(n) for n in ("hidden_done", "silu_done", "combine_columns_ready", "silu_times_up",
                                "hidden_weighed", "hidden_high"))
        hidh = sb("hidden_high_half", [P, 2, T], adaln, F32R)
        hidl = sb("hidden_low_half", [P, 2, T], adaln, F32R)

        def experts(l, last):
            assert ring.place % RING == 0
            turns, per, per_slot = E_N // 4, 12, 12 // RING
            first, loads = ring.place, list(ring.loads)
            unit0, high0, split0 = ring.unit_done.n, ring.high_done.n, ring.split.n
            hid0, silu0, col0, prod0 = hidden_done.n, silu_done.n, column_ready.n, product_step.n
            weighed0, hhigh0 = weighed.n, hidden_high.n
            up_unit = [6 * (j // 2) + 2 * (j % 2) for j in range(4)]
            down_unit = [6 * (j // 2) + 4 + j % 2 for j in range(4)]
            hidden = [sq[:, j, :] for j in range(2)]
            looped = turns - 1 if last else turns

            def more(i, k, ahead):
                return not isinstance(i, int) or first + i * per + k + ahead * RING < ring.limit

            with new_block() as block:
                @block.sync
                def _(sp):
                    def turn(i):
                        for k in range(per):
                            if more(i, k, 2):
                                sp.wait_ge(ring.split.sem, i * per + (split0 + k + 1))
                                ring.load(sp, i * per + (ring.base + first + k + 2 * RING), k % RING)

                    with sp.Fori(0, looped) as i:
                        turn(i)
                    if last:
                        turn(looped)

                @block.tensor
                def _(pe):
                    pe.wait_ge(column_ready.sem, col0 + 1)
                    for b in range(4):
                        pe.matmul(ps[:, 4 + b, :], ones, flat(sq[:, 4:6, :]), start=True, stop=True,
                                  skip_group_check=True)
                    with pe.Fori(0, turns) as i:
                        def halves(k):
                            pe.wait_ge(ring.split.sem, i * per + (split0 - RING + k + 1))
                            return high[:, k % RING, :], low[:, k % RING, :]

                        def up(j):
                            pe.wait_ge(hidden_done.sem, i * 4 + (hid0 + j + 1))
                            if j == 0:
                                pe.wait_ge(column_ready.sem, i + (col0 + 2))
                            for t in range(TT):
                                pe.matmul(ps[:, 2 + j % 2, t * P:(t + 1) * P],
                                          ccol[:, t, j:j + 1].broadcast_to([P, P]), ident, start=True, stop=True)
                            for m in range(2):
                                w = halves(up_unit[j] + m)
                                for k in range(KD):
                                    ins = three_products(pe, ps[:, j % 2, m * T:(m + 1) * T],
                                                         [a[:, k * P:(k + 1) * P] for a in w], (hh[:, k, :], hl[:, k, :]),
                                                         k == 0, k == KD - 1)
                                ins.then_inc(ring.unit_done.sem, 1)

                        def down(j):
                            w = halves(down_unit[j])
                            pe.wait_ge(hidden_done.sem, i * 4 + (hid0 + 2 + j + 1))
                            for m in range(KD):
                                ins = three_products(pe, ps[:, 4 + m // 2, m % 2 * T:(m % 2 + 1) * T],
                                                     [a[:, m * P:(m + 1) * P] for a in w],
                                                     (hidh[:, j % 2, :], hidl[:, j % 2, :]), False, False,
                                                     skip_group_check=True)
                            ins.then_inc(ring.unit_done.sem, 1)

                        for j in (0, 2):
                            up(j)
                            up(j + 1)
                            down(j)
                            down(j + 1)

                @block.scalar
                def _(act):
                    def turn(i):
                        def next_high(k):
                            if more(i, k, 1):
                                s = k % RING
                                act.wait_ge(ring.unit_done.sem, i * per + (unit0 + k + 1))
                                act.wait_ge(ring.raw_full[s], i * (16 * per_slot) + 16 * (loads[s] + k // RING + 1))
                                ring.round_high(act, s).then_inc(ring.high_done.sem, 1)

                        for j in range(4):
                            k = up_unit[j]
                            next_high(k)
                            act.wait_ge(ring.unit_done.sem, i * per + (unit0 + k + 2))
                            act.wait_ge(hidden_done.sem, i * 4 + (hid0 + j + 1))
                            act.activation(hidden[j % 2], ps[:, j % 2, 0:T], ACT.Silu).then_inc(silu_done.sem, 1)
                            next_high(k + 1)
                            act.wait_ge(weighed.sem, i * 4 + (weighed0 + j + 1))
                            act.wait_ge(ring.unit_done.sem, i * per + (unit0 + down_unit[j] - 5))
                            act.copy(hidh[:, j % 2, :], hidden[j % 2]).then_inc(hidden_high.sem, 1)
                            if j % 2:
                                next_high(down_unit[j] - 1)
                                next_high(down_unit[j])

                    with act.Fori(0, looped) as i:
                        turn(i)
                    if last:
                        turn(looped)

                @block.vector
                def _(dve):
                    dve.memset(sq[:, 4:6, :], 0.0).then_inc(column_ready.sem, 1)
                    dve.memset(small[:, 0, 0:1], 0.0).then_inc(hidden_done.sem, 1)
                    dve.memset(small[:, 0, 1:2], 0.0).then_inc(hidden_done.sem, 1)

                    def turn(i):
                        def next_low(k):
                            if more(i, k, 1):
                                dve.wait_ge(ring.high_done.sem, i * per + (high0 + k + 1))
                                ring.take_low(dve, k % RING).then_inc(ring.split.sem, 1)

                        dve.tensor_copy(ccol[:, :, :], combine[:, :, bass.ds(i * 4, 4)]).then_inc(column_ready.sem, 1)
                        for j in range(4):
                            next_low(up_unit[j])
                            dve.wait_ge(silu_done.sem, i * 4 + (silu0 + j + 1))
                            dve.tensor_tensor(hidden[j % 2], hidden[j % 2], ps[:, j % 2, T:2 * T], ALU.mult) \
                                .then_inc(product_step.sem, 1)
                            dve.wait_ge(product_step.sem, i * 4 + (prod0 + j + 1))
                            dve.tensor_tensor(hidden[j % 2], hidden[j % 2], ps[:, 2 + j % 2, 0:T], ALU.mult) \
                                .then_inc(weighed.sem, 1)
                            next_low(up_unit[j] + 1)
                            dve.wait_ge(hidden_high.sem, i * 4 + (hhigh0 + j + 1))
                            dve.tensor_tensor(hidl[:, j % 2, :], hidden[j % 2], hidh[:, j % 2, :].bitcast(F32),
                                              ALU.subtract).then_inc(hidden_done.sem, 1)
                            if j % 2:
                                next_low(down_unit[j] - 1)
                                next_low(down_unit[j])

                    with dve.Fori(0, looped) as i:
                        turn(i)
                    if last:
                        turn(looped)
                    dve.wait_ge(ring.unit_done.sem, unit0 + turns * per)
                    for m in range(KD):
                        dve.scalar_tensor_tensor(xT[:, m, :], ps[:, 4 + m // 2, m % 2 * T:(m % 2 + 1) * T],
                                                 gate(l, 1)[:, m:m + 1], xT[:, m, :], ALU.mult, ALU.add)
            for count, n in ((ring.unit_done, turns * per), (ring.split, turns * per), (ring.high_done, turns * per),
                             (hidden_done, 2 + E_N), (silu_done, E_N), (column_ready, 1 + turns),
                             (product_step, E_N), (weighed, E_N), (hidden_high, E_N)):
                count.n += n
            ring.place += turns * per
            ring.loads = [n + turns * per_slot for n in loads]

        def mamba():
            mb = ExitStack()
            z = sb("z", [P, KS, T], mb)
            inner = mb.enter_context(ExitStack())
            xbc = sb("xbc", [P, KX, T], inner)
            xdt = sb("xdt", [P, TT, SSM_IN], inner)
            cv = sb("cv", [P, 2, 2, T], inner)
            dt = sb("dt", [P, TT, SSM_H], inner)
            a = sb("a", [P, TT, SSM_H], inner)
            acs = sb("acs", [P, TT, SSM_H], inner)
            soft = sb("soft", [P, TT * SSM_H], inner)
            cbm = sb("cbm", [P, 2, 3 * P], inner)
            seg = sb("seg", [P, 4, 3 * P], inner)
            yt = sb("yt", [P, 2, T], inner)
            w = ring.claim(48)
            prod = Product(w, 0, KS + KX, KD, banks)
            conv_w = P2("conv_w").rearrange("p (i c) -> p i c", i=SSM_CONV)
            with new_block() as block:
                @block.sync
                def _(sp):
                    w.sync(sp)

                @block.tensor
                def _(pe):
                    for j in range(24):
                        prod.tensor(pe, h, j)

                @block.vector
                def _(dve):
                    done = InOrder(dve, dve_step)
                    for i in range(16):
                        w.vector(dve, i)
                    for j in range(KX // 2):
                        w.vector(dve, 16 + 2 * j)
                        acc = prod.wait(dve, 8 + j)
                        buf = cv[:, j % 2, :, :]
                        if j >= 2:
                            dve.wait_ge(to_dve.sem, to_dve.base + j - 1)
                        for m in range(2):
                            ins = dve.tensor_scalar(buf[:, m, :], acc[:, m * T:(m + 1) * T],
                                                    conv_w[:, SSM_CONV - 1, 2 * j + m:2 * j + m + 1], None, ALU.mult)
                        for s in range(1, SSM_CONV):
                            done(ins)
                            for m in range(2):
                                ins = dve.scalar_tensor_tensor(
                                    buf[:, m, s:T], acc[:, m * T:(m + 1) * T - s],
                                    conv_w[:, SSM_CONV - 1 - s, 2 * j + m:2 * j + m + 1], buf[:, m, s:T],
                                    ALU.mult, ALU.add)
                        ins.then_inc(prod.read(8 + j), 1)
                        w.vector(dve, 17 + 2 * j)

                @block.scalar
                def _(act):
                    for j in range(8):
                        w.scalar(act, 2 * j)
                        acc = prod.wait(act, j)
                        act.activation(flat(z[:, 2 * j:2 * j + 2, :]), acc, ACT.Silu).then_inc(prod.read(j), 1)
                        w.scalar(act, 2 * j + 1)
                    for j in range(KX // 2):
                        w.scalar(act, 16 + 2 * j)
                        w.scalar(act, 17 + 2 * j)
                        prod.after_read(act, 8 + j)
                        for m in range(2):
                            c = 2 * j + m
                            ins = act.activation(xbc[:, c, :], cv[:, j % 2, m, :], ACT.Silu,
                                                 bias=P2("conv_b")[:, c:c + 1])
                        tell(ins, to_dve)

            with new_block() as block:
                @block.tensor
                def _(pe):
                    for t in range(TT):
                        for k in range(KD):
                            ins = pe.matmul(ps[:, 4, t * SSM_H:(t + 1) * SSM_H], hT[:, k, t * P:(t + 1) * P],
                                            P2("w_dt")[:, k * SSM_H:(k + 1) * SSM_H], start=(k == 0), stop=(k == KD - 1))
                    tell(ins, to_dve)
                    pe.wait_ge(to_pe.sem, to_pe.base + 1)
                    pe.matmul(ps[:, 5, 0:SSM_H], C("upper", 0, P), a[:, 0, :], start=True, stop=True)
                    pe.matmul(ps[:, 5, SSM_H:2 * SSM_H], ones, a[:, 0, :], start=True, stop=False)
                    ins = pe.matmul(ps[:, 5, SSM_H:2 * SSM_H], C("upper", 0, P), a[:, 1, :], start=False, stop=True)
                    tell(ins, to_dve)

                @block.scalar
                def _(act):
                    log_sigmoid_tail(act, soft[:, :], (to_act.sem, to_act.base + 1), to_dve2)
                    tell(act.activation(acs[:, 0, :], P2("a_log"), ACT.Exp), to_dve2)

                @block.vector
                def _(dve):
                    done = InOrder(dve, dve_step)
                    dve.wait_ge(to_dve.sem, to_dve.base + 1)
                    for t in range(TT):
                        ins = dve.tensor_tensor(dt[:, t, :], ps[:, 4, t * SSM_H:(t + 1) * SSM_H], P2("dt_b"), ALU.add)
                    done(ins)
                    tell(dve.tensor_copy(soft[:, :], flat(dt[:, :, :])), to_act)
                    dve.wait_ge(to_dve2.sem, to_dve2.base + 2)
                    done(dve.scalar_tensor_tensor(flat(dt[:, :, :]), flat(dt[:, :, :]), 0.0, soft[:, :], ALU.max, ALU.add))
                    for t in range(TT):
                        ins = dve.scalar_tensor_tensor(a[:, t, :], dt[:, t, :], -1.0, acs[:, 0, :], ALU.mult, ALU.mult)
                    tell(ins, to_pe)
                    dve.wait_ge(to_dve.sem, to_dve.base + 2)
                    dve.tensor_copy(flat(acs[:, :, :]), ps[:, 5, 0:2 * SSM_H])

            rounds = [(c4, t) for c4 in range(KS // 4) for t in range(TT)]
            with new_block() as block:
                @block.tensor
                def _(pe):
                    for n, (c4, t) in enumerate(rounds):
                        if n >= 4:
                            pe.wait_ge(to_pe.sem, to_pe.base + n - 3)
                        for m in range(4):
                            ins = pe.transpose(ps[:, 4 + n % 4, m * P:(m + 1) * P],
                                               xbc[:, 4 * c4 + m, t * P:(t + 1) * P], ident)
                        tell(ins, to_dve)

                @block.vector
                def _(dve):
                    for n, (c4, t) in enumerate(rounds):
                        dve.wait_ge(to_dve.sem, to_dve.base + n + 1)
                        heads = BANK // SSM_P
                        tell(dve.tensor_tensor(
                            xdt[:, t, c4 * BANK:(c4 + 1) * BANK].rearrange("p (h n) -> p h n", n=SSM_P),
                            ps[:, 4 + n % 4, :].rearrange("p (h n) -> p h n", n=SSM_P),
                            dt[:, t, c4 * heads:(c4 + 1) * heads].unsqueeze(2).broadcast_to([P, heads, SSM_P]),
                            ALU.mult), to_pe)

            per = SSM_H // SSM_G
            cb_done, cb_read, bc_done, seg_ready, exp_done, m_ready, y_done, y_read = (
                pt_done, pt_ready, score_done, to_act, to_dve, prob_ready, pv_done, to_pe2)
            with new_block() as block:
                @block.tensor
                def _(pe):
                    def group(g):
                        if g >= 2:
                            pe.wait_ge(cb_read.sem, cb_read.base + g - 1)
                        B, Cm = xbc[:, KS + g, :], xbc[:, KS + SSM_G + g, :]
                        pe.matmul(ps[:, 4 + g % 2, 0:T], B[:, 0:P], Cm, start=True, stop=True)
                        tell(pe.matmul(ps[:, 4 + g % 2, T:T + P], B[:, P:T], Cm[:, P:T], start=True, stop=True), cb_done)

                    def running_sum(h):
                        if h >= 2:
                            pe.wait_ge(seg_ready.sem, seg_ready.base + h - 1)
                        o = ps[:, 6 + h % 2, :]
                        pe.matmul(o[:, 0:T], a[:, 0, h:h + 1].broadcast_to([P, P]), C("upper"), start=True, stop=False)
                        tell(pe.matmul(o[:, P:T], a[:, 1, h:h + 1].broadcast_to([P, P]), C("upper", 0, P), start=False,
                                       stop=True), bc_done)

                    def outputs(h):
                        ct, lo = h // 2, h % 2 * SSM_P
                        if ct >= 4 and h % 2 == 0:
                            pe.wait_ge(y_read.sem, y_read.base + ct - 3)
                        pe.wait_ge(m_ready.sem, m_ready.base + h + 1)
                        o = ps[lo:lo + SSM_P, ct % 4, 0:T]
                        cols = slice(h * SSM_P, (h + 1) * SSM_P)
                        pe.matmul(o, xdt[:, 0, cols], seg[:, h % 4, 0:T], start=True, stop=False)
                        tell(pe.matmul(o[:, P:T], xdt[:, 1, cols], seg[:, h % 4, T:T + P], start=False, stop=True), y_done)

                    group(0)
                    running_sum(0)
                    running_sum(1)
                    for h in range(SSM_H):
                        if h + 2 < SSM_H:
                            if (h + 2) % per == 0:
                                group((h + 2) // per)
                            running_sum(h + 2)
                        outputs(h)

                @block.vector
                def _(dve):
                    done = InOrder(dve, dve_step)

                    def exponents(h):
                        g = h // per
                        if h % per == 0:
                            dve.wait_ge(cb_done.sem, cb_done.base + g + 1)
                            if g >= 2:
                                dve.wait_ge(m_ready.sem, m_ready.base + per * (g - 1))
                            tell(dve.tensor_tensor(cbm[:, g % 2, :], ps[:, 4 + g % 2, 0:3 * P], C("ssd"), ALU.mult),
                                 cb_read)
                        dve.wait_ge(bc_done.sem, bc_done.base + h + 1)
                        if h >= 4:
                            dve.wait_ge(y_done.sem, y_done.base + h - 3)
                        o = ps[:, 6 + h % 2, :]
                        dve.tensor_scalar(seg[:, h % 4, 0:T], o[:, 0:T], acs[:, 0, h:h + 1], 0.0, ALU.subtract, ALU.min)
                        tell(dve.tensor_scalar(seg[:, h % 4, T:T + P], o[:, P:T], acs[:, 1, h:h + 1], 0.0, ALU.subtract,
                                               ALU.min), seg_ready)

                    def gated(ct):
                        dve.wait_ge(y_done.sem, y_done.base + 2 * ct + 2)
                        tell(dve.scalar_tensor_tensor(yt[:, ct % 2, :], xbc[:, ct, :], P2("d_skip")[:, ct:ct + 1],
                                                      ps[:, ct % 4, 0:T], ALU.mult, ALU.add), y_read)
                        dve.wait_ge(y_read.sem, y_read.base + ct + 1)
                        done(dve.tensor_tensor(z[:, ct, :], z[:, ct, :], yt[:, ct % 2, :], ALU.mult))

                    exponents(0)
                    for h in range(SSM_H):
                        if h + 1 < SSM_H:
                            exponents(h + 1)
                        dve.wait_ge(exp_done.sem, exp_done.base + h + 1)
                        if h % per == 0:
                            dve.wait_ge(cb_read.sem, cb_read.base + h // per + 1)
                        tell(dve.tensor_tensor(seg[:, h % 4, :], seg[:, h % 4, :], cbm[:, h // per % 2, :], ALU.mult), m_ready)
                        if h % 2 and h >= 3:
                            gated(h // 2 - 1)
                    gated(KS - 1)

                @block.scalar
                def _(act):
                    for h in range(SSM_H):
                        act.wait_ge(seg_ready.sem, seg_ready.base + h + 1)
                        tell(act.activation(seg[:, h % 4, :], seg[:, h % 4, :], ACT.Exp), exp_done)

            sqz = xdt[:, :, :].rearrange("p a b -> p (a b)")
            var = flat(xbc[:, 0:SSM_G, :])
            with new_block() as block:
                @block.scalar
                def _(act):
                    for c in range(4):
                        tell(act.activation(sqz[:, c * 4 * T:(c + 1) * 4 * T], flat(z[:, 4 * c:4 * c + 4, :]), ACT.Square),
                             squares)
                    act.wait_ge(variance.sem, variance.base + 1)
                    tell(act.activation(var, var, ACT.Sqrt), deviation)

                @block.tensor
                def _(pe):
                    for g in range(SSM_G):
                        if g % 2 == 0:
                            pe.wait_ge(squares.sem, squares.base + g // 2 + 1)
                        for m in range(2):
                            ins = pe.matmul(ps[:, 4 + g // 2, g % 2 * T:(g % 2 + 1) * T], ones,
                                            sqz[:, (2 * g + m) * T:(2 * g + m + 1) * T], start=(m == 0), stop=(m == 1))
                    tell(ins, summed)

                @block.vector
                def _(dve):
                    done = InOrder(dve, dve_step)
                    dve.wait_ge(summed.sem, summed.base + 1)
                    for b in range(4):
                        ins = dve.tensor_scalar(var[:, b * BANK:(b + 1) * BANK], ps[:, 4 + b, :], 1.0 / (2 * P), EPS,
                                                ALU.mult, ALU.add)
                    tell(ins, variance)
                    dve.wait_ge(deviation.sem, deviation.base + 1)
                    done(dve.reciprocal(var, var))
                    for c in range(KS):
                        dve.scalar_tensor_tensor(z[:, c, :], z[:, c, :], P2("ssm_norm")[:, c:c + 1],
                                                 var[:, c // 2 * T:(c // 2 + 1) * T], ALU.mult, ALU.mult)
            inner.close()
            zh = sb("z_high", [P, KS, T], mb, F32R)
            zl = sb("z_low", [P, KS, T], mb, F32R)
            with new_block() as block:
                @block.scalar
                def _(act):
                    for c in range(4):
                        tell(act.copy(zh[:, 4 * c:4 * c + 4, :], z[:, 4 * c:4 * c + 4, :]), to_dve)

                @block.vector
                def _(dve):
                    for c in range(4):
                        dve.wait_ge(to_dve.sem, to_dve.base + c + 1)
                        dve.tensor_tensor(zl[:, 4 * c:4 * c + 4, :], z[:, 4 * c:4 * c + 4, :],
                                          zh[:, 4 * c:4 * c + 4, :].bitcast(F32), ALU.subtract)
            residual_product(16, KS, (zh, zl), gate(1, 0))
            mb.close()

        modulated_gains()
        rms_norm(mgain[:, 0, :], shift(0, 0))
        pool_and_chunk_attention()
        rms_norm(mgain[:, 1, :], shift(0, 1), out=hT)
        router(0)
        experts(0, False)
        rms_norm(mgain[:, 2, :], shift(1, 0), out=hT)
        mamba()
        rms_norm(mgain[:, 3, :], shift(1, 1), out=hT)
        router(1)
        experts(1, True)
        rms_norm(P2("final"), out=xT)
        with new_block() as block:
            @block.sync
            def _(sp):
                sp.dma_start(out, xT[:, :, :]).then_inc(stored, 16)
                sp.wait_ge(stored, 16)




def kernel(x, norm1_g, w_in, hg_lb, hg_norm_g, gla_w2, gla_b, gla_norm_g, cmp_pos_k, cmp_pos_v,
           cmp_w1_k, cmp_w2_k, cmp_w1_v, cmp_w2_v, w_br_hg, w_br_gla, w_br_nsa, w_out, norm2_g,
           w_ffn_gate, w_ffn_up, w_ffn_down, final_norm_g, c_2, ada_w_2, ada_b_2, norm1_w_2, norm2_w_2,
           mix_w_in_2, pool_w_2, pool_scale_2, rel_bias_2, mix_w_out_2, ssm_w_in_2, ssm_conv_w_2,
           ssm_conv_b_2, ssm_dt_bias_2, ssm_A_log_2, ssm_D_2, ssm_norm_w_2, ssm_w_out_2, moe_w_group_2,
           moe_b_group_2, moe_w_expert_2, moe_b_expert_2, moe_w1_2, moe_w3_2, moe_w2_2, final_norm_w_2):
    import concourse.bacc as bacc
    from concourse.bass_utils import run_bass_kernel_spmd

    A = np.asarray
    fc = lambda v: feature_columns(A(v))
    units = []
    for l in range(DEPTH):
        units += stream_hybrid(*(A(w[l]) for w in (w_in, cmp_w1_k, cmp_w1_v, w_br_hg, w_br_gla, w_br_nsa, w_out,
                                                   w_ffn_gate, w_ffn_up, w_ffn_down)))
    feature = lambda w: units_of(weight_blocks(A(w)))
    mix = A(mix_w_in_2[0])
    ssm = A(ssm_w_in_2[0])
    units += [feature(mix), feature(mix_w_out_2[0]), moe_units(A(moe_w1_2[0]), A(moe_w3_2[0]), A(moe_w2_2[0])),
              feature(ssm[:, :SSM_IN + KX * P]), feature(ssm_w_out_2[0]),
              moe_units(A(moe_w1_2[1]), A(moe_w3_2[1]), A(moe_w2_2[1]))]
    stream = np.concatenate(units)

    def pos(v):
        return A(v).reshape(-1, 2, NSA_DH).transpose(1, 2, 0).reshape(P, -1)

    par1 = np.stack([pack(PAR1, N_PAR1, {
        "norm1": fc(norm1_g[l]), "norm2": fc(norm2_g[l]), "hg_norm": fc(hg_norm_g[l]), "gla_norm": fc(gla_norm_g[l]),
        "gla_b": fc(gla_b[l]), "gla_w2": A(gla_w2[l]), "pos_k": pos(cmp_pos_k[l]), "pos_v": pos(cmp_pos_v[l]),
        "w2_k": np.concatenate([A(cmp_w2_k[l])] * 2, 1), "w2_v": A(cmp_w2_v[l])}) for l in range(DEPTH)])

    def k_major(w):
        return w.reshape(KD, P, -1).transpose(1, 0, 2)

    def router(l):
        return k_major(np.concatenate([A(moe_w_group_2[l]), A(moe_w_expert_2[l]).reshape(D, E_N)], 1))

    def router_bias(l):
        return rows(np.concatenate([A(moe_b_group_2[l]), A(moe_b_expert_2[l]).reshape(-1)]))

    par2 = pack(PAR2, N_PAR2, {
        "norm1_0": fc(norm1_w_2[0]), "norm1_1": fc(norm1_w_2[1]), "norm2_0": fc(norm2_w_2[0]),
        "norm2_1": fc(norm2_w_2[1]), "final": fc(final_norm_w_2), "final_1": fc(final_norm_g),
        "ada_b0": fc(ada_b_2[0]), "ada_b1": fc(ada_b_2[1]), "pool_w": A(pool_w_2[0]).transpose(1, 0, 2),
        "pool_scale": fc(pool_scale_2[0]), "conv_w": np.stack([fc(ssm_conv_w_2[0][i]) for i in range(SSM_CONV)], 1),
        "conv_b": fc(ssm_conv_b_2[0]), "dt_b": rows(A(ssm_dt_bias_2[0])), "a_log": rows(A(ssm_A_log_2[0])),
        "d_skip": fc(np.repeat(A(ssm_D_2[0]), SSM_P)), "ssm_norm": fc(ssm_norm_w_2[0]),
        "w_dt": k_major(ssm[:, SSM_IN + KX * P:]), "router_0": router(0), "router_1": router(1),
        "router_b0": router_bias(0), "router_b1": router_bias(1)})
    arrays = {"stream": stream, "const": constants(), "par1": par1, "par2": par2,
              "lb": np.concatenate([fc(hg_lb[l]) for l in range(DEPTH)], 1), "bias": A(rel_bias_2[0]), "c": rows(A(c_2)),
              "ada": np.concatenate([A(ada_w_2[l]).T.reshape(-1, P, D) for l in range(2)]),
              "xT": A(x)[0].T.reshape(KD, P, T).transpose(1, 0, 2)}
    nc = bacc.Bacc("TRN2", target_bir_lowering=False, num_devices=1)
    arrays = {f"in_{n}": np.ascontiguousarray(a) for n, a in arrays.items()}
    aps = {n: nc.dram_tensor(n, a.shape, mybir.dt.from_np(a.dtype), kind="ExternalInput").ap()
           for n, a in arrays.items()}
    out = nc.dram_tensor("out", (P, KD, T), F32, kind="ExternalOutput").ap()
    hybrid_and_moe(nc, aps["in_stream"], aps["in_const"], aps["in_par1"], aps["in_lb"], aps["in_par2"], aps["in_ada"], aps["in_c"], aps["in_bias"],
                   aps["in_xT"], out)
    r = run_bass_kernel_spmd(nc, [arrays], core_ids=[0])
    return np.ascontiguousarray(r.results[0]["out"].transpose(2, 1, 0).reshape(1, T, D))
```

```python
from contextlib import ExitStack

import numpy as np

import concourse.bass as bass
from concourse import mybir

ALU = mybir.AluOpType
ACT = mybir.ActivationFunctionType
F32 = mybir.dt.float32
U32 = mybir.dt.uint32
AX_X = mybir.AxisListType.X

P = 128
T = 256
TT = T // P
D = 1024
KD = D // P
DEPTH = 2
EPS = 1e-6
NEG = -1e30
F32R = mybir.dt.float32r
BLOCKS = 8
UNIT = BLOCKS * P
RING = 4
BANK = 512

HG_H, HG_D = 4, 128
GLA_H, GLA_DK, GLA_DV, GLA_RANK = 4, 64, 128, 16
GLA_TAU = 16.0
NSA_H, NSA_G, NSA_DH = 8, 2, 64
CMP_STRIDE, CMP_BLK, CMP_HID = 16, 32, 128
NCMP = T // CMP_STRIDE - 1
ROT = NSA_DH // 4
THETA = 500000.0
N_BR = 3
FF = 2816
KF = FF // P
LEVELS = 7

CHUNK = 64
POOL_WINDOWS = (2, 4, 8, 16)
ATT_H, ATT_DH = 8, 64
REL = 256
SSM_IN = 2048
KS = SSM_IN // P
SSM_H, SSM_P, SSM_G, SSM_N, SSM_CONV = 32, 64, 8, 128, 4
KX = (SSM_IN + 2 * SSM_G * SSM_N) // P
E_G, E_PER = 4, 8
E_N = E_G * E_PER
RT = E_G + E_N



def columns(spec):
    at, out = 0, {}
    for name, n in spec:
        out[name] = (at, n)
        at += n
    return out, at


CONST, N_CONST = columns([
    ("ident", P), ("ones", P), ("upper", P + P), ("rot", P), ("cos", T), ("sin", T),
    ("causal_neg", 3 * P), ("chunk_neg", P), ("cmp_neg", TT * 32), ("cmp_keep", TT * 32), ("ssd", 3 * P),
    ("count", 4 * 16), ("iota4", 4), ("iota8", 8), ("one_hot", 64), ("level", LEVELS * P),
])
PAR1, N_PAR1 = columns([
    ("norm1", KD), ("norm2", KD), ("hg_norm", HG_H), ("gla_norm", GLA_H), ("gla_b", 2), ("gla_w2", 2 * P),
    ("pos_k", 16), ("pos_v", 16), ("w2_k", P), ("w2_v", NSA_DH),
])
PAR2, N_PAR2 = columns([
    ("norm1_0", KD), ("norm1_1", KD), ("norm2_0", KD), ("norm2_1", KD), ("final", KD), ("final_1", KD),
    ("ada_b0", 48), ("ada_b1", 48), ("pool_w", 4 * P), ("pool_scale", 4), ("conv_w", SSM_CONV * KX),
    ("conv_b", KX), ("dt_b", SSM_H), ("a_log", SSM_H), ("d_skip", KS), ("ssm_norm", KS), ("w_dt", KD * SSM_H),
    ("router_0", KD * RT), ("router_1", KD * RT), ("router_b0", RT), ("router_b1", RT),
])

IN_AT = {}
_at = 0
for _n, _w in (("hq", 512), ("hf", 512), ("hi", 512), ("hog", 512), ("gq", 256), ("gk", 256), ("gv", 512),
               ("glr", 16), ("gog", 512), ("nq", 512), ("nkc", 128), ("nvc", 128), ("nks", 128), ("nvs", 128),
               ("nkw", 128), ("nvw", 128), ("ngate", 24), ("mgate", 3072)):
    IN_AT[_n] = (_at, _w)
    _at += _w
IN_COLS = _at

UNITS1 = [("hf", 4), ("hq", 4), ("hi", 4), ("hog", 4), ("gq", 2), ("gk", 2), ("gv", 4), ("misc", 1), ("gog", 4),
          ("nkc", 2), ("nvc", 2), ("nks", 2), ("nkw", 2), ("nq", 4), ("nvsw", 2), ("mix0", 9), ("w1k", 2),
          ("w1v", 2), ("mix", 27), ("w_out", 8), ("ffn_gu", 44), ("ffn_d", 22), ("filler", 3)]
N_U1 = sum(n for _, n in UNITS1)
assert N_U1 % RING == 0
UNITS2 = [("mix_in", 16), ("mix_out", 8), ("moe0", 97), ("ssm_in", 48), ("ssm_out", 16), ("moe1", 97)]
N_U2 = sum(n for _, n in UNITS2)
N_UNITS = DEPTH * N_U1 + N_U2


def weight_blocks(w):
    k, n = w.shape
    return w.reshape(k // P, P, n // P, P).transpose(2, 0, 1, 3).reshape(-1, P, P)


def units_of(blocks):
    n = len(blocks) // BLOCKS
    return blocks.reshape(n, BLOCKS, P, P).transpose(0, 2, 1, 3).reshape(n, P, UNIT)


def token_major_units(w):
    k, n = w.shape
    return w.reshape(-1, 4, P, n // (2 * P), 2 * P).transpose(3, 0, 2, 1, 4).reshape(-1, P, UNIT)


def feature_columns(v):
    return v.reshape(-1, P).T


def rows(v):
    return np.broadcast_to(v.reshape(1, -1), (P, v.size))


def pack(spec, total, parts, dtype=np.float32):
    out = np.zeros((P, total), dtype)
    for name, a in parts.items():
        at, n = spec[name]
        a = a.reshape(a.shape[0], -1)
        assert a.shape[1] == n, (name, a.shape, n)
        out[:a.shape[0], at:at + n] = a
    return out


def stream_hybrid(w_in, w1k, w1v, br_hg, br_gla, br_nsa, w_out, wg, wu, wd):
    def cols(name):
        at, n = IN_AT[name]
        return w_in[:, at:at + n]

    def twice(name):
        w = cols(name).reshape(D, NSA_G, 1, NSA_DH)
        return np.concatenate([w, w], axis=2).reshape(D, 2 * P)

    feature = lambda w: units_of(weight_blocks(w))
    misc = np.zeros((D, P), w_in.dtype)
    misc[:, 0:GLA_RANK] = cols("glr")
    misc[:, 32:32 + 24] = cols("ngate")
    gu = np.concatenate([wg.reshape(D, -1, 2 * P), wu.reshape(D, -1, 2 * P)], axis=2).reshape(D, 2 * FF)
    mgate, mix = feature(cols("mgate")), []
    for b, w in enumerate((br_hg, br_gla, br_nsa)):
        branch = feature(w)
        for j in range(KD // 2):
            mix += [mgate[8 * b + 2 * j:8 * b + 2 * j + 2], branch[j:j + 1]]
    mix = np.concatenate(mix)
    parts = {n: feature(cols(n)) for n in ("hf", "hq", "gq", "gk", "nq", "hog", "gog")}
    parts.update({n: feature(twice(n)) for n in ("nkc", "nvc", "nks", "nkw")})
    parts.update({
        "hi": token_major_units(cols("hi")), "gv": token_major_units(cols("gv")),
        "misc": feature(misc), "nvsw": token_major_units(np.concatenate([cols("nvs"), cols("nvw")], axis=1)),
        "w1k": units_of(w1k.reshape(-1, P, CMP_HID)), "w1v": units_of(w1v.reshape(-1, P, CMP_HID)),
        "mix0": mix[:9], "mix": mix[9:], "w_out": feature(w_out), "ffn_gu": feature(gu), "ffn_d": feature(wd),
        "filler": np.zeros((3, P, UNIT), w_in.dtype)})
    for name, n in UNITS1:
        assert len(parts[name]) == n, (name, len(parts[name]))
    return [parts[name] for name, n in UNITS1]


def moe_units(w1, w3, w2):
    before, out = np.zeros((1, P, UNIT), w2.dtype), []
    for e in range(E_N):
        out += [units_of(weight_blocks(w1[e])), units_of(weight_blocks(w3[e])), before]
        before = w2[e:e + 1]
    return np.concatenate(out + [before])


def constants():
    i = np.arange(P)
    t = np.arange(T)
    s_, t_ = i[:, None], i[None, :]
    upper = (s_ <= t_).astype(np.float32)
    ones = np.ones((P, P), np.float32)
    zeros = np.zeros((P, P), np.float32)
    rot = np.zeros((P, P), np.float32)
    half = ROT // 2
    for base in (0, NSA_DH):
        for j in range(half):
            rot[base + half + j, base + j] = 1.0
            rot[base + j, base + half + j] = 1.0
    inv = np.float32(THETA) ** (-np.arange(0, ROT, 2, dtype=np.float32) / np.float32(ROT))
    ang = np.arange(T, dtype=np.float32)[:, None] * inv.astype(np.float32)[None, :]
    cos, sin = np.cos(ang).T, np.sin(ang).T
    c = np.ones((P, T), np.float32)
    s = np.zeros((P, T), np.float32)
    for base in (0, NSA_DH):
        c[base:base + half], c[base + half:base + ROT] = cos, cos
        s[base:base + half], s[base + half:base + ROT] = -sin, sin
    n = np.arange(32)
    tok = i[:, None, None] + P * np.arange(TT)[None, :, None]
    keep = ((n * CMP_STRIDE + CMP_BLK - 1)[None, None, :] <= tok) & (n < NCMP)[None, None, :]
    count = np.stack([w / np.minimum(np.arange(16) + 1, w) for w in POOL_WINDOWS]).astype(np.float32)
    causal = np.where(t_ <= s_, 0.0, NEG).astype(np.float32)
    level = []
    for lv in range(LEVELS):
        m = 1 << lv
        level.append((s_ // (2 * m) == t_ // (2 * m)) & (s_ // m % 2 == 0) & (t_ // m % 2 == 1))
    return pack(CONST, N_CONST, {
        "ident": np.eye(P, dtype=np.float32), "ones": ones, "upper": np.concatenate([upper, ones], 1),
        "rot": rot, "cos": c, "sin": s,
        "causal_neg": np.concatenate([causal, zeros, causal], 1),
        "chunk_neg": np.where(t_ // CHUNK <= s_ // CHUNK, 0.0, NEG).astype(np.float32),
        "cmp_neg": np.where(keep, 0.0, NEG).astype(np.float32), "cmp_keep": keep.astype(np.float32),
        "ssd": np.concatenate([upper, ones, upper], 1), "count": rows(count), "iota4": rows(np.arange(4.0)),
        "iota8": rows(np.arange(8.0)), "one_hot": rows(np.eye(8)), "level": np.concatenate(level, 1).astype(np.float32),
    })




class Count:

    def __init__(self, sem):
        self.sem, self.n, self.base = sem, 0, 0

    def one(self):
        self.n += 1
        return 1


class InOrder:

    def __init__(self, eng, count):
        self.eng, self.count = eng, count

    def __call__(self, ins):
        ins.then_inc(self.count.sem, self.count.one())
        self.eng.wait_ge(self.count.sem, self.count.n)


class Ring:

    def __init__(self, dram, raw, high, low, raw_full, unit_done, high_done, split):
        self.dram, self.raw, self.high, self.low, self.raw_full = dram, raw, high, low, raw_full
        self.unit_done, self.high_done, self.split = unit_done, high_done, split
        self.place, self.loads, self.base, self.limit = 0, [0] * RING, 0, None

    def load(self, sp, index, slot):
        src = self.dram[index, :, :] if isinstance(index, int) else \
            self.dram[bass.ds(index, 1), :, :].rearrange("o p n -> p (o n)")
        sp.dma_start(self.raw[:, slot, :], src).then_inc(self.raw_full[slot], 16)

    def round_high(self, act, slot):
        return act.copy(self.high[:, slot, :], self.raw[:, slot, :])

    def take_low(self, dve, slot):
        return dve.tensor_tensor(self.low[:, slot, :], self.raw[:, slot, :], self.high[:, slot, :].bitcast(F32),
                                 ALU.subtract)

    def claim(self, n):
        return Units(self, n)


class Units:

    def __init__(self, ring, n):
        self.ring, self.first, self.n = ring, ring.place, n
        self.done0, self.split0, self.high0 = ring.unit_done.n, ring.split.n, ring.high_done.n
        self.turn = []
        for i in range(n):
            s = (self.first + i) % RING
            ring.loads[s] += 1
            self.turn.append(ring.loads[s])
        self.more = [ring.limit is None or self.first + i + RING < ring.limit for i in range(n)]
        self.load_more = [ring.limit is None or self.first + i + 2 * RING < ring.limit for i in range(n)]
        ring.place += n
        ring.unit_done.n += n
        ring.split.n += n
        ring.high_done.n += n

    def done(self, i):
        return self.ring.unit_done.sem, self.done0 + i + 1

    def arrived(self, pe, i):
        pe.wait_ge(self.ring.split.sem, self.split0 - RING + i + 1)
        return self.halves(i)

    def halves(self, i):
        s = (self.first + i) % RING
        return self.ring.high[:, s, :], self.ring.low[:, s, :]

    def scalar(self, act, i):
        if self.more[i]:
            s = (self.first + i) % RING
            act.wait_ge(*self.done(i))
            act.wait_ge(self.ring.raw_full[s], 16 * self.turn[i])
            self.ring.round_high(act, s).then_inc(self.ring.high_done.sem, 1)

    def vector(self, dve, i):
        if self.more[i]:
            dve.wait_ge(self.ring.high_done.sem, self.high0 + i + 1)
            self.ring.take_low(dve, (self.first + i) % RING).then_inc(self.ring.split.sem, 1)

    def sync(self, sp, which=None):
        for i in range(self.n) if which is None else which:
            if self.load_more[i]:
                sp.wait_ge(self.ring.split.sem, self.split0 + i + 1)
                self.ring.load(sp, self.ring.base + (self.first + i + 2 * RING), (self.first + i) % RING)


def three_products(pe, out, stationary, moving, start, stop, **more):
    (sh, sl), (mh, ml) = stationary, moving
    pe.matmul(out, sh, mh, start=start, stop=False, **more)
    pe.matmul(out, sl, mh, start=False, stop=False, **more)
    return pe.matmul(out, sh, ml, start=False, stop=stop, **more)


class Product:

    def __init__(self, units, block0, tiles, kt, banks, token_major=False):
        self.units, self.block0, self.kt, self.banks, self.token_major = units, block0, kt, banks, token_major
        self.pairs = []
        for j in range((tiles + 1) // 2):
            last = block0 + min(2 * (j + 1), tiles) * kt - 1
            if last % BLOCKS == BLOCKS - 1:
                done = units.done(last // BLOCKS)
            else:
                banks.done.n += 1
                done = (banks.done.sem, banks.done.n)
            b = banks.take()
            self.pairs.append((b, banks.reads[b] - 1, done, min(2, tiles - 2 * j)))

    def units_of(self, j):
        lo = self.block0 + 2 * j * self.kt
        hi = lo + self.pairs[j][3] * self.kt
        return range(lo // BLOCKS, hi // BLOCKS)

    def psum(self, j):
        return self.banks.ps[:, self.banks.first + self.pairs[j][0], :]

    def wait(self, eng, j):
        eng.wait_ge(*self.pairs[j][2])
        return self.psum(j)

    def read(self, j):
        return self.banks.read[self.pairs[j][0]]

    def after_read(self, eng, j):
        eng.wait_ge(self.read(j), self.pairs[j][1] + 1)

    def tensor(self, pe, x, j, only=None):
        b, before, done, tiles = self.pairs[j]
        if before and not only:
            pe.wait_ge(self.banks.read[b], before)
        blk = self.block0 + 2 * j * self.kt
        xh, xl = x
        for m in range(tiles):
            if only is not None and m != only:
                blk += self.kt
                continue
            if self.token_major:
                for k in range(self.kt):
                    i = blk // BLOCKS + k // 4
                    if m == 0 and k % 4 == 0:
                        self.units.arrived(pe, i)
                    at = k % 4 * 2 * P
                    ins = three_products(pe, self.banks.ps[:, self.banks.first + b, m * T:(m + 1) * T],
                                         (xh[:, k, m * P:(m + 1) * P], xl[:, k, m * P:(m + 1) * P]),
                                         [a[:, at:at + 2 * P] for a in self.units.halves(i)], k == 0, k == self.kt - 1)
                    if m == 1 and k % 4 == 3:
                        ins.then_inc(self.units.ring.unit_done.sem, 1)
                continue
            for k in range(self.kt):
                if blk % BLOCKS == 0 or (m == 0 and k == 0):
                    high, low = self.units.arrived(pe, blk // BLOCKS)
                at = blk % BLOCKS * P
                ins = three_products(pe, self.banks.ps[:, self.banks.first + b, m * T:(m + 1) * T], (high[:, at:at + P], low[:, at:at + P]),
                                     (xh[:, k, :], xl[:, k, :]), k == 0, k == self.kt - 1)
                if blk % BLOCKS == BLOCKS - 1:
                    ins.then_inc(self.units.ring.unit_done.sem, 1)
                elif m == tiles - 1 and k == self.kt - 1:
                    ins.then_inc(self.banks.done.sem, 1)
                blk += 1


class Banks:

    def __init__(self, ps, read, done, first, n):
        self.ps, self.read, self.done, self.first, self.n = ps, read, done, first, n
        self.reads, self.turn = [0] * n, 0

    def take(self):
        b = self.turn
        self.turn = (b + 1) % self.n
        self.reads[b] += 1
        return b




def hybrid_and_moe(nc, stream, const_in, par1_in, lb_in, par2_in, ada_in, c_in, bias_in, x_in, out):
    with ExitStack() as everywhere:
        def sem(name):
            return everywhere.enter_context(nc.semaphore(name))

        counts = []

        def signal(name):
            counts.append(Count(sem(name)))
            return counts[-1]

        def sb(name, shape, scope=everywhere, dt=F32):
            return scope.enter_context(nc.sbuf_tensor(name, shape, dt))

        ps = everywhere.enter_context(nc.psum_tensor("ps", [P, 8, BANK], F32))
        raw = sb("raw", [P, RING, UNIT])
        high = sb("high", [P, RING, UNIT], dt=F32R)
        low = sb("low", [P, RING, UNIT], dt=F32R)
        const = sb("const", [P, N_CONST])
        par1 = sb("par1", [P, N_PAR1])
        par2 = sb("par2", [P, N_PAR2])
        xT = sb("xT", [P, KD, T])
        hh = sb("hh", [P, KD, T], dt=F32R)
        hl = sb("hl", [P, KD, T], dt=F32R)
        h = (hh, hl)
        mod = sb("mod", [P, 2, 48])
        sq = sb("sq", [P, KD, T])
        stat = sb("stat", [P, 4, T])
        small = sb("small", [P, 2, 8])
        lb = sb("lb", [P, DEPTH * HG_H])

        def C(name, lo=0, n=None):
            at, w = CONST[name]
            return const[:, at + lo:at + lo + (w - lo if n is None else n)]

        def P1(name):
            at, w = PAR1[name]
            return par1[:, at:at + w]

        def P2(name):
            at, w = PAR2[name]
            return par2[:, at:at + w]

        ident, ones = C("ident"), C("ones")

        ring = Ring(stream, raw, high, low, [sem(f"raw_full{i}") for i in range(RING)], signal("unit_done"),
                    signal("high_done"), signal("unit_split"))
        banks = Banks(ps, [sem(f"bank_read{i}") for i in range(4)], signal("bank_done"), 0, 4)
        mix_banks = Banks(ps, [sem(f"mix_bank_read{i}") for i in range(2)], banks.done, 2, 2)
        loaded = sem("inputs_loaded")
        par_loaded = sem("layer_parameters_loaded")
        stored = sem("output_stored")
        dve_step, act_step, pool_step = signal("dve_step"), signal("act_step"), signal("pool_step")
        squares, summed, variance, deviation = (signal(n) for n in ("squares", "summed", "variance", "deviation"))
        to_pe, to_pe2, to_act, to_act2, to_dve, to_dve2, c_ready = (
            signal(n) for n in ("for_tensor", "for_tensor2", "for_scalar", "for_scalar2", "for_vector",
                                "for_vector2", "silu_of_c_ready"))
        pv_done, pt_ready, pt_done, score_done, prob_ready = (
            signal(n) for n in ("values_weighted", "transposed_ready", "transposed", "scores_done", "probs_ready"))

        def new_block():
            for c in counts:
                c.base = c.n
            return nc.Block()

        def tell(ins, count):
            return ins.then_inc(count.sem, count.one())

        def restart_counts():
            with new_block() as block:
                @block.sync
                def _(sp):
                    for c in counts:
                        sp.sem_clear(c.sem)
                    for s in (*banks.read, *mix_banks.read):
                        sp.sem_clear(s)
                    for s in (par_loaded, c_loaded, *ada_full):
                        sp.sem_clear(s)
            for c in counts:
                c.n = c.base = 0
            for b in (banks, mix_banks):
                b.reads, b.turn = [0] * b.n, 0

        def restart_ring():
            with new_block() as block:
                @block.sync
                def _(sp):
                    for s in range(RING):
                        sp.wait_ge(ring.raw_full[s], 16 * (ring.loads[s] + 1))
            with new_block() as block:
                @block.sync
                def _(sp):
                    for s in range(RING):
                        sp.sem_clear(ring.raw_full[s])
            with new_block() as block:
                @block.sync
                def _(sp):
                    for s in range(RING):
                        sp.sem_inc(ring.raw_full[s], 16)
                    sp.sem_inc(ring.high_done.sem, RING)
                    sp.sem_inc(ring.split.sem, RING)
            ring.loads = [0] * RING
            ring.high_done.n = ring.split.n = RING

        with new_block() as block:
            @block.sync
            def _(sp):
                sp.dma_start(lb[:, :], lb_in).then_inc(loaded, 16)
                for s in range(RING):
                    ring.load(sp, s, s)
                for s in range(RING):
                    sp.wait_ge(ring.split.sem, s + 1)
                    ring.load(sp, RING + s, s)
                sp.wait_ge(loaded, 16 * 4)

            @block.scalar
            def _(act):
                act.dma_start(xT[:, :, :], x_in).then_inc(loaded, 16)
                act.dma_start(const[:, :], const_in).then_inc(loaded, 16)
                act.dma_start(par2[:, :], par2_in).then_inc(loaded, 16)
                for s in range(RING):
                    act.wait_ge(ring.raw_full[s], 16)
                    ring.round_high(act, s).then_inc(ring.high_done.sem, 1)

            @block.vector
            def _(dve):
                for s in range(RING):
                    dve.wait_ge(ring.high_done.sem, s + 1)
                    ring.take_low(dve, s).then_inc(ring.split.sem, 1)
        ring.loads = [1] * RING
        ring.high_done.n = ring.split.n = RING


        def square_tiles(act, c):
            tell(act.activation(sq[:, 2 * c:2 * c + 2, :], xT[:, 2 * c:2 * c + 2, :], ACT.Square), squares)

        def add_squares(pe, c):
            pe.wait_ge(squares.sem, squares.base + c + 1)
            for k in (2 * c, 2 * c + 1):
                pe.matmul(ps[:, 4, 0:T], ones, sq[:, k, :], start=(k == 0), stop=(k == KD - 1))

        def sum_of_squares():
            with new_block() as block:
                @block.scalar
                def _(act):
                    for c in range(KD // 2):
                        square_tiles(act, c)

                @block.tensor
                def _(pe):
                    for c in range(KD // 2):
                        add_squares(pe, c)

        def rms_norm(gain, shift=None, out=None, width=D):
            out, halves = (sq if out is None else out), out is not xT
            with new_block() as block:
                @block.scalar
                def _(act):
                    done = InOrder(act, act_step)
                    act.wait_ge(variance.sem, variance.base + 1)
                    tell(act.activation(stat[:, 1, :], stat[:, 0, :], ACT.Sqrt), deviation)
                    for k in range(0, KD if halves else 0, 2):
                        act.wait_ge(to_act.sem, to_act.base + k // 2 + 1)
                        if shift is not None:
                            for m in (k, k + 1):
                                ins = act.activation(out[:, m, :], out[:, m, :], ACT.Identity, bias=shift[:, m:m + 1])
                            done(ins)
                        tell(act.copy(hh[:, k:k + 2, :], out[:, k:k + 2, :]), to_dve)

                @block.vector
                def _(dve):
                    done = InOrder(dve, dve_step)
                    tell(dve.tensor_scalar(stat[:, 0, :], ps[:, 4, 0:T], 1.0 / width, EPS, ALU.mult, ALU.add), variance)
                    dve.wait_ge(deviation.sem, deviation.base + 1)
                    done(dve.reciprocal(stat[:, 2, :], stat[:, 1, :]))
                    for k in range(KD):
                        ins = dve.scalar_tensor_tensor(out[:, k, :], xT[:, k, :], gain[:, k:k + 1], stat[:, 2, :],
                                                       ALU.mult, ALU.mult)
                        if halves and k % 2:
                            tell(ins, to_act)
                        if halves and k % 2 and k > 1:
                            low_half(dve, k // 2 - 1, out)
                    if halves:
                        low_half(dve, KD // 2 - 1, out)

        def low_half(dve, c, x):
            dve.wait_ge(to_dve.sem, to_dve.base + c + 1)
            dve.tensor_tensor(hl[:, 2 * c:2 * c + 2, :], x[:, 2 * c:2 * c + 2, :], hh[:, 2 * c:2 * c + 2, :].bitcast(F32),
                              ALU.subtract)

        def residual_product(n_units, kt, x, gate=None, mods=None):
            w = ring.claim(n_units)
            prod = Product(w, 0, KD, kt, banks)

            def modulate(dve, i):
                if mods is not None:
                    mods.vector(dve, IN_SWIGLU + i + 1)

            with new_block() as block:
                @block.sync
                def _(sp):
                    for i in range(n_units):
                        if mods is not None:
                            mods.sync(sp, IN_SWIGLU + i)
                        w.sync(sp, [i])

                @block.tensor
                def _(pe):
                    for j in range(KD // 2):
                        prod.tensor(pe, x, j)
                        if j:
                            add_squares(pe, j - 1)
                    add_squares(pe, KD // 2 - 1)

                @block.scalar
                def _(act):
                    for j in range(KD // 2):
                        for i in prod.units_of(j):
                            w.scalar(act, i)
                        prod.after_read(act, j)
                        square_tiles(act, j)

                @block.vector
                def _(dve):
                    for j in range(KD // 2):
                        for i in list(prod.units_of(j))[:-1]:
                            w.vector(dve, i)
                            modulate(dve, i)
                        acc = prod.wait(dve, j)
                        for m in range(2):
                            k = 2 * j + m
                            if gate is None:
                                ins = dve.tensor_tensor(xT[:, k, :], xT[:, k, :], acc[:, m * T:(m + 1) * T], ALU.add)
                            else:
                                ins = dve.scalar_tensor_tensor(xT[:, k, :], acc[:, m * T:(m + 1) * T],
                                                               gate[:, k:k + 1], xT[:, k, :], ALU.mult, ALU.add)
                        ins.then_inc(prod.read(j), 1)
                        for i in list(prod.units_of(j))[-1:]:
                            w.vector(dve, i)
                            modulate(dve, i)
                    if mods is not None:
                        mods.finish(dve)

        hybrid = ExitStack()
        lbw = sb("lbw", [P, 6, HG_H], hybrid)
        ln_lb = sb("ln_lb", [P, DEPTH, HG_H], hybrid)
        ln_1m = sb("ln_1m", [P, DEPTH, HG_H], hybrid)
        lb_now = sb("lb_now", [P, 2, HG_H], hybrid)
        branches = ExitStack()
        hf = sb("hf", [P, HG_H, T], branches)
        hq = sb("hq", [P, HG_H, T], branches)
        hk = sb("hk", [P, HG_H, T], branches)
        hv = sb("hv", [P, TT, 512], branches)
        hog = sb("hog", [P, 4, T], branches)
        gq = sb("gq", [P, 2, T], branches)
        gk = sb("gk", [P, 2, T], branches)
        gg = sb("gg", [P, 2, T], branches)
        gv = sb("gv", [P, TT, 512], branches)
        glr = sb("glr", [P, T], branches)
        gates = sb("gates", [P, TT, 24], branches)
        gog = sb("gog", [P, 4, T], branches)
        qk = sb("qk", [P, 10, T], branches)
        vc = sb("vc", [P, 2, T], branches)
        vsw = sb("vsw", [P, TT, 2 * P], branches)
        yh = sb("yh", [P, 3, 4, T], branches, F32R)
        yl = sb("yl", [P, 3, 4, T], branches, F32R)
        W = sb("W", [P, 3, 4 * T], branches)
        scores = sb("scores", [P, 8, P], branches)
        cross = sb("cross", [P, 4, P], branches)

        with new_block() as block:
            @block.vector
            def _(dve):
                done = InOrder(dve, dve_step)
                a0, a1 = lb[:, 0:HG_H], lb[:, HG_H:2 * HG_H]
                done(dve.tensor_tensor(lbw[:, 0, :], a0, a1, ALU.max))
                dve.tensor_tensor(lbw[:, 1, :], a0, lbw[:, 0, :], ALU.subtract)
                tell(dve.tensor_tensor(lbw[:, 2, :], a1, lbw[:, 0, :], ALU.subtract), to_act)
                dve.wait_ge(to_dve.sem, to_dve.base + 1)
                done(dve.tensor_tensor(lbw[:, 5, :], lbw[:, 3, :], lbw[:, 4, :], ALU.add))
                dve.memset(ln_lb[:, 0, :], NEG)
                tell(dve.memset(ln_1m[:, 0, :], 0.0), to_act)
                dve.wait_ge(to_dve.sem, to_dve.base + 2)
                dve.tensor_tensor(ln_lb[:, 1, :], lbw[:, 2, :], lbw[:, 0, :], ALU.subtract)
                dve.tensor_tensor(ln_1m[:, 1, :], lbw[:, 1, :], lbw[:, 0, :], ALU.subtract)

            @block.tensor
            def _(pe):
                for c in range(KD // 2):
                    add_squares(pe, c)

            @block.scalar
            def _(act):
                for c in range(KD // 2):
                    square_tiles(act, c)
                act.wait_ge(to_act.sem, to_act.base + 1)
                act.activation(lbw[:, 3, :], lbw[:, 1, :], ACT.Exp)
                tell(act.activation(lbw[:, 4, :], lbw[:, 2, :], ACT.Exp), to_dve)
                act.wait_ge(to_act.sem, to_act.base + 2)
                tell(act.activation(lbw[:, 0, :], lbw[:, 5, :], ACT.Ln), to_dve)

        class Projections:

            def __init__(self):
                self.w = ring.claim(sum(n for _, n in UNITS1[:15]))
                self.pairs, at = [], 0
                for name, n in UNITS1[:15]:
                    prod = Product(self.w, at * BLOCKS, n, KD, banks, name in ("hi", "gv", "nvsw"))
                    self.pairs += [(name, prod, j) for j in range((n + 1) // 2)]
                    at += n
                self.mine = range(0)

            def take(self, n):
                self.mine = range(self.mine.stop, self.mine.stop + n)
                return self.mine

            def units(self, p):
                return list(self.pairs[p][1].units_of(self.pairs[p][2]))

            def sync(self, sp):
                for p in self.mine:
                    self.w.sync(sp, self.units(p))

            def tensor(self, pe, p):
                _, prod, j = self.pairs[p]
                prod.tensor(pe, h, j)

            def scalar(self, act, p):
                name, prod, j = self.pairs[p]
                units = self.units(p)
                for i in units[:-1]:
                    self.w.scalar(act, i)
                if name in ("hq", "hog", "gog"):
                    dst = {"hq": hq, "hog": hog, "gog": gog}[name]
                    acc = prod.wait(act, j)
                    act.activation(dst[:, 2 * j:2 * j + 2, :], acc.rearrange("p (m t) -> p m t", m=2), ACT.Silu) \
                        .then_inc(prod.read(j), 1)
                self.w.scalar(act, units[-1])

            def vector(self, dve, p):
                name, prod, j = self.pairs[p]
                units = self.units(p)
                for i in units[:-1]:
                    self.w.vector(dve, i)
                if name not in ("hq", "hog", "gog"):
                    acc = prod.wait(dve, j)
                    acc3 = acc.rearrange("p (m t) -> p m t", m=2)
                    if name == "misc":
                        dve.tensor_copy(glr[0:GLA_RANK, :], acc[0:GLA_RANK, 0:T])
                        ins = dve.tensor_copy(glr[32:32 + 24, :], acc[32:32 + 24, 0:T])
                    elif name == "gq":
                        ins = dve.tensor_scalar(gq[:, :, :], acc3, GLA_DK ** -0.5, None, ALU.mult)
                    elif name in ("hi", "gv", "nvsw"):
                        dst = {"hi": hv, "gv": gv, "nvsw": vsw}[name]
                        ins = dve.tensor_copy(dst[:, :, j * 2 * P:(j + 1) * 2 * P], acc3)
                    else:
                        dst = {"hf": hf, "gk": gk, "nkc": qk[:, 4:6, :], "nks": qk[:, 6:8, :], "nkw": qk[:, 8:10, :],
                               "nq": qk[:, 0:4, :], "nvc": vc}[name]
                        ins = dve.tensor_copy(dst[:, 2 * j:2 * j + 2, :], acc3)
                    ins.then_inc(prod.read(j), 1)
                self.w.vector(dve, units[-1])

        def project(proj, n):
            mine = proj.take(n)
            with new_block() as block:
                @block.sync
                def _(sp):
                    proj.sync(sp)

                @block.tensor
                def _(pe):
                    for p in mine:
                        proj.tensor(pe, p)

                @block.scalar
                def _(act):
                    for p in mine:
                        proj.scalar(act, p)

                @block.vector
                def _(dve):
                    for p in mine:
                        proj.vector(dve, p)


        def log_sigmoid_tail(act, buf, wait_for, tell_to):
            done = InOrder(act, act_step)
            if wait_for is not None:
                act.wait_ge(*wait_for)
            done(act.activation(buf, buf, ACT.Abs))
            done(act.activation(buf, buf, ACT.Exp, scale=-1.0))
            tell(act.activation(buf, buf, ACT.Ln, bias=1.0), tell_to)

        def flat(a):
            return a.rearrange("p a b -> p (a b)")

        def prepare_hgrn(layer, proj, n):
            c, dist = W[:, 1, :], W[:, 2, :]
            c3, dist3 = (a.rearrange("p (h t) -> p h t", h=HG_H) for a in (c, dist))
            mine = proj.take(n)
            with new_block() as block:
                @block.sync
                def _(sp):
                    proj.sync(sp)

                @block.tensor
                def _(pe):
                    for p in mine:
                        proj.tensor(pe, p)

                @block.vector
                def _(dve):
                    done = InOrder(dve, dve_step)
                    dve.tensor_copy(lb_now[:, 0:1, :], ln_lb[:, bass.ds(layer, 1), :])
                    dve.tensor_copy(lb_now[:, 1:2, :], ln_1m[:, bass.ds(layer, 1), :])
                    tell(dve.tensor_copy(dist, flat(hf[:, :, :])), to_act)
                    dve.wait_ge(to_dve.sem, to_dve.base + 1)
                    done(dve.scalar_tensor_tensor(c, flat(hf[:, :, :]), 0.0, dist, ALU.min, ALU.subtract))
                    for h in range(HG_H):
                        ins = dve.tensor_scalar(c3[:, h, :], c3[:, h, :], lb_now[:, 1, h:h + 1], None, ALU.add)
                    done(ins)
                    tell(dve.tensor_tensor(flat(hk[:, :, :]), c, flat(hf[:, :, :]), ALU.subtract), to_act)
                    for h in range(HG_H):
                        ins = dve.tensor_scalar(dist3[:, h, :], c3[:, h, :], lb_now[:, 0, h:h + 1], None, ALU.subtract)
                    tell(ins, to_act)
                    proj.vector(dve, mine[0])
                    dve.wait_ge(to_dve.sem, to_dve.base + 2)
                    for h in range(HG_H):
                        dve.scalar_tensor_tensor(hf[:, h, :], c3[:, h, :], lb_now[:, 0, h:h + 1], dist3[:, h, :],
                                                 ALU.max, ALU.add)
                    for p in mine[1:]:
                        proj.vector(dve, p)

                @block.scalar
                def _(act):
                    log_sigmoid_tail(act, dist, (to_act.sem, to_act.base + 1), to_dve)
                    proj.scalar(act, mine[0])
                    act.wait_ge(to_act.sem, to_act.base + 2)
                    act.activation(flat(hk[:, :, :]), flat(hk[:, :, :]), ACT.Exp)
                    log_sigmoid_tail(act, dist, (to_act.sem, to_act.base + 3), to_dve)
                    for p in mine[1:]:
                        proj.scalar(act, p)

        def prepare_gla(proj, n):
            mine = proj.take(n)
            with new_block() as block:
                @block.sync
                def _(sp):
                    proj.sync(sp)

                @block.tensor
                def _(pe):
                    for t in range(TT):
                        ins = pe.transpose(ps[:, 4, t * 32:t * 32 + 24], glr[32:32 + 24, t * P:(t + 1) * P],
                                           ident[32:32 + 24, 32:32 + 24])
                    tell(ins, to_dve)
                    for p in mine:
                        proj.tensor(pe, p)
                    for m in range(2):
                        ins = pe.matmul(ps[:, 5, m * T:(m + 1) * T], P1("gla_w2")[0:GLA_RANK, m * P:(m + 1) * P],
                                        glr[0:GLA_RANK, :], start=True, stop=True)
                    tell(ins, to_dve)

                @block.vector
                def _(dve):
                    done = InOrder(dve, dve_step)
                    dve.wait_ge(to_dve.sem, to_dve.base + 1)
                    dve.tensor_copy(gates[:, :, :], ps[:, 4, 0:2 * 32].rearrange("p (t n) -> p t n", t=TT)[:, :, 0:24])
                    for p in mine:
                        proj.vector(dve, p)
                    dve.wait_ge(to_dve.sem, to_dve.base + 2)
                    for m in range(2):
                        ins = dve.tensor_scalar(gg[:, m, :], ps[:, 5, m * T:(m + 1) * T], P1("gla_b")[:, m:m + 1],
                                                None, ALU.add)
                    done(ins)
                    tell(dve.tensor_copy(W[:, 2, 0:2 * T], flat(gg[:, :, :])), to_act)
                    dve.wait_ge(to_dve2.sem, to_dve2.base + 1)
                    done(dve.scalar_tensor_tensor(flat(gg[:, :, :]), flat(gg[:, :, :]), 0.0, W[:, 2, 0:2 * T],
                                                  ALU.min, ALU.subtract))
                    dve.tensor_scalar(gg[:, :, :], gg[:, :, :], 1.0 / GLA_TAU, None, ALU.mult)

                @block.scalar
                def _(act):
                    for p in mine:
                        proj.scalar(act, p)
                    log_sigmoid_tail(act, W[:, 2, 0:2 * T], (to_act.sem, to_act.base + 1), to_dve2)

        def linear_attention(q, k, v, g, tiles, dk, gate, gain, branch, proj, n_steps, n_tail):
            taken = list(proj.take(n_steps + n_tail))
            mine, tail = taken[:n_steps], taken[n_steps:]
            n = tiles * T
            b = W[:, 0, 0:n]
            b4 = b.rearrange("p (f t s) -> p f t s", f=tiles, t=TT)
            fold = [W[:, 1, 0:n], W[:, 2, 0:n]]
            decay = [flat(sq[:, 4 * i:4 * i + tiles, :]) for i in range(2)]
            qf, kf = flat(q[:, :, :]), flat(k[:, :, :])
            steps = LEVELS + 2
            per_head = P // dk

            def head(buf3, h, t):
                lo = h % per_head * dk
                return buf3[lo:lo + dk, h // per_head, t * P:(t + 1) * P]

            def place(h, t):
                return (t, h) if per_head == 1 else (h % 2, 2 * t + h // 2)

            def cross_place(h):
                return h if per_head == 1 else h % 2 * 2 + h // 2

            with new_block() as block:
                @block.sync
                def _(sp):
                    proj.sync(sp)

                @block.vector
                def _(dve):
                    done = InOrder(dve, dve_step)
                    for f in range(tiles):
                        for t in range(TT):
                            ins = dve.tensor_tensor_scan(b4[:, f, t, :], ones, g[:, f, t * P:(t + 1) * P], 0.0,
                                                         ALU.mult, ALU.add)
                    done(ins)

                    def halves(a, lv):
                        m = 1 << lv
                        v4 = a.rearrange("p (n two m) -> p n two m", two=2, m=m)
                        return v4[:, :, 0, :], v4[:, :, 1, :]

                    def exponents(lv):
                        if lv >= 2:
                            dve.wait_ge(to_pe.sem, to_pe.base + lv - 1)
                        first, second = halves(b, lv)
                        e1, e2 = halves(decay[lv % 2], lv)
                        ref = first[:, :, (1 << lv) - 1:1 << lv].broadcast_to(list(first.shape))
                        dve.tensor_tensor(e1, ref, first, ALU.subtract)
                        if lv < LEVELS:
                            ins = dve.tensor_tensor(e2, second, ref, ALU.subtract)
                        else:
                            ins = dve.tensor_copy(e2, second)
                        tell(ins, to_act)

                    def weigh(lv):
                        dve.wait_ge(to_dve.sem, to_dve.base + lv + 1)
                        if lv >= 2:
                            dve.wait_ge(score_done.sem, score_done.base + lv)
                        e1, e2 = halves(decay[lv % 2], lv)
                        f1, f2 = halves(fold[lv % 2], lv)
                        dve.tensor_tensor(f1, halves(kf, lv)[0], e1, ALU.mult)
                        tell(dve.tensor_tensor(f2, halves(qf, lv)[1], e2, ALU.mult), to_pe)

                    def pick(step):
                        dve.wait_ge(score_done.sem, score_done.base + step + 1)
                        if step:
                            dve.wait_ge(prob_ready.sem, prob_ready.base + step)
                        bank = 4 + step % 2 * 2
                        if step == 0:
                            for i in range(2):
                                ins = dve.tensor_tensor(
                                    scores[:, 4 * i:4 * i + 4, :],
                                    ps[:, bank + i, :].rearrange("p (h t) -> p h t", h=4),
                                    ident.unsqueeze(1).broadcast_to([P, 4, P]), ALU.mult)
                        elif step <= LEVELS:
                            mask = C("level", (step - 1) * P, P).bitcast(U32).unsqueeze(1).broadcast_to([P, 4, P])
                            for i in range(2):
                                ins = dve.copy_predicated(scores[:, 4 * i:4 * i + 4, :], mask,
                                                          ps[:, bank + i, :].rearrange("p (h t) -> p h t", h=4))
                        else:
                            for i in range(per_head):
                                w = 4 // per_head
                                ins = dve.tensor_copy(cross[:, i * w:(i + 1) * w, :],
                                                      ps[:, bank + i, 0:w * P].rearrange("p (h t) -> p h t", h=w))
                        tell(ins, prob_ready)

                    exponents(0)
                    for step in range(steps):
                        if step + 1 < LEVELS + 1:
                            exponents(step + 1)
                        if step < LEVELS + 1:
                            weigh(step)
                        pick(step)
                        if step:
                            for p in mine[step - 1:step]:
                                proj.vector(dve, p)
                    for p in mine[steps - 1:]:
                        proj.vector(dve, p)
                    dve.wait_ge(to_act.sem, to_act.base + LEVELS + 1)
                    dve.wait_ge(to_pe.sem, to_pe.base + LEVELS + 1)
                    dve.wait_ge(summed.sem, summed.base + 1)
                    for i in range(2):
                        ins = dve.tensor_scalar(W[:, 0, i * BANK:(i + 1) * BANK], ps[:, 6 + i, :], 1.0 / 128, EPS,
                                                ALU.mult, ALU.add)
                    tell(ins, variance)
                    for p in tail[:1]:
                        proj.vector(dve, p)
                    dve.wait_ge(deviation.sem, deviation.base + 1)
                    done(dve.reciprocal(W[:, 0, :], W[:, 0, :]))
                    for h in range(4):
                        ins = dve.scalar_tensor_tensor(
                            W[:, 1, h * T:(h + 1) * T], ps[:, 4 + h // 2, h % 2 * T:(h % 2 + 1) * T],
                            gain[:, h:h + 1], W[:, 0, h * T:(h + 1) * T], ALU.mult, ALU.mult)
                    done(ins)
                    tell(dve.tensor_tensor(W[:, 1, :], W[:, 1, :], flat(gate[:, :, :]), ALU.mult), to_act)
                    dve.wait_ge(to_dve.sem, to_dve.base + LEVELS + 2)
                    dve.tensor_tensor(flat(yl[:, branch, :, :]), W[:, 1, :], flat(yh[:, branch, :, :]).bitcast(F32),
                                      ALU.subtract)
                    for p in tail[1:]:
                        proj.vector(dve, p)

                @block.scalar
                def _(act):
                    for lv in range(LEVELS + 1):
                        act.wait_ge(to_act.sem, to_act.base + lv + 1)
                        tell(act.activation(decay[lv % 2], decay[lv % 2], ACT.Exp), to_dve)
                        if lv >= 2:
                            for p in mine[lv - 2:lv - 1]:
                                proj.scalar(act, p)
                    for p in mine[LEVELS - 1:]:
                        proj.scalar(act, p)
                    act.wait_ge(pv_done.sem, pv_done.base + 1)
                    for i in range(2):
                        ins = act.activation(flat(sq[:, 2 * i:2 * i + 2, :]), ps[:, 4 + i, :], ACT.Square)
                    tell(ins, squares)
                    act.wait_ge(variance.sem, variance.base + 1)
                    tell(act.activation(W[:, 0, :], W[:, 0, :], ACT.Sqrt), deviation)
                    for p in tail[:1]:
                        proj.scalar(act, p)
                    act.wait_ge(to_act.sem, to_act.base + LEVELS + 2)
                    tell(act.copy(flat(yh[:, branch, :, :]), W[:, 1, :]), to_dve)
                    for p in tail[1:]:
                        proj.scalar(act, p)

                @block.tensor
                def _(pe):
                    for step in range(steps):
                        if step:
                            pe.wait_ge(to_pe.sem, to_pe.base + step)
                        if step >= 2:
                            pe.wait_ge(prob_ready.sem, prob_ready.base + step - 1)
                        bank = 4 + step % 2 * 2
                        f3 = fold[(step - 1) % 2].rearrange("p (f t) -> p f t", f=tiles)
                        for t in range(TT if step <= LEVELS else 1):
                            for h in range(4):
                                i, c0 = place(h, t)
                                out_ = ps[:, bank + i, c0 * P:(c0 + 1) * P]
                                if step == 0:
                                    a, c = head(k, h, t), head(q, h, t)
                                elif step <= LEVELS:
                                    a = c = head(f3, h, t)
                                else:
                                    a, c = head(f3, h, 0), head(f3, h, 1)
                                ins = pe.matmul(out_, a, c, start=True, stop=True)
                        tell(ins, score_done)
                        for p in mine[step:step + 1]:
                            proj.tensor(pe, p)
                    pe.wait_ge(prob_ready.sem, prob_ready.base + steps)
                    for h in range(4):
                        o = ps[:, 4 + h // 2, h % 2 * T:(h % 2 + 1) * T]
                        vh = [v[:, t, h * P:(h + 1) * P] for t in range(TT)]
                        own = [scores[:, 4 * place(h, t)[0] + place(h, t)[1], :] for t in range(TT)]
                        pe.matmul(o[:, 0:P], vh[0], own[0], start=True, stop=True)
                        pe.matmul(o[:, P:T], vh[1], own[1], start=True, stop=False)
                        ins = pe.matmul(o[:, P:T], vh[0], cross[:, cross_place(h), :], start=False, stop=True)
                    tell(ins, pv_done)
                    pe.wait_ge(squares.sem, squares.base + 1)
                    for i in range(2):
                        ins = pe.matmul(ps[:, 6 + i, :], ones, flat(sq[:, 2 * i:2 * i + 2, :]), start=True, stop=True)
                    tell(ins, summed)
                    for p in tail:
                        proj.tensor(pe, p)

        def attention(block, items, q_of, k_of, add_of, weight_of, small, prob, turned, values, act_after,
                      dve_after, beside=None):
            parts = ((0, P), (P, 3 * P))

            @block.tensor
            def _(pe):
                def score(i):
                    if i >= 2:
                        pe.wait_ge(to_pe.sem, to_pe.base + i - 1)
                    for t, (lo, hi) in enumerate(parts):
                        ins = pe.matmul(ps[:, 4 + i % 2, lo:hi], q_of(i, t), k_of(i, hi - lo), start=True, stop=True)
                    tell(ins, score_done)

                def turn(i):
                    pe.wait_ge(prob_ready.sem, prob_ready.base + i + 1)
                    if i >= 2:
                        pe.wait_ge(pt_ready.sem, pt_ready.base + i - 1)
                    for c in range(3):
                        ins = pe.transpose(ps[:, 6 + i % 2, c * P:(c + 1) * P], prob[i % 2][:, c * P:(c + 1) * P], ident)
                    tell(ins, pt_done)

                score(0)
                score(1)
                for i in range(items):
                    turn(i)
                    if i + 2 < items:
                        score(i + 2)
                    if beside is not None:
                        beside.tensor_item(pe, i)
                    values(pe, i)

            @block.vector
            def _(dve):
                done = InOrder(dve, dve_step)

                def rows_max(i):
                    s = small[:, i % 2, :]
                    dve.wait_ge(score_done.sem, score_done.base + i + 1)
                    if i >= 2:
                        dve.wait_ge(pt_done.sem, pt_done.base + i - 1)
                    tell(dve.scalar_tensor_tensor(prob[i % 2], ps[:, 4 + i % 2, 0:3 * P], NSA_DH ** -0.5, add_of(i),
                                                  ALU.mult, ALU.add), to_pe)
                    dve.wait_ge(to_pe.sem, to_pe.n)
                    for t, (lo, hi) in enumerate(parts):
                        ins = dve.tensor_reduce(s[:, t:t + 1], prob[i % 2][:, lo:hi], AX_X, ALU.max)
                    done(ins)
                    tell(dve.tensor_scalar(s[:, 2:4], s[:, 0:2], -1.0, None, ALU.mult), to_act)

                def normalise(i):
                    s = small[:, i % 2, :]
                    dve.wait_ge(to_dve.sem, to_dve.base + i + 1)
                    done(dve.reciprocal(s[:, 6:8], s[:, 4:6]))
                    if weight_of(i) is not None:
                        done(dve.tensor_tensor(s[:, 6:8], s[:, 6:8], weight_of(i), ALU.mult))
                    for t, (lo, hi) in enumerate(parts):
                        ins = dve.tensor_scalar(prob[i % 2][:, lo:hi], prob[i % 2][:, lo:hi], s[:, 6 + t:7 + t], None,
                                                ALU.mult)
                    tell(ins, prob_ready)

                rows_max(0)
                for i in range(items):
                    if i + 1 < items:
                        rows_max(i + 1)
                    normalise(i)
                    if beside is not None:
                        beside.vector_item(dve, i)
                dve_after(dve)

            @block.scalar
            def _(act):
                def exponentials(i):
                    s = small[:, i % 2, :]
                    act.wait_ge(to_act.sem, to_act.base + i + 1)
                    for t, (lo, hi) in enumerate(parts):
                        ins = act.activation(prob[i % 2][:, lo:hi], prob[i % 2][:, lo:hi], ACT.Exp,
                                             bias=s[:, 2 + t:3 + t], accum_out=s[:, 4 + t:5 + t])
                    tell(ins, to_dve)

                exponentials(0)
                for i in range(items):
                    if i + 1 < items:
                        exponentials(i + 1)
                    if beside is not None:
                        beside.scalar_item(act, i)
                    act.wait_ge(pt_done.sem, pt_done.base + i + 1)
                    act_after(act, i)
                    tell(act.copy(turned(i), ps[:, 6 + i % 2, 0:3 * P]), pt_ready)
                act_after(act, items)

        cstat = sb("cstat", [P, 4, 16], branches)
        kcd = sb("kcd", [P, 2 * NCMP], branches)
        vcm = sb("vcm", [P, NSA_G * NSA_DH], branches)
        hid = sb("hid", [P, 2, 2 * NCMP], branches)
        both = sb("window_halves", [P, 2, 16, 2 * (2 * NCMP + 2)], branches, F32R)

        class Mix:

            def __init__(self):
                self.turns = N_BR * KD // 2
                self.gate, self.branch, self.units = [], [], []
                self.mine = range(0)

            def claim(self, turns):
                w, base = ring.claim(3 * turns), len(self.gate)
                for n in range(turns):
                    self.gate.append(Product(w, 3 * n * BLOCKS, 2, KD, mix_banks))
                    self.branch.append(Product(w, (3 * n + 2) * BLOCKS, 2, 4, mix_banks))
                    self.units += [(w, 3 * n + c) for c in range(3)]

            def take(self, turns):
                self.mine = range(self.mine.stop, self.mine.stop + 3 * turns)
                return self.mine

            def sync(self, sp):
                for p in self.mine:
                    w, i = self.units[p]
                    w.sync(sp, [i])

            def sig(self, n):
                return flat(hf[:, n % 2 * 2:n % 2 * 2 + 2, :])

            def tensor(self, pe, p):
                n, c = divmod(p, 3)
                if c < 2:
                    self.gate[n].tensor(pe, h, 0, only=c)
                else:
                    b = n // (KD // 2)
                    self.branch[n].tensor(pe, (yh[:, b, :, :], yl[:, b, :, :]), 0)

            def scalar(self, act, p):
                n, c = divmod(p, 3)
                w, i = self.units[p]
                if c == 1:
                    acc = self.gate[n].wait(act, 0)
                    if n >= 2:
                        self.branch[n - 2].after_read(act, 0)
                    act.activation(self.sig(n), acc, ACT.Tanh, scale=0.5).then_inc(self.gate[n].read(0), 1)
                w.scalar(act, i)

            def vector(self, dve, p):
                n, c = divmod(p, 3)
                w, i = self.units[p]
                if c == 2:
                    b, j = n // (KD // 2), n % (KD // 2)
                    acc = self.branch[n].wait(dve, 0)
                    self.gate[n].after_read(dve, 0)
                    m = flat((hk, hog)[j // 2][:, j % 2 * 2:j % 2 * 2 + 2, :])
                    if b == 0:
                        dve.scalar_tensor_tensor(m, self.sig(n), 1.0, acc, ALU.add, ALU.mult).then_inc(self.branch[n].read(0), 1)
                    else:
                        part = flat(hq[:, j % 2 * 2:j % 2 * 2 + 2, :])
                        dve.scalar_tensor_tensor(part, self.sig(n), 1.0, acc, ALU.add, ALU.mult).then_inc(self.branch[n].read(0), 1)
                        self.branch[n].after_read(dve, 0)
                        tell(dve.tensor_tensor(m, m, part, ALU.add), mixed)
                w.vector(dve, i)

            def tensor_item(self, pe, i):
                for p in self.mine[max(i - 1, 0):max(i, 0)]:
                    self.tensor(pe, p)

            def scalar_item(self, act, i):
                for p in self.mine[max(i - 3, 0):max(i - 2, 0)]:
                    self.scalar(act, p)

            def vector_item(self, dve, i):
                for p in self.mine[max(i - 3, 0):max(i - 2, 0)]:
                    self.vector(dve, p)

        def mix_rest(mix, turns):
            mine = mix.take(turns)
            with new_block() as block:
                @block.sync
                def _(sp):
                    mix.sync(sp)

                @block.tensor
                def _(pe):
                    for p in mine:
                        mix.tensor(pe, p)

                @block.scalar
                def _(act):
                    for p in mine:
                        mix.scalar(act, p)

                @block.vector
                def _(dve):
                    for p in mine:
                        mix.vector(dve, p)
            with new_block() as block:
                @block.scalar
                def _(act):
                    for c in range(KD // 2):
                        tell(act.activation(hh[:, 2 * c:2 * c + 2, :], (hk, hog)[c // 2][:, c % 2 * 2:c % 2 * 2 + 2, :],
                                            ACT.Copy, scale=0.5), to_dve)

                @block.vector
                def _(dve):
                    for c in range(KD // 2):
                        dve.wait_ge(to_dve.sem, to_dve.base + c + 1)
                        dve.scalar_tensor_tensor(hl[:, 2 * c:2 * c + 2, :],
                                                 (hk, hog)[c // 2][:, c % 2 * 2:c % 2 * 2 + 2, :], 0.5,
                                                 hh[:, 2 * c:2 * c + 2, :].bitcast(F32), ALU.mult, ALU.subtract)

        mixed = signal("mixed")

        def rope(mix, turns):
            mine = mix.take(turns)
            with new_block() as block:
                @block.sync
                def _(sp):
                    mix.sync(sp)

                @block.scalar
                def _(act):
                    for p in mine:
                        mix.scalar(act, p)

                @block.tensor
                def _(pe):
                    for j in range(5):
                        if j == 4:
                            pe.wait_ge(to_pe.sem, to_pe.base + 1)
                        tell(pe.matmul(ps[:, 4 + j % 4, :], C("rot"), flat(qk[:, 2 * j:2 * j + 2, :]), start=True,
                                       stop=True), to_dve)
                    for p in mine:
                        mix.tensor(pe, p)

                @block.vector
                def _(dve):
                    done = InOrder(dve, dve_step)
                    cos, sin = (C(n).unsqueeze(1).broadcast_to([P, 2, T]) for n in ("cos", "sin"))
                    for j in range(5):
                        x = qk[:, 2 * j:2 * j + 2, :]
                        turned = W[:, j % 2, 0:BANK].rearrange("p (m t) -> p m t", m=2)
                        dve.wait_ge(to_dve.sem, to_dve.base + j + 1)
                        ins = dve.tensor_tensor(turned, ps[:, 4 + j % 4, :].rearrange("p (m t) -> p m t", m=2), sin,
                                                ALU.mult)
                        if j == 0:
                            tell(ins, to_pe)
                        done(dve.tensor_tensor(x, x, cos, ALU.mult))
                        done(dve.tensor_tensor(x, x, turned, ALU.add))
                    for p in mine:
                        mix.vector(dve, p)

        def compress(w, mix, turns):
            cols = 2 * NCMP + 2
            win = [W[:, i, 0:16 * cols].rearrange("p (j c) -> p j c", c=cols) for i in range(2)]
            at, _ = PAR1["pos_k"]
            mine = mix.take(turns)
            with new_block() as block:
                @block.sync
                def _(sp):
                    mix.sync(sp)
                    w.sync(sp)

                @block.vector
                def _(dve):
                    for i, src in enumerate((qk[:, 4:6, :], vc[:, :, :])):
                        for half in range(2):
                            r = slice(half * NSA_DH, (half + 1) * NSA_DH)
                            for g in range(NSA_G):
                                first = src[r, g, 0:T].rearrange("p (n j two) -> p two j n", j=8, two=2)[:, half, :, :]
                                c = slice(g * NCMP, (g + 1) * NCMP)
                                dve.tensor_copy(win[i][r, 0:8, c], first[:, :, 0:NCMP])
                                dve.tensor_copy(win[i][r, 8:16, c], first[:, :, 1:NCMP + 1])
                        pos = par1[:, at + 16 * i:at + 16 * (i + 1)]
                        tell(dve.tensor_copy(win[i][:, :, 2 * NCMP:cols], pos.unsqueeze(2).broadcast_to([P, 16, 2])),
                             to_act)
                    for p in mine[:2]:
                        mix.vector(dve, p)
                    for i in range(2):
                        dve.wait_ge(to_dve.sem, to_dve.base + i + 1)
                        tell(dve.tensor_tensor(both[:, i, :, cols:2 * cols], win[i],
                                               both[:, i, :, 0:cols].bitcast(F32), ALU.subtract), to_pe)
                    for p in mine[2:]:
                        mix.vector(dve, p)
                    for i in range(2):
                        w.vector(dve, 2 * i)
                        dve.wait_ge(*w.done(2 * i + 1))
                        done = InOrder(dve, dve_step)
                        s = W[:, 2, 64 * i:64 * i + cols]
                        done(dve.tensor_copy(s, ps[:, 4 + i, cols:2 * cols]))
                        done(dve.tensor_tensor(s, s, ps[:, 4 + i, 0:cols], ALU.add))
                        tell(dve.tensor_copy(cstat[:, 0, i:i + 1], s[:, cols - 1:cols]), to_act)
                        w.vector(dve, 2 * i + 1)
                    dve.wait_ge(to_dve.sem, to_dve.base + 3)
                    dve.tensor_copy(kcd[:, :], ps[:, 6, 0:2 * NCMP])
                    for i in range(4):
                        dve.tensor_copy(vcm[32 * i:32 * i + NCMP, :], ps[32 * i:32 * i + NCMP, 7, 0:NSA_G * NSA_DH])

                @block.tensor
                def _(pe):
                    for p in mine:
                        mix.tensor(pe, p)
                    for i in range(2):
                        pe.wait_ge(to_pe.sem, to_pe.base + i + 1)
                        halves = [w.arrived(pe, 2 * i + u) for u in range(2)]
                        for j in range(2 * BLOCKS):
                            at = j % BLOCKS * P
                            wh, wl = (a[:, at:at + P] for a in halves[j // BLOCKS])
                            pe.matmul(ps[:, 4 + i, 0:2 * cols], wh, both[:, i, j, :], start=(j == 0), stop=False,
                                      skip_group_check=True)
                            ins = pe.matmul(ps[:, 4 + i, 0:cols], wl, both[:, i, j, 0:cols], start=False,
                                            stop=(j == 2 * BLOCKS - 1), skip_group_check=True)
                            if j % BLOCKS == BLOCKS - 1:
                                ins.then_inc(ring.unit_done.sem, 1)
                    pe.wait_ge(to_pe2.sem, to_pe2.base + 2)
                    pe.matmul(ps[:, 6, 0:2 * NCMP], P1("w2_k"), hid[:, 0, :], start=True, stop=True)
                    for i in range(4):
                        for g in range(NSA_G):
                            ins = pe.matmul(ps[32 * i:32 * i + NCMP, 7, g * NSA_DH:(g + 1) * NSA_DH],
                                            hid[:, 1, g * NCMP:(g + 1) * NCMP], P1("w2_v"), start=True, stop=True,
                                            tile_position=(0, 32 * i))
                    tell(ins, to_dve)

                @block.scalar
                def _(act):
                    for p in mine[:2]:
                        mix.scalar(act, p)
                    for i in range(2):
                        act.wait_ge(to_act.sem, to_act.base + i + 1)
                        tell(act.copy(both[:, i, :, 0:cols], win[i]), to_dve)
                    for p in mine[2:]:
                        mix.scalar(act, p)
                    for i in range(2):
                        w.scalar(act, 2 * i)
                        act.wait_ge(to_act.sem, to_act.base + i + 3)
                        tell(act.activation(hid[:, i, :], W[:, 2, 64 * i:64 * i + 2 * NCMP], ACT.Gelu_apprx_tanh,
                                            bias=cstat[:, 0, i:i + 1]), to_pe2)
                        w.scalar(act, 2 * i + 1)
                    act.activation(flat(gates[:, :, :]), flat(gates[:, :, :]), ACT.Sigmoid)

        def query_half(h, buf, t):
            lo = h % 2 * NSA_DH
            return buf[lo:lo + NSA_DH, h // 2, t * P:(t + 1) * P]

        pc = W[:, 1, 0:BANK].rearrange("p (t h n) -> p t h n", t=TT, h=NSA_H)
        ptc = W[:, 2, 0:BANK].rearrange("p (i t) -> p i t", i=4)

        def compressed_probabilities(mix, turns):
            def over_heads(name, n):
                return C(name).rearrange("p (t n) -> p t n", t=TT)[:, :, 0:n].unsqueeze(2) \
                    .broadcast_to([P, TT, NSA_H, n])

            def over_keys(a, n):
                return a.rearrange("p (t h) -> p t h", t=TT).unsqueeze(3).broadcast_to([P, TT, NSA_H, n])

            mine = mix.take(turns)
            with new_block() as block:
                @block.sync
                def _(sp):
                    mix.sync(sp)

                @block.tensor
                def _(pe):
                    for t in range(TT):
                        for h in range(NSA_H):
                            lo, g = h % 2 * NSA_DH, h // 4
                            at = t * P + h // 2 * 32
                            ins = pe.matmul(ps[:, 4 + h % 2, at:at + NCMP], query_half(h, qk, t),
                                            kcd[lo:lo + NSA_DH, g * NCMP:(g + 1) * NCMP], start=True, stop=True)
                    tell(ins, score_done)
                    for p in mine:
                        mix.tensor(pe, p)
                    pe.wait_ge(prob_ready.sem, prob_ready.base + 1)
                    for i in range(4):
                        ins = pe.transpose(ps[:, 6, i * P:(i + 1) * P], W[:, 1, i * P:(i + 1) * P], ident)
                    tell(ins, pt_done)

                @block.vector
                def _(dve):
                    done = InOrder(dve, dve_step)
                    done(dve.memset(W[:, 1, 0:BANK], 0.0))
                    dve.wait_ge(score_done.sem, score_done.base + 1)
                    pairs = pc.rearrange("p t (h two) n -> p t h two n", two=2)
                    for i in range(2):
                        s4 = ps[:, 4 + i, 0:T].rearrange("p (t h n) -> p t h n", t=TT, h=NSA_H // 2)
                        ins = dve.tensor_tensor(pairs[:, :, :, i, 0:NCMP], s4[:, :, :, 0:NCMP],
                                                over_heads("cmp_neg", NCMP)[:, :, 0:NSA_H // 2, :], ALU.add)
                    done(ins)
                    done(dve.tensor_reduce(cstat[:, 1, :].rearrange("p (t h) -> p t h", t=TT), pc[:, :, :, 0:NCMP], AX_X,
                                           ALU.max))
                    tell(dve.tensor_tensor(pc[:, :, :, 0:NCMP], pc[:, :, :, 0:NCMP], over_keys(cstat[:, 1, :], NCMP),
                                           ALU.subtract), to_act)
                    dve.wait_ge(to_dve.sem, to_dve.base + 1)
                    done(dve.tensor_reduce(cstat[:, 2, :].rearrange("p (t h) -> p t h", t=TT), pc[:, :, :, 0:NCMP], AX_X,
                                           ALU.add))
                    done(dve.reciprocal(cstat[:, 3, :], cstat[:, 2, :]))
                    gate = gates[:, :, :].rearrange("p t (h k) -> p t h k", k=3)[:, :, :, 0]
                    rec = cstat[:, 3, :].rearrange("p (t h) -> p t h", t=TT)
                    dve.tensor_tensor(rec, rec, gate, ALU.mult)
                    done(dve.tensor_tensor(pc, pc, over_heads("cmp_keep", 32), ALU.mult))
                    tell(dve.tensor_tensor(pc, pc, over_keys(cstat[:, 3, :], 32), ALU.mult), prob_ready)
                    dve.wait_ge(pt_done.sem, pt_done.base + 1)
                    dve.tensor_copy(W[:, 2, 0:BANK], ps[:, 6, :])
                    for p in mine:
                        mix.vector(dve, p)

                @block.scalar
                def _(act):
                    act.wait_ge(to_act.sem, to_act.base + 1)
                    tell(act.activation(W[:, 1, 0:BANK], W[:, 1, 0:BANK], ACT.Exp, scale=NSA_DH ** -0.5), to_dve)
                    for p in mine:
                        mix.scalar(act, p)

        def sparse_attention(mix, turns):
            sqf = flat(sq[:, :, :])
            turned = lambda i: sqf[:, i % 4 * BANK:i % 4 * BANK + 3 * P]
            prob = [W[:, 0, 0:3 * P], W[:, 0, BANK:BANK + 3 * P]]
            gate4 = gates[:, :, :].rearrange("p t (h k) -> p t h k", k=3)

            def values(pe, i):
                if i % 2 == 0:
                    return
                h = i // 2
                g, lo, c32 = h // 4, h % 2 * NSA_DH, 32 * (h % 4)
                pe.wait_ge(pt_ready.sem, pt_ready.base + i + 1)
                for t in range(TT):
                    o = ps[lo:lo + NSA_DH, h // 4, h // 2 % 2 * T + t * P:h // 2 % 2 * T + (t + 1) * P]
                    pe.matmul(o, vcm[c32:c32 + NCMP, g * NSA_DH:(g + 1) * NSA_DH],
                              ptc[c32:c32 + NCMP, 2 * t + h // 4, :], start=True, stop=False, tile_position=(c32, lo))
                    for b in range(2):
                        for s in range(t + 1):
                            ins = pe.matmul(o, vsw[:, s, b * P + g * NSA_DH:b * P + (g + 1) * NSA_DH],
                                            turned(2 * h + b)[:, (t + s) * P:(t + s + 1) * P], start=False,
                                            stop=(b == 1 and s == t))
                tell(ins, pv_done)

            def act_after(act, i):
                if 4 <= i < 2 * NSA_H:
                    act.wait_ge(pv_done.sem, pv_done.base + (i - 4) // 2 + 1)
                if i == 2 * NSA_H:
                    act.wait_ge(pv_done.sem, pv_done.base + NSA_H)
                    for m in range(2):
                        ins = act.copy(flat(yh[:, 2, 2 * m:2 * m + 2, :]), ps[:, m, :])
                    tell(ins, to_dve2)

            def dve_after(dve):
                dve.wait_ge(to_dve2.sem, to_dve2.base + 1)
                for m in range(2):
                    dve.tensor_tensor(flat(yl[:, 2, 2 * m:2 * m + 2, :]), ps[:, m, :],
                                      flat(yh[:, 2, 2 * m:2 * m + 2, :]).bitcast(F32), ALU.subtract)

            mix.take(turns)
            with new_block() as block:
                @block.sync
                def _(sp):
                    mix.sync(sp)

                attention(block, 2 * NSA_H, lambda i, t: query_half(i // 2, qk, t),
                          lambda i, n: qk[i // 2 % 2 * NSA_DH:(i // 2 % 2 + 1) * NSA_DH, 6 + 2 * (i % 2) + i // 8, 0:n],
                          lambda i: C("causal_neg"), lambda i: gate4[:, :, i // 2, 1 + i % 2],
                          small, prob, turned, values, act_after, dve_after, mix)

        ada_full = [sem(f"ada_full{i}") for i in range(2)]
        c_loaded = sem("c_loaded")
        ada_used = signal("ada_used")
        ADA = 6 * KD

        class Modulation:

            def __init__(self, layer, scope):
                self.layer = layer
                self.rows = sb("ada_rows", [P, 2, D], scope)
                self.c = sb("c_act", [P, D], scope)
                self.now = sb("mod_now", [P, ADA], scope)
                self.dealt = self.loads = 0

            def sync(self, sp, upto):
                if self.loads == 0:
                    sp.dma_start(self.c[:, :], c_in).then_inc(c_loaded, 16)
                for i in range(self.loads, min(upto + 2, ADA)):
                    self.loads = i + 1
                    if i >= 2:
                        sp.wait_ge(ada_used.sem, i - 1)
                    sp.dma_start(self.rows[:, i % 2, :], ada_in[bass.ds(self.layer * ADA + i, 1), :, :]
                                   .rearrange("o p n -> p (o n)")).then_inc(ada_full[i % 2], 16)

            def scalar(self, act):
                act.wait_ge(c_loaded, 16)
                tell(act.activation(self.c[:, :], self.c[:, :], ACT.Silu), c_ready)

            def vector(self, dve, upto):
                for i in range(self.dealt, min(upto, ADA)):
                    if i == 0:
                        dve.wait_ge(c_ready.sem, c_ready.base + 1)
                    dve.wait_ge(ada_full[i % 2], 16 * (i // 2 + 1))
                    r = self.rows[:, i % 2, :]
                    dve.scalar_tensor_tensor(r, r, 1.0, self.c[:, :], ALU.mult, ALU.mult,
                                             accum_out=self.now[:, i:i + 1]).then_inc(ada_used.sem, ada_used.one())
                    self.dealt = i + 1

            def finish(self, dve):
                dve.wait_ge(ada_used.sem, ADA)
                at, _ = PAR2["ada_b0"]
                both = par2[:, at:at + 2 * ADA].rearrange("p (l n) -> p l n", l=2)
                dve.tensor_tensor(mod[:, bass.ds(self.layer, 1), :], self.now[:, :].unsqueeze(1),
                                  both[:, bass.ds(self.layer, 1), :], ALU.add)

        IN_SWIGLU = 32

        def swiglu_hidden(fh, fl, mods):
            w = ring.claim(2 * KF)
            prod = Product(w, 0, 2 * KF, KD, banks)
            sqf = flat(sq[:, :, :])
            buf = lambda i: sqf[:, i % 4 * BANK:(i % 4 + 1) * BANK]
            with new_block() as block:
                @block.sync
                def _(sp):
                    for i in range(w.n):
                        mods.sync(sp, min(i // 4 * 3 + min(i % 4, 2), IN_SWIGLU))
                        w.sync(sp, [i])

                @block.tensor
                def _(pe):
                    for j in range(KF):
                        prod.tensor(pe, h, j)

                @block.scalar
                def _(act):
                    mods.scalar(act)
                    for i in range(KF // 2):
                        w.scalar(act, 4 * i)
                        acc = prod.wait(act, 2 * i)
                        if i >= 4:
                            act.wait_ge(to_act.sem, to_act.base + i - 3)
                        act.activation(buf(i), acc, ACT.Silu).then_inc(prod.read(2 * i), 1)
                        for u in range(1, 4):
                            w.scalar(act, 4 * i + u)
                        prod.after_read(act, 2 * i + 1)
                        tell(act.copy(flat(fh[:, 2 * i:2 * i + 2, :]), buf(i)), to_dve)

                @block.vector
                def _(dve):
                    for i in range(KF // 2):
                        for u in range(3):
                            w.vector(dve, 4 * i + u)
                            mods.vector(dve, min(3 * i + u, IN_SWIGLU))
                        acc = prod.wait(dve, 2 * i + 1)
                        prod.after_read(dve, 2 * i)
                        dve.tensor_tensor(buf(i), buf(i), acc, ALU.mult).then_inc(prod.read(2 * i + 1), 1)
                        w.vector(dve, 4 * i + 3)
                        dve.wait_ge(to_dve.sem, to_dve.base + i + 1)
                        tell(dve.tensor_tensor(flat(fl[:, 2 * i:2 * i + 2, :]), buf(i),
                                               flat(fh[:, 2 * i:2 * i + 2, :]).bitcast(F32), ALU.subtract), to_act)
                    mods.vector(dve, IN_SWIGLU)

        def skip_fillers():
            w = ring.claim(3)
            with new_block() as block:
                @block.sync
                def _(sp):
                    w.sync(sp)

                @block.tensor
                def _(pe):
                    for i in range(w.n):
                        hi, _ = w.arrived(pe, i)
                        pe.matmul(ps[:, 5, 0:P], hi[:, 0:P], hi[:, 0:P], start=True, stop=True) \
                            .then_inc(ring.unit_done.sem, 1)

                @block.scalar
                def _(act):
                    for i in range(w.n):
                        w.scalar(act, i)

                @block.vector
                def _(dve):
                    for i in range(w.n):
                        w.vector(dve, i)

        restart_counts()
        restart_ring()
        with nc.Fori(0, DEPTH) as layer:
            ring.place, ring.base = 0, layer * N_U1
            with new_block() as block:
                @block.scalar
                def _(act):
                    act.dma_start(par1[:, :], par1_in[bass.ds(layer, 1), :, :].rearrange("o p n -> p (o n)")) \
                        .then_inc(par_loaded, 16)
                    act.wait_ge(par_loaded, 16)
            rms_norm(P1("norm1"))
            proj = Projections()
            project(proj, 4)
            prepare_hgrn(layer, proj, 3)
            linear_attention(hq, hk, hv, hf, HG_H, HG_D, hog, P1("hg_norm"), 0, proj, 6, 2)
            prepare_gla(proj, 1)
            linear_attention(gq, gk, gv, gg, GLA_H * GLA_DK // P, GLA_DK, gog, P1("gla_norm"), 1, proj, 4, 2)
            assert proj.mine.stop == len(proj.pairs)
            mix = Mix()
            mix.claim(3)
            windows = ring.claim(4)
            mix.claim(mix.turns - 3)
            rope(mix, 1)
            compress(windows, mix, 2)
            compressed_probabilities(mix, 1)
            sparse_attention(mix, 4)
            mix_rest(mix, 4)
            branches.close()
            ffn = ExitStack()
            fh = sb("ffn_high", [P, KF, T], ffn, F32R)
            fl = sb("ffn_low", [P, KF, T], ffn, F32R)
            mods = Modulation(layer, ffn)
            residual_product(8, KD, h)
            rms_norm(P1("norm2"))
            swiglu_hidden(fh, fl, mods)
            residual_product(22, KF, (fh, fl), mods=mods)
            skip_fillers()
            ffn.close()
            restart_counts()
            restart_ring()
        rms_norm(P2("final_1"), out=xT)
        hybrid.close()

        ring.place, ring.base, ring.limit = 0, DEPTH * N_U1, N_U2
        adaln = everywhere.enter_context(ExitStack())
        hT = sb("hT", [P, KD, T], adaln)
        mgain = sb("mgain", [P, 4, KD], adaln)
        logits = sb("logits", [P, TT, RT], adaln)
        rtmp = sb("rtmp", [P, TT, 80], adaln)
        combine = sb("combine", [P, TT, E_N], adaln)

        def modulated_gains():
            with new_block() as block:
                @block.vector
                def _(dve):
                    for l in range(2):
                        for i, scale_at in enumerate((8, 32)):
                            dve.scalar_tensor_tensor(mgain[:, 2 * l + i, :], mod[:, l, scale_at:scale_at + 8], 1.0,
                                                     P2(f"norm{i + 1}_{l}"), ALU.add, ALU.mult)

        def shift(l, i):
            return mod[:, l, 24 * i:24 * i + 8]

        def gate(l, i):
            return mod[:, l, 24 * i + 16:24 * i + 24]

        def pool_and_chunk_attention():
            pa = ExitStack()
            u = sb("u", [P, 3, 4, T], pa)
            q = sb("q", [P, 4, T], pa)
            k = sb("k", [P, 4, T], pa)
            v = sb("v", [P, TT, 512], pa)
            mean = sb("mean", [P, 2, 4, T], pa)
            cath = sb("cat_high", [P, KD, T], pa, F32R)
            catl = sb("cat_low", [P, KD, T], pa, F32R)
            bias = sb("bias", [P, ATT_H, 3 * P], pa)
            rev = sb("rev", [P, ATT_H, 3 * P], pa)
            probs = sb("probs", [P, 2, 3 * P], pa)
            w = ring.claim(16)
            prods = [Product(w, 4 * BLOCKS * i, 4, KD, banks, token_major=(i == 3)) for i in range(4)]
            with new_block() as block:
                @block.sync
                def _(sp):
                    w.sync(sp)

                @block.tensor
                def _(pe):
                    for prod in prods:
                        for j in range(2):
                            prod.tensor(pe, h, j)

                @block.vector
                def _(dve):
                    for prod, dst in zip(prods, (u[:, 0, :, :], q, k, v)):
                        for j in range(2):
                            units = list(prod.units_of(j))
                            w.vector(dve, units[0])
                            acc = prod.wait(dve, j).rearrange("p (m t) -> p m t", m=2)
                            to = dst[:, :, j * T:(j + 1) * T] if dst is v else dst[:, 2 * j:2 * j + 2, :]
                            dve.tensor_copy(to, acc).then_inc(prod.read(j), 1)
                            w.vector(dve, units[1])

                @block.scalar
                def _(act):
                    for h in range(ATT_H):
                        for lo, n, first in ((0, P, REL - (P - 1)), (P, 2 * P, REL + P - (T - 1))):
                            row = bias_in[h, first:first + P + n - 1]
                            src = bass.AP(tensor=row.tensor, offset=row.offset, ap=[[1, P], [1, n]])
                            act.dma_start(rev[:, h, lo:lo + n], src).then_inc(loaded, 16)
                    for i in range(w.n):
                        w.scalar(act, i)
                    act.wait_ge(loaded, 16 * (4 + 2 * ATT_H))
            with new_block() as block:
                @block.vector
                def _(dve):
                    done = InOrder(dve, dve_step)
                    for lo, n in ((0, P), (P, 2 * P)):
                        ins = dve.tensor_copy(bias[:, :, lo:lo + n], rev[:, :, lo:lo + n][:, :, ::-1])
                    done(ins)
                    for lo in (0, 2 * P):
                        dve.tensor_tensor(bias[:, :, lo:lo + P], bias[:, :, lo:lo + P],
                                          C("chunk_neg").unsqueeze(1).broadcast_to([P, ATT_H, P]), ALU.add)
                    for d in range(4):
                        s = 1 << d
                        src, dst = u[:, 0 if d == 0 else 1 + (d - 1) % 2, :, :], u[:, 1 + d % 2, :, :]
                        dve.tensor_tensor(dst[:, d:4, s:T], src[:, d:4, s:T], src[:, d:4, 0:T - s], ALU.add)
                        done(dve.tensor_copy(dst[:, d:4, 0:s], src[:, d:4, 0:s]))
                        win = dst[:, d, :]
                        done(dve.tensor_tensor(mean[:, 0, d, 0:16], win[:, 0:16], C("count", 16 * d, 16), ALU.mult))
                        done(dve.tensor_copy(mean[:, 0, d, 16:T], win[:, 16:T]))
                        done(dve.scalar_tensor_tensor(mean[:, 1, d, :], mean[:, 0, d, :], 1.0 / POOL_WINDOWS[d],
                                                      u[:, 0, d, :], ALU.mult, ALU.subtract))
                    tell(dve.memset(small[:, 0, 0:1], 0.0), to_pe)
                    dve.wait_ge(to_dve.sem, to_dve.base + 1)
                    for d in range(4):
                        tell(dve.tensor_scalar(mean[:, 0, d, :], ps[:, 4 + d // 2, d % 2 * T:(d % 2 + 1) * T],
                                               P2("pool_scale")[:, d:d + 1], None, ALU.mult), to_act)
                    for d in range(4):
                        dve.wait_ge(to_dve.sem, to_dve.base + d + 2)
                        dve.tensor_tensor(catl[:, d, :], mean[:, 0, d, :], cath[:, d, :].bitcast(F32), ALU.subtract)

                @block.scalar
                def _(act):
                    for d in range(4):
                        act.wait_ge(to_act.sem, to_act.base + d + 1)
                        tell(act.copy(cath[:, d, :], mean[:, 0, d, :]), to_dve)

                @block.tensor
                def _(pe):
                    pe.wait_ge(to_pe.sem, to_pe.base + 1)
                    for d in range(4):
                        ins = pe.matmul(ps[:, 4 + d // 2, d % 2 * T:(d % 2 + 1) * T], P2("pool_w")[:, d * P:(d + 1) * P],
                                        mean[:, 1, d, :], start=True, stop=True)
                    tell(ins, to_dve)
            sqf = flat(sq[:, :, :])
            turned = lambda i: sqf[:, i % 4 * BANK:i % 4 * BANK + 3 * P]

            def values(pe, h):
                lo = h % 2 * ATT_DH
                pe.wait_ge(pt_ready.sem, pt_ready.base + h + 1)
                for t in range(TT):
                    for s in range(t + 1):
                        ins = pe.matmul(ps[lo:lo + ATT_DH, h // 2, t * P:(t + 1) * P], v[:, s, h * ATT_DH:(h + 1) * ATT_DH],
                                        turned(h)[:, (t + s) * P:(t + s + 1) * P], start=(s == 0), stop=(s == t))
                tell(ins, pv_done)

            def act_after(act, i):
                if 4 <= i < ATT_H:
                    act.wait_ge(pv_done.sem, pv_done.base + i - 3)
                if i == ATT_H:
                    act.wait_ge(pv_done.sem, pv_done.base + ATT_H)
                    for m in range(4):
                        ins = act.copy(cath[:, 4 + m, :], ps[:, m, 0:T])
                    tell(ins, to_dve2)

            def dve_after(dve):
                dve.wait_ge(to_dve2.sem, to_dve2.base + 1)
                for m in range(4):
                    dve.tensor_tensor(catl[:, 4 + m, :], ps[:, m, 0:T], cath[:, 4 + m, :].bitcast(F32), ALU.subtract)

            with new_block() as block:
                attention(block, ATT_H, lambda i, t: query_half(i, q, t),
                          lambda i, n: k[i % 2 * ATT_DH:(i % 2 + 1) * ATT_DH, i // 2, 0:n],
                          lambda i: bias[:, i, :], lambda i: None, small, [probs[:, 0, :], probs[:, 1, :]], turned,
                          values, act_after, dve_after)
            residual_product(8, KD, (cath, catl), gate(0, 0))
            pa.close()

        def router(l):
            parts = [0]

            def scratch(n):
                parts[0] += n
                return rtmp[:, :, parts[0] - n:parts[0]]

            glog, elog = logits[:, :, 0:E_G], logits[:, :, E_G:RT]
            gmax, gexp, gsum, gcand, gleast, ghot = (scratch(n) for n in (1, E_G, 1, E_G, 1, E_G))
            esel, emax, cand, least, hot1, hot2, rest, top1, top2, share = (
                scratch(n) for n in (E_PER, 1, E_PER, 1, E_PER, E_PER, E_PER, 1, 1, 1))
            weigh, weigh2 = scratch(E_PER), scratch(E_PER)

            def wide(a, n):
                return a.broadcast_to([P, TT, n])

            with new_block() as block:
                @block.tensor
                def _(pe):
                    for t in range(TT):
                        for k in range(KD):
                            ins = pe.matmul(ps[:, 4, t * RT:(t + 1) * RT], hT[:, k, t * P:(t + 1) * P],
                                            P2(f"router_{l}")[:, k * RT:(k + 1) * RT], start=(k == 0), stop=(k == KD - 1))
                    tell(ins, to_dve)

                @block.scalar
                def _(act):
                    act.wait_ge(to_act.sem, to_act.base + 1)
                    tell(act.activation(gexp, gexp, ACT.Exp), to_dve)
                    act.wait_ge(to_act.sem, to_act.base + 2)
                    tell(act.activation(esel, esel, ACT.Exp), to_dve)

                @block.vector
                def _(dve):
                    done = InOrder(dve, dve_step)

                    def first_maximum(a, most, candidates, smallest, onehot, n):
                        done(dve.tensor_reduce(most, a, AX_X, ALU.max))
                        done(dve.tensor_tensor(candidates, a, wide(most, n), ALU.is_equal))
                        iota = C(f"iota{n}").unsqueeze(1).broadcast_to([P, TT, n])
                        done(dve.scalar_tensor_tensor(candidates, candidates, -64.0, iota, ALU.mult, ALU.add))
                        done(dve.tensor_reduce(smallest, candidates, AX_X, ALU.min))
                        done(dve.tensor_tensor(onehot, candidates, wide(smallest, n), ALU.is_equal))

                    dve.wait_ge(to_dve.sem, to_dve.base + 1)
                    done(dve.tensor_tensor(logits[:, :, :], ps[:, 4, 0:TT * RT].rearrange("p (t n) -> p t n", t=TT),
                                           P2(f"router_b{l}").unsqueeze(1).broadcast_to([P, TT, RT]), ALU.add))
                    done(dve.tensor_reduce(gmax, glog, AX_X, ALU.max))
                    tell(dve.tensor_tensor(gexp, glog, wide(gmax, E_G), ALU.subtract), to_act)
                    dve.wait_ge(to_dve.sem, to_dve.base + 2)
                    done(dve.tensor_reduce(gsum, gexp, AX_X, ALU.add))
                    first_maximum(gexp, gmax, gcand, gleast, ghot, E_G)
                    chosen = combine[:, :, :].rearrange("p t (g e) -> p t g e", g=E_G)
                    done(dve.tensor_tensor(chosen, elog.rearrange("p t (g e) -> p t g e", g=E_G),
                                           ghot.unsqueeze(3).broadcast_to([P, TT, E_G, E_PER]), ALU.mult))
                    done(dve.tensor_reduce(esel, chosen.rearrange("p t g e -> p t e g"), AX_X, ALU.add))
                    done(dve.tensor_reduce(emax, esel, AX_X, ALU.max))
                    tell(dve.tensor_tensor(esel, esel, wide(emax, E_PER), ALU.subtract), to_act)
                    dve.wait_ge(to_dve.sem, to_dve.base + 3)
                    first_maximum(esel, top1, cand, least, hot1, E_PER)
                    done(dve.scalar_tensor_tensor(rest, hot1, -2.0, esel, ALU.mult, ALU.add))
                    first_maximum(rest, top2, cand, least, hot2, E_PER)
                    done(dve.tensor_tensor(share, top1, top2, ALU.add))
                    done(dve.tensor_tensor(share, share, gsum, ALU.mult))
                    done(dve.reciprocal(share, share))
                    done(dve.tensor_tensor(share, share, gmax, ALU.mult))
                    dve.tensor_tensor(weigh, hot1, wide(top1, E_PER), ALU.mult)
                    done(dve.tensor_tensor(weigh2, hot2, wide(top2, E_PER), ALU.mult))
                    done(dve.tensor_tensor(weigh, weigh, weigh2, ALU.add))
                    done(dve.tensor_tensor(weigh, weigh, wide(share, E_PER), ALU.mult))
                    dve.tensor_tensor(chosen, ghot.unsqueeze(3).broadcast_to([P, TT, E_G, E_PER]),
                                      weigh.unsqueeze(2).broadcast_to([P, TT, E_G, E_PER]), ALU.mult)

        hidden_done, silu_done, zeros_ready, product_step, weighed, hidden_high = (
            signal(n) for n in ("hidden_done", "silu_done", "zeros_ready", "silu_times_up",
                                "hidden_weighed", "hidden_high"))
        comb_t = sb("combine_t", [E_N, T], adaln)
        comb_h = sb("combine_high", [E_N, T], adaln, F32R)
        comb_l = sb("combine_low", [E_N, T], adaln, F32R)
        eye = sb("eye", [E_N, E_N], adaln, F32R)

        def spread_weights(weight):
            with new_block() as block:
                @block.tensor
                def _(pe):
                    for t in range(TT):
                        ins = pe.transpose(ps[0:E_N, 4, t * P:(t + 1) * P], combine[:, t, :], ident)
                    tell(ins, to_dve)
                    pe.wait_ge(to_pe.sem, to_pe.base + 1)
                    for e in range(E_N):
                        b = e // 2
                        if e % 2 == 0 and b >= 4:
                            pe.wait_ge(banks_read[b % 2].sem, banks_read[b % 2].base + (b - 4) // 2 + 1)
                        o = ps[:, b % 4, e % 2 * T:(e % 2 + 1) * T]
                        one = eye[:, e:e + 1].broadcast_to([E_N, P])
                        pe.matmul(o, one, comb_h[:, :], start=True, stop=False)
                        ins = pe.matmul(o, one, comb_l[:, :], start=False, stop=True)
                        if e % 2:
                            tell(ins, score_done)

                @block.scalar
                def _(act):
                    act.copy(eye[:, :], ident[0:E_N, 0:E_N])
                    act.wait_ge(to_act.sem, to_act.base + 1)
                    tell(act.copy(comb_h[:, :], comb_t[:, :]), to_dve)
                    for b in range(0, E_N // 2, 2):
                        act.wait_ge(score_done.sem, score_done.base + b + 1)
                        tell(act.copy(flat(weight[:, 2 * b:2 * b + 2, :]), ps[:, b % 4, :]), banks_read[0])

                @block.vector
                def _(dve):
                    dve.wait_ge(to_dve.sem, to_dve.base + 1)
                    tell(dve.tensor_copy(comb_t[:, :], ps[0:E_N, 4, 0:T]), to_act)
                    dve.wait_ge(to_dve.sem, to_dve.base + 2)
                    tell(dve.tensor_tensor(comb_l[:, :], comb_t[:, :], comb_h[:, :].bitcast(F32), ALU.subtract), to_pe)
                    for b in range(1, E_N // 2, 2):
                        dve.wait_ge(score_done.sem, score_done.base + b + 1)
                        tell(dve.tensor_copy(flat(weight[:, 2 * b:2 * b + 2, :]), ps[:, b % 4, :]), banks_read[1])

        banks_read = [to_pe2, pt_ready]
        hidh = sb("hidden_high_half", [P, 2, T], adaln, F32R)
        hidl = sb("hidden_low_half", [P, 2, T], adaln, F32R)

        def experts(l, last, weight):
            some = 8
            turns, per, per_slot = E_N // some, 3 * some, 3 * some // RING
            first, loads = ring.place, list(ring.loads)
            unit0, high0, split0 = ring.unit_done.n, ring.high_done.n, ring.split.n
            hid0, silu0, col0, prod0 = hidden_done.n, silu_done.n, zeros_ready.n, product_step.n
            weighed0, hhigh0 = weighed.n, hidden_high.n
            slot = lambda k: (first + k) % RING
            hidden = [sq[:, j, :] for j in range(2)]
            looped = turns - 1 if last else turns

            def more(i, k, ahead):
                return not isinstance(i, int) or first + i * per + k + ahead * RING < ring.limit

            with new_block() as block:
                @block.sync
                def _(sp):
                    def turn(i):
                        for k in range(per):
                            if more(i, k, 2):
                                sp.wait_ge(ring.split.sem, i * per + (split0 + k + 1))
                                ring.load(sp, i * per + (ring.base + first + k + 2 * RING), slot(k))

                    with sp.Fori(0, looped) as i:
                        turn(i)
                    if last:
                        turn(looped)
                    else:
                        sp.wait_ge(ring.split.sem, split0 + turns * per + 1)
                        ring.load(sp, ring.base + first + turns * per + 2 * RING, slot(0))

                @block.tensor
                def _(pe):
                    pe.wait_ge(zeros_ready.sem, col0 + 1)
                    for b in range(4):
                        pe.matmul(ps[:, 4 + b, :], ones, flat(sq[:, 4:6, :]), start=True, stop=True,
                                  skip_group_check=True)
                    def halves(i, k):
                        pe.wait_ge(ring.split.sem, i * per + (split0 - RING + k + 1))
                        return high[:, slot(k), :], low[:, slot(k), :]

                    def down(i, j):
                        pe.wait_ge(hidden_done.sem, i * some + (hid0 + 1 + j + 1))
                        w = halves(i, 3 * j + 2 if j < some else per)
                        for m in range(KD):
                            ins = three_products(pe, ps[:, 4 + m // 2, m % 2 * T:(m % 2 + 1) * T],
                                                 [a[:, m * P:(m + 1) * P] for a in w],
                                                 (hidh[:, (j + 1) % 2, :], hidl[:, (j + 1) % 2, :]), False, False,
                                                 skip_group_check=True)
                        ins.then_inc(ring.unit_done.sem, 1)

                    with pe.Fori(0, turns) as i:

                        def up(j):
                            pe.wait_ge(hidden_done.sem, i * some + (hid0 + j + 1))
                            for m in range(2):
                                w = halves(i, 3 * j + m)
                                for k in range(KD):
                                    ins = three_products(pe, ps[:, j % 2, m * T:(m + 1) * T],
                                                         [a[:, k * P:(k + 1) * P] for a in w], (hh[:, k, :], hl[:, k, :]),
                                                         k == 0, k == KD - 1)
                                ins.then_inc(ring.unit_done.sem, 1)

                        for j in range(some):
                            up(j)
                            down(i, j)
                    down(turns - 1, some)

                @block.scalar
                def _(act):
                    def next_high(i, k):
                        if more(i, k, 1):
                            s = slot(k)
                            act.wait_ge(ring.unit_done.sem, i * per + (unit0 + k + 1))
                            act.wait_ge(ring.raw_full[s], i * (16 * per_slot) + 16 * (loads[s] + k // RING + 1))
                            ring.round_high(act, s).then_inc(ring.high_done.sem, 1)

                    def turn(i):
                        for j in range(some):
                            k = 3 * j
                            next_high(i, k)
                            act.wait_ge(ring.unit_done.sem, i * per + (unit0 + k + 2))
                            act.wait_ge(hidden_done.sem, i * some + (hid0 + j + 1))
                            act.activation(hidden[j % 2], ps[:, j % 2, 0:T], ACT.Silu).then_inc(silu_done.sem, 1)
                            next_high(i, k + 1)
                            act.wait_ge(weighed.sem, i * some + (weighed0 + j + 1))
                            act.wait_ge(ring.unit_done.sem, i * per + (unit0 + k))
                            act.copy(hidh[:, j % 2, :], hidden[j % 2]).then_inc(hidden_high.sem, 1)
                            next_high(i, k + 2)

                    with act.Fori(0, looped) as i:
                        turn(i)
                    if last:
                        turn(looped)
                    else:
                        next_high(turns - 1, per)

                @block.vector
                def _(dve):
                    dve.memset(sq[:, 4:6, :], 0.0).then_inc(zeros_ready.sem, 1)
                    dve.memset(small[:, 0, 0:1], 0.0).then_inc(hidden_done.sem, 1)
                    dve.wait_ge(zeros_ready.sem, col0 + 1)
                    for half in (hidh, hidl):
                        ins = dve.tensor_copy(half[:, 1, :], sq[:, 4, :])
                    ins.then_inc(hidden_done.sem, 1)

                    def next_low(i, k):
                        if more(i, k, 1):
                            dve.wait_ge(ring.high_done.sem, i * per + (high0 + k + 1))
                            ring.take_low(dve, slot(k)).then_inc(ring.split.sem, 1)

                    def turn(i):
                        for j in range(some):
                            next_low(i, 3 * j)
                            dve.wait_ge(silu_done.sem, i * some + (silu0 + j + 1))
                            dve.tensor_tensor(hidden[j % 2], hidden[j % 2], ps[:, j % 2, T:2 * T], ALU.mult) \
                                .then_inc(product_step.sem, 1)
                            dve.wait_ge(product_step.sem, i * some + (prod0 + j + 1))
                            dve.tensor_tensor(hidden[j % 2], hidden[j % 2], weight[:, bass.ds(i * some + j, 1), :]
                                              .rearrange("p o t -> p (o t)"), ALU.mult) \
                                .then_inc(weighed.sem, 1)
                            next_low(i, 3 * j + 1)
                            dve.wait_ge(hidden_high.sem, i * some + (hhigh0 + j + 1))
                            dve.tensor_tensor(hidl[:, j % 2, :], hidden[j % 2], hidh[:, j % 2, :].bitcast(F32),
                                              ALU.subtract).then_inc(hidden_done.sem, 1)
                            next_low(i, 3 * j + 2)

                    with dve.Fori(0, looped) as i:
                        turn(i)
                    if last:
                        turn(looped)
                    else:
                        next_low(turns - 1, per)
                    dve.wait_ge(ring.unit_done.sem, unit0 + turns * per + 1)
                    for m in range(KD):
                        dve.scalar_tensor_tensor(xT[:, m, :], ps[:, 4 + m // 2, m % 2 * T:(m % 2 + 1) * T],
                                                 gate(l, 1)[:, m:m + 1], xT[:, m, :], ALU.mult, ALU.add)
            for count, n in ((ring.unit_done, turns * per + 1), (ring.split, turns * per + 1),
                             (ring.high_done, turns * per + 1),
                             (hidden_done, 2 + E_N), (silu_done, E_N), (zeros_ready, 1),
                             (product_step, E_N), (weighed, E_N), (hidden_high, E_N)):
                count.n += n
            ring.place += turns * per + 1
            ring.loads = [n + turns * per_slot + (s == slot(0)) for s, n in enumerate(loads)]

        def mamba():
            mb = ExitStack()
            z = sb("z", [P, KS, T], mb)
            inner = mb.enter_context(ExitStack())
            xbc = sb("xbc", [P, KX, T], inner)
            xdt = sb("xdt", [P, TT, SSM_IN], inner)
            cv = sb("cv", [P, 2, 2, T], inner)
            dt = sb("dt", [P, TT, SSM_H], inner)
            a = sb("a", [P, TT, SSM_H], inner)
            acs = sb("acs", [P, TT, SSM_H], inner)
            soft = sb("soft", [P, TT * SSM_H], inner)
            cbm = sb("cbm", [P, 2, 3 * P], inner)
            seg = sb("seg", [P, 4, 3 * P], inner)
            yt = sb("yt", [P, 2, T], inner)
            w = ring.claim(48)
            prod = Product(w, 0, KS + KX, KD, banks)
            conv_w = P2("conv_w").rearrange("p (i c) -> p i c", i=SSM_CONV)
            with new_block() as block:
                @block.sync
                def _(sp):
                    w.sync(sp)

                @block.tensor
                def _(pe):
                    for j in range(24):
                        prod.tensor(pe, h, j)

                @block.vector
                def _(dve):
                    done = InOrder(dve, dve_step)
                    for i in range(16):
                        w.vector(dve, i)
                    for j in range(KX // 2):
                        w.vector(dve, 16 + 2 * j)
                        acc = prod.wait(dve, 8 + j)
                        buf = cv[:, j % 2, :, :]
                        dve.wait_ge(to_dve2.sem, to_dve2.base + j + 1)
                        for s in range(1, SSM_CONV):
                            if s > 1:
                                done(ins)
                            for m in range(2):
                                ins = dve.scalar_tensor_tensor(
                                    buf[:, m, s:T], acc[:, m * T:(m + 1) * T - s],
                                    conv_w[:, SSM_CONV - 1 - s, 2 * j + m:2 * j + m + 1], buf[:, m, s:T],
                                    ALU.mult, ALU.add)
                        ins.then_inc(prod.read(8 + j), 1)
                        w.vector(dve, 17 + 2 * j)

                @block.scalar
                def _(act):
                    for j in range(8):
                        w.scalar(act, 2 * j)
                        acc = prod.wait(act, j)
                        act.activation(flat(z[:, 2 * j:2 * j + 2, :]), acc, ACT.Silu).then_inc(prod.read(j), 1)
                        w.scalar(act, 2 * j + 1)
                    for j in range(KX // 2):
                        w.scalar(act, 16 + 2 * j)
                        acc = prod.wait(act, 8 + j)
                        if j >= 2:
                            act.wait_ge(to_dve.sem, to_dve.base + j - 1)
                        for m in range(2):
                            ins = act.activation(cv[:, j % 2, m, :], acc[:, m * T:(m + 1) * T], ACT.Copy,
                                                 scale=conv_w[:, SSM_CONV - 1, 2 * j + m:2 * j + m + 1])
                        tell(ins, to_dve2)
                        w.scalar(act, 17 + 2 * j)
                        prod.after_read(act, 8 + j)
                        for m in range(2):
                            c = 2 * j + m
                            ins = act.activation(xbc[:, c, :], cv[:, j % 2, m, :], ACT.Silu,
                                                 bias=P2("conv_b")[:, c:c + 1])
                        tell(ins, to_dve)

            with new_block() as block:
                @block.tensor
                def _(pe):
                    for t in range(TT):
                        for k in range(KD):
                            ins = pe.matmul(ps[:, 4, t * SSM_H:(t + 1) * SSM_H], hT[:, k, t * P:(t + 1) * P],
                                            P2("w_dt")[:, k * SSM_H:(k + 1) * SSM_H], start=(k == 0), stop=(k == KD - 1))
                    tell(ins, to_dve)
                    pe.wait_ge(to_pe.sem, to_pe.base + 1)
                    pe.matmul(ps[:, 5, 0:SSM_H], C("upper", 0, P), a[:, 0, :], start=True, stop=True)
                    pe.matmul(ps[:, 5, SSM_H:2 * SSM_H], ones, a[:, 0, :], start=True, stop=False)
                    ins = pe.matmul(ps[:, 5, SSM_H:2 * SSM_H], C("upper", 0, P), a[:, 1, :], start=False, stop=True)
                    tell(ins, to_dve)

                @block.scalar
                def _(act):
                    log_sigmoid_tail(act, soft[:, :], (to_act.sem, to_act.base + 1), to_dve2)
                    tell(act.activation(acs[:, 0, :], P2("a_log"), ACT.Exp), to_dve2)

                @block.vector
                def _(dve):
                    done = InOrder(dve, dve_step)
                    dve.wait_ge(to_dve.sem, to_dve.base + 1)
                    for t in range(TT):
                        ins = dve.tensor_tensor(dt[:, t, :], ps[:, 4, t * SSM_H:(t + 1) * SSM_H], P2("dt_b"), ALU.add)
                    done(ins)
                    tell(dve.tensor_copy(soft[:, :], flat(dt[:, :, :])), to_act)
                    dve.wait_ge(to_dve2.sem, to_dve2.base + 2)
                    done(dve.scalar_tensor_tensor(flat(dt[:, :, :]), flat(dt[:, :, :]), 0.0, soft[:, :], ALU.max, ALU.add))
                    for t in range(TT):
                        ins = dve.scalar_tensor_tensor(a[:, t, :], dt[:, t, :], -1.0, acs[:, 0, :], ALU.mult, ALU.mult)
                    tell(ins, to_pe)
                    dve.wait_ge(to_dve.sem, to_dve.base + 2)
                    dve.tensor_copy(flat(acs[:, :, :]), ps[:, 5, 0:2 * SSM_H])

            rounds = [(c4, t) for c4 in range(KS // 4) for t in range(TT)]
            with new_block() as block:
                @block.tensor
                def _(pe):
                    for n, (c4, t) in enumerate(rounds):
                        if n >= 4:
                            pe.wait_ge(to_pe.sem, to_pe.base + n - 3)
                        for m in range(4):
                            ins = pe.transpose(ps[:, 4 + n % 4, m * P:(m + 1) * P],
                                               xbc[:, 4 * c4 + m, t * P:(t + 1) * P], ident)
                        tell(ins, to_dve)

                @block.vector
                def _(dve):
                    for n, (c4, t) in enumerate(rounds):
                        dve.wait_ge(to_dve.sem, to_dve.base + n + 1)
                        heads = BANK // SSM_P
                        tell(dve.tensor_tensor(
                            xdt[:, t, c4 * BANK:(c4 + 1) * BANK].rearrange("p (h n) -> p h n", n=SSM_P),
                            ps[:, 4 + n % 4, :].rearrange("p (h n) -> p h n", n=SSM_P),
                            dt[:, t, c4 * heads:(c4 + 1) * heads].unsqueeze(2).broadcast_to([P, heads, SSM_P]),
                            ALU.mult), to_pe)

            per = SSM_H // SSM_G
            cb_done, cb_read, bc_done, seg_ready, exp_done, m_ready, y_done, y_read = (
                pt_done, pt_ready, score_done, to_act, to_dve, prob_ready, pv_done, to_pe2)
            with new_block() as block:
                @block.tensor
                def _(pe):
                    def group(g):
                        if g >= 2:
                            pe.wait_ge(cb_read.sem, cb_read.base + g - 1)
                        B, Cm = xbc[:, KS + g, :], xbc[:, KS + SSM_G + g, :]
                        pe.matmul(ps[:, 4 + g % 2, 0:T], B[:, 0:P], Cm, start=True, stop=True)
                        tell(pe.matmul(ps[:, 4 + g % 2, T:T + P], B[:, P:T], Cm[:, P:T], start=True, stop=True), cb_done)

                    def running_sum(h):
                        if h >= 2:
                            pe.wait_ge(seg_ready.sem, seg_ready.base + h - 1)
                        o = ps[:, 6 + h % 2, :]
                        pe.matmul(o[:, 0:T], a[:, 0, h:h + 1].broadcast_to([P, P]), C("upper"), start=True, stop=False)
                        tell(pe.matmul(o[:, P:T], a[:, 1, h:h + 1].broadcast_to([P, P]), C("upper", 0, P), start=False,
                                       stop=True), bc_done)

                    def outputs(h):
                        ct, lo = h // 2, h % 2 * SSM_P
                        if ct >= 4 and h % 2 == 0:
                            pe.wait_ge(y_read.sem, y_read.base + ct - 3)
                        pe.wait_ge(m_ready.sem, m_ready.base + h + 1)
                        o = ps[lo:lo + SSM_P, ct % 4, 0:T]
                        cols = slice(h * SSM_P, (h + 1) * SSM_P)
                        pe.matmul(o, xdt[:, 0, cols], seg[:, h % 4, 0:T], start=True, stop=False)
                        tell(pe.matmul(o[:, P:T], xdt[:, 1, cols], seg[:, h % 4, T:T + P], start=False, stop=True), y_done)

                    group(0)
                    running_sum(0)
                    running_sum(1)
                    for h in range(SSM_H):
                        if h + 2 < SSM_H:
                            if (h + 2) % per == 0:
                                group((h + 2) // per)
                            running_sum(h + 2)
                        outputs(h)

                @block.vector
                def _(dve):
                    done = InOrder(dve, dve_step)

                    def exponents(h):
                        g = h // per
                        if h % per == 0:
                            dve.wait_ge(cb_done.sem, cb_done.base + g + 1)
                            if g >= 2:
                                dve.wait_ge(m_ready.sem, m_ready.base + per * (g - 1))
                            tell(dve.tensor_tensor(cbm[:, g % 2, :], ps[:, 4 + g % 2, 0:3 * P], C("ssd"), ALU.mult),
                                 cb_read)
                        dve.wait_ge(bc_done.sem, bc_done.base + h + 1)
                        if h >= 4:
                            dve.wait_ge(y_done.sem, y_done.base + h - 3)
                        o = ps[:, 6 + h % 2, :]
                        dve.tensor_scalar(seg[:, h % 4, 0:T], o[:, 0:T], acs[:, 0, h:h + 1], 0.0, ALU.subtract, ALU.min)
                        tell(dve.tensor_scalar(seg[:, h % 4, T:T + P], o[:, P:T], acs[:, 1, h:h + 1], 0.0, ALU.subtract,
                                               ALU.min), seg_ready)

                    def gated(ct):
                        dve.wait_ge(y_done.sem, y_done.base + 2 * ct + 2)
                        tell(dve.scalar_tensor_tensor(yt[:, ct % 2, :], xbc[:, ct, :], P2("d_skip")[:, ct:ct + 1],
                                                      ps[:, ct % 4, 0:T], ALU.mult, ALU.add), y_read)
                        dve.wait_ge(y_read.sem, y_read.base + ct + 1)
                        done(dve.tensor_tensor(z[:, ct, :], z[:, ct, :], yt[:, ct % 2, :], ALU.mult))

                    exponents(0)
                    for h in range(SSM_H):
                        if h + 1 < SSM_H:
                            exponents(h + 1)
                        dve.wait_ge(exp_done.sem, exp_done.base + h + 1)
                        if h % per == 0:
                            dve.wait_ge(cb_read.sem, cb_read.base + h // per + 1)
                        tell(dve.tensor_tensor(seg[:, h % 4, :], seg[:, h % 4, :], cbm[:, h // per % 2, :], ALU.mult), m_ready)
                        if h % 2 and h >= 3:
                            gated(h // 2 - 1)
                    gated(KS - 1)

                @block.scalar
                def _(act):
                    for h in range(SSM_H):
                        act.wait_ge(seg_ready.sem, seg_ready.base + h + 1)
                        tell(act.activation(seg[:, h % 4, :], seg[:, h % 4, :], ACT.Exp), exp_done)

            sqz = xdt[:, :, :].rearrange("p a b -> p (a b)")
            dev = flat(seg[0:SSM_G, :, :])
            with new_block() as block:
                @block.scalar
                def _(act):
                    for c in range(4):
                        tell(act.activation(sqz[:, c * 4 * T:(c + 1) * 4 * T], flat(z[:, 4 * c:4 * c + 4, :]), ACT.Square),
                             squares)
                    act.wait_ge(variance.sem, variance.base + 1)
                    tell(act.activation(dev[:, T:2 * T], dev[:, 0:T], ACT.Sqrt), deviation)

                @block.tensor
                def _(pe):
                    for c in range(KS):
                        if c % 4 == 0:
                            pe.wait_ge(squares.sem, squares.base + c // 4 + 1)
                        g = c // 2
                        ins = pe.matmul(ps[0:SSM_G, 0, 0:T], C("one_hot", g * SSM_G, SSM_G), sqz[:, c * T:(c + 1) * T],
                                        start=(c == 0), stop=(c == KS - 1))
                    tell(ins, summed)
                    pe.wait_ge(to_pe.sem, to_pe.base + 1)
                    for g in range(SSM_G):
                        ins = pe.matmul(ps[:, 4 + g // 2, g % 2 * T:(g % 2 + 1) * T],
                                        ident[0:SSM_G, g:g + 1].broadcast_to([SSM_G, P]), dev[:, 0:T], start=True,
                                        stop=True)
                        if g % 2:
                            tell(ins, to_dve)

                @block.vector
                def _(dve):
                    dve.wait_ge(summed.sem, summed.base + 1)
                    tell(dve.tensor_scalar(dev[:, 0:T], ps[0:SSM_G, 0, 0:T], 1.0 / (2 * P), EPS, ALU.mult, ALU.add),
                         variance)
                    dve.wait_ge(deviation.sem, deviation.base + 1)
                    tell(dve.reciprocal(dev[:, 0:T], dev[:, T:2 * T]), to_pe)
                    for c in range(KS):
                        if c % 4 == 0:
                            dve.wait_ge(to_dve.sem, to_dve.base + c // 4 + 1)
                        g = c // 2
                        dve.scalar_tensor_tensor(z[:, c, :], z[:, c, :], P2("ssm_norm")[:, c:c + 1],
                                                 ps[:, 4 + g // 2, g % 2 * T:(g % 2 + 1) * T], ALU.mult, ALU.mult)
            inner.close()
            zh = sb("z_high", [P, KS, T], mb, F32R)
            zl = sb("z_low", [P, KS, T], mb, F32R)
            with new_block() as block:
                @block.scalar
                def _(act):
                    for c in range(4):
                        tell(act.copy(zh[:, 4 * c:4 * c + 4, :], z[:, 4 * c:4 * c + 4, :]), to_dve)

                @block.vector
                def _(dve):
                    for c in range(4):
                        dve.wait_ge(to_dve.sem, to_dve.base + c + 1)
                        dve.tensor_tensor(zl[:, 4 * c:4 * c + 4, :], z[:, 4 * c:4 * c + 4, :],
                                          zh[:, 4 * c:4 * c + 4, :].bitcast(F32), ALU.subtract)
            residual_product(16, KS, (zh, zl), gate(1, 0))
            mb.close()

        modulated_gains()
        sum_of_squares()
        rms_norm(mgain[:, 0, :], shift(0, 0))
        pool_and_chunk_attention()
        rms_norm(mgain[:, 1, :], shift(0, 1), out=hT)
        router(0)
        moe = ExitStack()
        weight = sb("weight", [P, E_N, T], moe)
        spread_weights(weight)
        experts(0, False, weight)
        moe.close()
        sum_of_squares()
        rms_norm(mgain[:, 2, :], shift(1, 0), out=hT)
        mamba()
        rms_norm(mgain[:, 3, :], shift(1, 1), out=hT)
        router(1)
        moe = ExitStack()
        weight = sb("weight_1", [P, E_N, T], moe)
        spread_weights(weight)
        experts(1, True, weight)
        moe.close()
        sum_of_squares()
        rms_norm(P2("final"), out=xT)
        with new_block() as block:
            @block.sync
            def _(sp):
                sp.dma_start(out, xT[:, :, :]).then_inc(stored, 16)
                sp.wait_ge(stored, 16)




def kernel(x, norm1_g, w_in, hg_lb, hg_norm_g, gla_w2, gla_b, gla_norm_g, cmp_pos_k, cmp_pos_v,
           cmp_w1_k, cmp_w2_k, cmp_w1_v, cmp_w2_v, w_br_hg, w_br_gla, w_br_nsa, w_out, norm2_g,
           w_ffn_gate, w_ffn_up, w_ffn_down, final_norm_g, c_2, ada_w_2, ada_b_2, norm1_w_2, norm2_w_2,
           mix_w_in_2, pool_w_2, pool_scale_2, rel_bias_2, mix_w_out_2, ssm_w_in_2, ssm_conv_w_2,
           ssm_conv_b_2, ssm_dt_bias_2, ssm_A_log_2, ssm_D_2, ssm_norm_w_2, ssm_w_out_2, moe_w_group_2,
           moe_b_group_2, moe_w_expert_2, moe_b_expert_2, moe_w1_2, moe_w3_2, moe_w2_2, final_norm_w_2):
    import concourse.bacc as bacc
    from concourse.bass_utils import run_bass_kernel_spmd

    A = np.asarray
    fc = lambda v: feature_columns(A(v))
    units = []
    for l in range(DEPTH):
        units += stream_hybrid(*(A(w[l]) for w in (w_in, cmp_w1_k, cmp_w1_v, w_br_hg, w_br_gla, w_br_nsa, w_out,
                                                   w_ffn_gate, w_ffn_up, w_ffn_down)))
    feature = lambda w: units_of(weight_blocks(A(w)))
    mix = A(mix_w_in_2[0])
    ssm = A(ssm_w_in_2[0])
    units += [feature(mix[:, :1536]), token_major_units(mix[:, 1536:]), feature(mix_w_out_2[0]), moe_units(A(moe_w1_2[0]), A(moe_w3_2[0]), A(moe_w2_2[0])),
              feature(ssm[:, :SSM_IN + KX * P]), feature(ssm_w_out_2[0]),
              moe_units(A(moe_w1_2[1]), A(moe_w3_2[1]), A(moe_w2_2[1]))]
    stream = np.concatenate(units)

    def pos(v):
        return A(v).reshape(-1, 2, NSA_DH).transpose(1, 2, 0).reshape(P, -1)

    par1 = np.stack([pack(PAR1, N_PAR1, {
        "norm1": fc(norm1_g[l]), "norm2": fc(norm2_g[l]), "hg_norm": fc(hg_norm_g[l]), "gla_norm": fc(gla_norm_g[l]),
        "gla_b": fc(gla_b[l]), "gla_w2": A(gla_w2[l]), "pos_k": pos(cmp_pos_k[l]), "pos_v": pos(cmp_pos_v[l]),
        "w2_k": np.concatenate([A(cmp_w2_k[l])] * 2, 1), "w2_v": A(cmp_w2_v[l])}) for l in range(DEPTH)])

    def k_major(w):
        return w.reshape(KD, P, -1).transpose(1, 0, 2)

    def router(l):
        return k_major(np.concatenate([A(moe_w_group_2[l]), A(moe_w_expert_2[l]).reshape(D, E_N)], 1))

    def router_bias(l):
        return rows(np.concatenate([A(moe_b_group_2[l]), A(moe_b_expert_2[l]).reshape(-1)]))

    par2 = pack(PAR2, N_PAR2, {
        "norm1_0": fc(norm1_w_2[0]), "norm1_1": fc(norm1_w_2[1]), "norm2_0": fc(norm2_w_2[0]),
        "norm2_1": fc(norm2_w_2[1]), "final": fc(final_norm_w_2), "final_1": fc(final_norm_g),
        "ada_b0": fc(ada_b_2[0]), "ada_b1": fc(ada_b_2[1]), "pool_w": A(pool_w_2[0]).transpose(1, 0, 2),
        "pool_scale": fc(pool_scale_2[0]), "conv_w": np.stack([fc(ssm_conv_w_2[0][i]) for i in range(SSM_CONV)], 1),
        "conv_b": fc(ssm_conv_b_2[0]), "dt_b": rows(A(ssm_dt_bias_2[0])), "a_log": rows(A(ssm_A_log_2[0])),
        "d_skip": fc(np.repeat(A(ssm_D_2[0]), SSM_P)), "ssm_norm": fc(ssm_norm_w_2[0]),
        "w_dt": k_major(ssm[:, SSM_IN + KX * P:]), "router_0": router(0), "router_1": router(1),
        "router_b0": router_bias(0), "router_b1": router_bias(1)})
    arrays = {"stream": stream, "const": constants(), "par1": par1, "par2": par2,
              "lb": np.concatenate([fc(hg_lb[l]) for l in range(DEPTH)], 1), "bias": A(rel_bias_2[0]), "c": rows(A(c_2)),
              "ada": np.concatenate([A(ada_w_2[l]).T.reshape(-1, P, D) for l in range(2)]),
              "xT": A(x)[0].T.reshape(KD, P, T).transpose(1, 0, 2)}
    nc = bacc.Bacc("TRN2", target_bir_lowering=False, num_devices=1)
    arrays = {f"in_{n}": np.ascontiguousarray(a) for n, a in arrays.items()}
    aps = {n: nc.dram_tensor(n, a.shape, mybir.dt.from_np(a.dtype), kind="ExternalInput").ap()
           for n, a in arrays.items()}
    out = nc.dram_tensor("out", (P, KD, T), F32, kind="ExternalOutput").ap()
    hybrid_and_moe(nc, aps["in_stream"], aps["in_const"], aps["in_par1"], aps["in_lb"], aps["in_par2"], aps["in_ada"], aps["in_c"], aps["in_bias"],
                   aps["in_xT"], out)
    r = run_bass_kernel_spmd(nc, [arrays], core_ids=[0])
    return np.ascontiguousarray(r.results[0]["out"].transpose(2, 1, 0).reshape(1, T, D))
```
